# Optimizing a Trainium2 kernel written in Bass

```python
import math
import jax, jax.numpy as jnp
from jax import lax
import numpy as np

D_MODEL = 1024
BATCH = 1
SEQ = 1024
DEPTH = 1

MIX_WIDTH = D_MODEL
ATT_WIDTH = MIX_WIDTH // 2
RNN_WIDTH = MIX_WIDTH - ATT_WIDTH
N_ATT_HEADS = 4
ATT_HEAD_DIM = ATT_WIDTH // N_ATT_HEADS
QK_DIM = ATT_HEAD_DIM // 2
N_RNN_BLOCKS = 8
RNN_BLOCK = RNN_WIDTH // N_RNN_BLOCKS
CONV_WIDTH = 4
LRU_C = 8.0
N_GROUPS = 4
EXPERTS_PER_GROUP = 8
N_EXPERTS = N_GROUPS * EXPERTS_PER_GROUP
TOP_K = 2
EXPERT_FF = D_MODEL // 2
Q_BLOCK = 128
MOE_CHUNK = 128
NORM_EPS = 1e-6
HEAD_NORM_EPS = 1e-5
IN_COLS = 3 * ATT_WIDTH + 2 * RNN_WIDTH

kernel_name = 'hymba_diffattn_rglru_hiermoe'

def rms_norm(x, w, eps=NORM_EPS):
    xf = x.astype(jnp.float32)
    y = xf * lax.rsqrt(jnp.mean(xf * xf, axis=-1, keepdims=True) + eps)
    return (y * w.astype(jnp.float32)).astype(x.dtype)

def alibi_slopes(n_heads):
    return np.array([2.0 ** (-8.0 * (i + 1) / n_heads) for i in range(n_heads)], dtype=np.float32)

def diff_attention(q, k, v, lam):
    b, h, _, s, dk = q.shape
    n_blocks = s // Q_BLOCK
    slopes = jnp.asarray(alibi_slopes(h))
    scale = dk ** -0.5
    k_pos = jnp.arange(s)

    def block(qb):
        start = qb * Q_BLOCK
        q_blk = lax.dynamic_slice_in_dim(q, start, Q_BLOCK, axis=3)
        sc = jnp.einsum('bhcqd,bhckd->bhcqk', q_blk, k).astype(jnp.float32) * scale
        dist = (start + jnp.arange(Q_BLOCK))[:, None] - k_pos[None, :]
        bias = jnp.where(dist >= 0, -slopes[:, None, None] * dist.astype(jnp.float32), -jnp.inf)
        prob = jax.nn.softmax(sc + bias[None, :, None], axis=-1)
        att = prob[:, :, 0] - lam * prob[:, :, 1]
        return jnp.einsum('bhqk,bhkd->bhqd', att.astype(v.dtype), v)

    out = lax.map(block, jnp.arange(n_blocks))
    return jnp.moveaxis(out, 0, 2).reshape(b, h, s, -1)

def rglru_branch(xr, gate, conv_w, conv_b, w_r, b_r, w_i, b_i, lru_lambda):
    b, s, c = xr.shape
    xc = lax.conv_general_dilated(xr, conv_w[:, None, :], window_strides=(1,),
                                  padding=[(CONV_WIDTH - 1, 0)],
                                  dimension_numbers=('NWC', 'WIO', 'NWC'),
                                  feature_group_count=c) + conv_b
    xb = xc.reshape(b, s, N_RNN_BLOCKS, RNN_BLOCK)
    r = jax.nn.sigmoid((jnp.einsum('bsni,nij->bsnj', xb, w_r).reshape(b, s, c) + b_r).astype(jnp.float32))
    i = jax.nn.sigmoid((jnp.einsum('bsni,nij->bsnj', xb, w_i).reshape(b, s, c) + b_i).astype(jnp.float32))
    log_a = -LRU_C * r * jax.nn.softplus(-lru_lambda.astype(jnp.float32))
    a = jnp.exp(log_a)
    u = jnp.sqrt(-jnp.expm1(2.0 * log_a)) * i * xc.astype(jnp.float32)

    def combine(left, right):
        a1, b1 = left
        a2, b2 = right
        return a1 * a2, a2 * b1 + b2

    _, hs = lax.associative_scan(combine, (a, u), axis=1)
    return (hs * jax.nn.gelu(gate.astype(jnp.float32))).astype(xr.dtype)

def hier_moe(xn, w_rg, b_rg, w_re, b_re, w_g, w_u, w_d):
    b, s, d = xn.shape
    t = b * s
    xf = xn.reshape(t, d)
    lg = (xf @ w_rg).astype(jnp.float32) + b_rg.astype(jnp.float32)
    pg = jax.nn.softmax(lg, axis=-1)
    g_sel = jnp.argmax(lg, axis=-1).astype(jnp.int32)
    pg_sel = jnp.take_along_axis(pg, g_sel[:, None], axis=1)[:, 0]
    le = ((xf @ w_re).astype(jnp.float32) + b_re.astype(jnp.float32)).reshape(t, N_GROUPS, EXPERTS_PER_GROUP)
    le_sel = jnp.take_along_axis(le, g_sel[:, None, None], axis=1)[:, 0]
    top_v, top_i = lax.top_k(le_sel, TOP_K)
    gates = pg_sel[:, None] * jax.nn.softmax(top_v, axis=-1)
    eid = (g_sel[:, None] * EXPERTS_PER_GROUP + top_i.astype(jnp.int32)).reshape(-1)
    tok = jnp.repeat(jnp.arange(t, dtype=jnp.int32), TOP_K)
    gate_flat = gates.reshape(-1)
    m = t * TOP_K

    order = jnp.argsort(eid)
    s_eid = eid[order]
    counts = jnp.bincount(eid, length=N_EXPERTS).astype(jnp.int32)
    start = jnp.cumsum(counts) - counts
    padded = (counts + MOE_CHUNK - 1) // MOE_CHUNK * MOE_CHUNK
    pend = jnp.cumsum(padded)
    pstart = pend - padded
    dest = pstart[s_eid] + jnp.arange(m, dtype=jnp.int32) - start[s_eid]
    n_chunks = -(-(m + N_EXPERTS * (MOE_CHUNK - 1)) // MOE_CHUNK)
    p = n_chunks * MOE_CHUNK
    slot_tok = jnp.full((p,), t, dtype=jnp.int32).at[dest].set(tok[order])
    slot_gate = jnp.zeros((p,), jnp.float32).at[dest].set(gate_flat[order])
    chunk_e = jnp.minimum(jnp.searchsorted(pend, jnp.arange(n_chunks, dtype=jnp.int32) * MOE_CHUNK, side='right'),
                          N_EXPERTS - 1).astype(jnp.int32)
    xpad = jnp.concatenate([xf, jnp.zeros((1, d), xf.dtype)], axis=0)

    def run_chunk(args):
        ct, cg, e = args
        xc = xpad[ct]
        hdn = jax.nn.silu(xc @ w_g[e]) * (xc @ w_u[e])
        return (hdn @ w_d[e]) * cg[:, None].astype(xc.dtype)

    y = lax.map(run_chunk, (slot_tok.reshape(n_chunks, MOE_CHUNK),
                            slot_gate.reshape(n_chunks, MOE_CHUNK), chunk_e))
    out = jnp.zeros((t + 1, d), xf.dtype).at[slot_tok].add(y.reshape(p, d))[:t]
    return out.reshape(b, s, d)

def setup_inputs(seed: int = 0) -> dict:
    key = jax.random.key(seed)
    ks = jax.random.split(key, 24)
    f32 = jnp.float32
    nrm = lambda k, shape, scale: jax.random.normal(k, shape, f32) * scale
    u = jax.random.uniform(ks[12], (DEPTH, RNN_WIDTH), f32, 0.9, 0.999)
    sa = u ** (1.0 / LRU_C)
    return {
        'x': jax.random.normal(ks[0], (BATCH, SEQ, D_MODEL), f32),
        'mix_norm_w': 1.0 + nrm(ks[1], (DEPTH, D_MODEL), 0.02),
        'w_in': nrm(ks[2], (DEPTH, D_MODEL, IN_COLS), D_MODEL ** -0.5),
        'lambda_q1': nrm(ks[3], (DEPTH, QK_DIM), 0.1),
        'lambda_k1': nrm(ks[4], (DEPTH, QK_DIM), 0.1),
        'lambda_q2': nrm(ks[5], (DEPTH, QK_DIM), 0.1),
        'lambda_k2': nrm(ks[6], (DEPTH, QK_DIM), 0.1),
        'head_norm_w': 1.0 + nrm(ks[7], (DEPTH, ATT_HEAD_DIM), 0.02),
        'conv_w': nrm(ks[8], (DEPTH, CONV_WIDTH, RNN_WIDTH), CONV_WIDTH ** -0.5),
        'conv_b': nrm(ks[9], (DEPTH, RNN_WIDTH), 0.01),
        'w_rgate': nrm(ks[10], (DEPTH, N_RNN_BLOCKS, RNN_BLOCK, RNN_BLOCK), RNN_BLOCK ** -0.5),
        'b_rgate': nrm(ks[11], (DEPTH, RNN_WIDTH), 0.01),
        'w_igate': nrm(ks[13], (DEPTH, N_RNN_BLOCKS, RNN_BLOCK, RNN_BLOCK), RNN_BLOCK ** -0.5),
        'b_igate': nrm(ks[14], (DEPTH, RNN_WIDTH), 0.01),
        'lru_lambda': jnp.log(sa) - jnp.log1p(-sa),
        'w_out': nrm(ks[15], (DEPTH, MIX_WIDTH, D_MODEL), MIX_WIDTH ** -0.5),
        'ffn_norm_w': 1.0 + nrm(ks[16], (DEPTH, D_MODEL), 0.02),
        'w_router_group': nrm(ks[17], (DEPTH, D_MODEL, N_GROUPS), D_MODEL ** -0.5),
        'b_router_group': nrm(ks[18], (DEPTH, N_GROUPS), 0.01),
        'w_router_expert': nrm(ks[19], (DEPTH, D_MODEL, N_EXPERTS), D_MODEL ** -0.5),
        'b_router_expert': nrm(ks[20], (DEPTH, N_EXPERTS), 0.01),
        'w_exp_gate': nrm(ks[21], (DEPTH, N_EXPERTS, D_MODEL, EXPERT_FF), D_MODEL ** -0.5),
        'w_exp_up': nrm(ks[22], (DEPTH, N_EXPERTS, D_MODEL, EXPERT_FF), D_MODEL ** -0.5),
        'w_exp_down': nrm(ks[23], (DEPTH, N_EXPERTS, EXPERT_FF, D_MODEL), EXPERT_FF ** -0.5),
        'final_norm_w': 1.0 + nrm(jax.random.fold_in(key, 99), (D_MODEL,), 0.02),
    }

def reference(x, mix_norm_w, w_in, lambda_q1, lambda_k1, lambda_q2, lambda_k2, head_norm_w,
              conv_w, conv_b, w_rgate, b_rgate, w_igate, b_igate, lru_lambda, w_out,
              ffn_norm_w, w_router_group, b_router_group, w_router_expert, b_router_expert,
              w_exp_gate, w_exp_up, w_exp_down, final_norm_w):
    b, s, _ = x.shape
    splits = [ATT_WIDTH, 2 * ATT_WIDTH, 3 * ATT_WIDTH, 3 * ATT_WIDTH + RNN_WIDTH]
    for l in range(DEPTH):
        lambda_init = 0.8 - 0.6 * math.exp(-0.3 * l)
        hn = rms_norm(x, mix_norm_w[l])
        proj = hn @ w_in[l]
        q, k, v, xr, gr = jnp.split(proj, splits, axis=-1)
        q = q.reshape(b, s, N_ATT_HEADS, 2, QK_DIM).transpose(0, 2, 3, 1, 4)
        k = k.reshape(b, s, N_ATT_HEADS, 2, QK_DIM).transpose(0, 2, 3, 1, 4)
        v = v.reshape(b, s, N_ATT_HEADS, ATT_HEAD_DIM).transpose(0, 2, 1, 3)
        lam = (jnp.exp(jnp.sum(lambda_q1[l].astype(jnp.float32) * lambda_k1[l].astype(jnp.float32)))
               - jnp.exp(jnp.sum(lambda_q2[l].astype(jnp.float32) * lambda_k2[l].astype(jnp.float32)))
               + lambda_init)
        att = diff_attention(q, k, v, lam)
        att = rms_norm(att, head_norm_w[l], HEAD_NORM_EPS) * (1.0 - lambda_init)
        att = att.transpose(0, 2, 1, 3).reshape(b, s, ATT_WIDTH)
        rnn = rglru_branch(xr, gr, conv_w[l], conv_b[l], w_rgate[l], b_rgate[l],
                           w_igate[l], b_igate[l], lru_lambda[l])
        x = x + jnp.concatenate([att, rnn], axis=-1) @ w_out[l]
        hn = rms_norm(x, ffn_norm_w[l])
        x = x + hier_moe(hn, w_router_group[l], b_router_group[l], w_router_expert[l],
                         b_router_expert[l], w_exp_gate[l], w_exp_up[l], w_exp_down[l])
    return rms_norm(x, final_norm_w)


_drawn_inputs = setup_inputs


def setup_inputs(seed=0):
    import zlib

    import numpy as np

    out = dict(_drawn_inputs(seed))
    spreads = {}
    factors = {'lambda_q2': 35.024,
     'b_rgate': 35.199,
     'b_igate': 33.283,
     'b_router_group': 3.235,
     'b_router_expert': 4.45,
     'final_norm_w': 8.156}
    for name, (base, spread) in spreads.items():
        noise = np.random.default_rng([zlib.crc32(name.encode()), seed]).standard_normal(out[name].shape)
        drawn = base * np.exp(spread * noise) if base else spread * noise
        out[name] = __import__('jax').numpy.asarray(drawn.astype(out[name].dtype))
    for name, factor in factors.items():
        out[name] = (out[name] * factor).astype(out[name].dtype)
    return out
```

```python
from contextlib import ExitStack

import concourse.bass as bass
from concourse import mybir

P = 128
F32 = mybir.dt.float32
F32R = mybir.dt.float32r
I32 = mybir.dt.int32
U32 = mybir.dt.uint32
ALU = mybir.AluOpType
ACT = mybir.ActivationFunctionType
AX = mybir.AxisListType
SEQ = 1024
D = 1024
KT = D // P
TT = SEQ // P
HALF = 512
HEADS = 4
DH = 128
QK = 64
CT = 4
NORM_EPS = 1e-6
HEAD_EPS = 1e-5
LAM_INIT = 0.2
NG = 4
EPG = 8
NE = NG * EPG
FF = D // 2
FT = FF // P
NX = SEQ * 2 // P - 1
SLOTS = (NE + NX) * P
BIG = 1e30


class Link:

    def __init__(self, eng, sem):
        self.eng, self.sem, self.n, self.i, self.per, self.mark = eng, sem, 0, None, 0, 0

    def loop(self, i, per):
        self.i, self.per, self.mark = i, per, self.n

    def again(self, i):
        assert self.n - self.mark == self.per, (self.n - self.mark, self.per)
        self.n, self.i = self.mark, i

    def end(self, times):
        assert self.n - self.mark == self.per, (self.n - self.mark, self.per)
        self.n, self.i = self.mark + self.per * times, None

    def __call__(self, ins):
        self.n += 1
        ins.then_inc(self.sem, 1)
        self.eng.wait_ge(self.sem, self.n if self.i is None else self.i * self.per + self.n)


def span(start, n):
    return slice(start, start + n) if isinstance(start, int) else bass.ds(start, n)


def split_products(pe, out, lh, ll, rh, rl, start, stop):
    nc_mm = pe.matmul
    for o, h in zip(out, range(len(out))):
        nc_mm(o, lh, rh[h], start=start, stop=False)
    for o, h in zip(out, range(len(out))):
        nc_mm(o, lh, rl[h], start=False, stop=False)
    for o, h in zip(out, range(len(out))):
        last = nc_mm(o, ll, rh[h], start=False, stop=stop)
    return last


def project_and_recur(nc, io, persist):
    mixT, qkvT, ident = persist["mixT"], persist["qkvT"], persist["ident"]
    with ExitStack() as ctx:
        sb = lambda name, shape, dt=F32: ctx.enter_context(nc.sbuf_tensor(name, shape, dt))
        sem = lambda name: ctx.enter_context(nc.semaphore(name))
        hT_hi = sb("hT_hi", [P, KT, SEQ], F32R)
        hT_lo = sb("hT_lo", [P, KT, SEQ], F32R)
        w_raw = sb("w_raw", [P, 2, KT, 2 * P])
        w_hi = sb("w_hi", [P, 2, KT, P], F32R)
        w_lo = sb("w_lo", [P, 2, KT, P], F32R)
        tmp = [sb(f"tmp{n}", [P, SEQ]) for n in range(5)]
        gate_w = sb("gate_w", [P, CT, 2, P])
        gate_cur = sb("gate_cur", [P, 2, P])
        rows = sb("rows", [32, P])
        chan = sb("chan", [P, 32])
        soft = sb("soft", [P, 8, CT])
        stat = sb("stat", [P, 3, TT])
        eps = sb("eps", [P, 1])
        ps = [ctx.enter_context(nc.psum_tensor(f"ps_proj{n}", [P, 2, HALF], F32)) for n in range(2)]
        ps_t = [ctx.enter_context(nc.psum_tensor(f"ps_turn{n}", [P, 2, HALF], F32)) for n in range(2)]
        x_sb, xn_sb, norm_w = tmp[0:2], tmp[2:4], tmp[4]
        conv_x, r_sb, i_sb, a_sb, t_sb = tmp

        rows_in = sem("rows_in")
        norm_w_in = sem("norm_w_in")
        gates_in = sem("gates_in")
        x_in = [sem(f"x_in{n}") for n in range(2)]
        w_in = [sem(f"w_in{n}") for n in range(2)]
        consts = sem("consts")
        ident0 = sem("ident0")
        chan_t = sem("chan_t")
        chan_ready = sem("chan_ready")
        exp_ready = sem("exp_ready")
        soft_ready = sem("soft_ready")
        x_free = sem("x_free")
        root_ready = sem("root_ready")
        xn_ready = sem("xn_ready")
        turned = sem("turned")
        hi_out = sem("hi_out")
        lo_out = sem("lo_out")
        w_free = sem("w_free")
        w_hi_ready = sem("w_hi_ready")
        w_lo_ready = sem("w_lo_ready")
        proj_done = sem("proj_done")
        proj_out = sem("proj_out")
        cur_ready = sem("cur_ready")
        conv_ready = sem("conv_ready")
        gates_done = sem("gates_done")
        gates_read = sem("gates_read")
        tanh_ready = sem("tanh_ready")
        ratio_ready = sem("ratio_ready")
        sqrt_ready = sem("sqrt_ready")
        gelu_ready = sem("gelu_ready")
        lru_done = sem("lru_done")
        act_own = sem("act_own")
        dve_own = sem("dve_own")
        block = ctx.enter_context(nc.Block("project"))

        w_cols = io["w_in"][0].rearrange("(k p) n -> p k n", p=P)

        @block.sync
        def _(sp):
            for src, at, n in ((io["conv_w"], 0, 16), (io["conv_b"], 16, 4), (io["b_rgate"], 20, 4),
                               (io["b_igate"], 24, 4), (io["lru_lambda"], 28, 4)):
                flat = src.rearrange("l w (t p) -> (l w t) p", p=P) if n == 16 else \
                    src.rearrange("l (t p) -> (l t) p", p=P)
                sp.dma_start(rows[at:at + n, :], flat).then_inc(rows_in, 16)
            sp.dma_start(norm_w[:, :], io["mix_norm_w"][0].partition_broadcast(P)).then_inc(norm_w_in, 16)
            with sp.Fori(0, TT // 2) as i:
                for c in range(2):
                    sp.wait_ge(x_free, i * 2 + (c + 1))
                    sp.dma_start(x_sb[c][:, :], io["x"][0][bass.ds(i * (2 * P) + c * P, P), :]).then_inc(x_in[c], 16)

            def load(col, n, c):
                sp.wait_ge(w_free, n)
                sp.dma_start(w_raw[:, c], w_cols[:, :, bass.ds(col, 2 * P)]).then_inc(w_in[c], 16)

            with sp.Fori(0, 2) as i:
                for c in range(2):
                    load((i * -HALF) + (4 * HALF + c * 2 * P), i * 2 + (c + 1), c)
            with sp.Fori(0, 2) as i:
                for c in range(2):
                    load(i * HALF + c * 2 * P, i * 2 + (c + 5), c)
            for c in range(2):
                load(2 * HALF + c * 2 * P, c + 9, c)

        @block.gpsimd
        def _(pool):
            pool.memset(ident[:, :], 0.0).then_inc(ident0, 1)
            pool.memset(eps[:, :], NORM_EPS).then_inc(ident0, 1)
            pool.memset(gate_w[:, :, :, :], 0.0).then_inc(ident0, 1)
            pool.wait_ge(ident0, 3)
            pool.affine_select(out=ident[:, :], in_=ident[:, :], compare_op=ALU.not_equal, fill=1.0, base=0,
                               pattern=[[-1, P]], channel_multiplier=1).then_inc(consts, 1)
            for g, src in enumerate((io["w_rgate"], io["w_igate"])):
                for b in range(2):
                    half = slice(64 * b, 64 * b + 64)
                    pool.dma_start(gate_w[half, :, g, half],
                                   src[0].rearrange("(t b) i j -> b i t j", b=2)[b]).then_inc(gates_in, 16)
            pool.wait_ge(gates_in, 64)
            with pool.Fori(0, CT) as t:
                pool.wait_ge(gates_done, t + 1)
                pool.tensor_copy(gate_cur[:, :, :], gate_w[:, bass.ds(t, 1)].rearrange("p o g j -> p (o g) j")).then_inc(cur_ready, 1)

        @block.scalar
        def _(act):
            link = Link(act, act_own)
            act.wait_ge(chan_ready, 2)
            act.activation(soft[:, 2, :], soft[:, 1, :], ACT.Exp, scale=-1.0).then_inc(exp_ready, 1)
            act.wait_ge(consts, 1)

            def square(i, c):
                act.wait_ge(x_in[c], i * 16 + 16)
                act.wait_ge(turned, i * 2 + (c + 1))
                link(act.activation(xn_sb[c][:, :], x_sb[c][:, :], ACT.Square,
                                    accum_out=stat[:, 0, bass.ds(i * 2 + c, 1)]))
                act.activation(stat[:, 1, bass.ds(i * 2 + c, 1)], stat[:, 0, bass.ds(i * 2 + c, 1)], ACT.Sqrt,
                               bias=eps[:, 0:1], scale=1.0 / D).then_inc(root_ready, 1)

            def high(i, c):
                act.wait_ge(turned, i * 2 + (c + 3))
                act.activation(hT_hi[:, :, bass.ds(i * 2 * P + c * P, P)],
                               ps_t[c][:, :, :].rearrange("p a (k n) -> p (a k) n", n=P), ACT.Copy).then_inc(hi_out, 1)

            with act.Fori(0, TT // 2) as i:
                link.loop(i, 2)
                square(i, 0)
                square(i, 1)
                high(i, 0)
                high(i, 1)
            link.end(TT // 2)

            def split_high(n, c):
                if c % 2 == 0:
                    act.wait_ge(w_in[c // 2], n[1])
                act.wait_ge(proj_done, n[0] + 1)
                act.activation(w_hi[:, c % 2], w_raw[:, c // 2, :, (c % 2) * P:(c % 2 + 1) * P],
                               ACT.Copy).then_inc(w_hi_ready, 1)

            def evacuate(n, dst, c):
                act.wait_ge(proj_done, n + 3)
                act.activation(dst, ps[c % 2][:, :, :].rearrange("p a n -> p (a n)"), ACT.Copy).then_inc(proj_out, 1)

            def gates(i, c):
                t = i * 2 + c // 2
                act.wait_ge(gates_done, t + 2)
                act.wait_ge(lru_done, t + 1)
                link(act.activation(r_sb[:, :], ps_t[0][:, :, :].rearrange("p a n -> p (a n)"), ACT.Sigmoid,
                                    bias=chan[:, bass.ds(t + 20, 1)]))
                act.activation(i_sb[:, :], ps_t[1][:, :, :].rearrange("p a n -> p (a n)"), ACT.Sigmoid,
                               bias=chan[:, bass.ds(t + 24, 1)]).then_inc(gates_read, 1)
                act.activation(t_sb[:, :], r_sb[:, :], ACT.Tanh, scale=soft[:, 6, bass.ds(t, 1)]).then_inc(tanh_ready, 1)
                act.activation(a_sb[:, :], r_sb[:, :], ACT.Exp, scale=soft[:, 7, bass.ds(t, 1)]).then_inc(tanh_ready, 1)
                act.wait_ge(ratio_ready, t + 1)
                act.activation(t_sb[:, :], t_sb[:, :], ACT.Sqrt).then_inc(sqrt_ready, 1)
                act.activation(mixT[:, bass.ds(t, 1)], mixT[:, bass.ds(t, 1)], ACT.Gelu_apprx_tanh).then_inc(gelu_ready, 1)

            split_high((0, 16), 0)
            for group in range(2):
                with act.Fori(0, 2) as i:
                    if group:
                        link.loop(i, 2)
                    for c in range(4):
                        base = 8 * group + c
                        nxt = (c + 1) % 4
                        nth = 2 * group + 1 + (c == 3)
                        split_high((i * 4 + (base + 1), i * 16 + 16 * nth), nxt)
                        if group and c == 0:
                            act.wait_ge(soft_ready, 1)
                            act.wait_ge(proj_out, 10)
                        if group and c % 2 == 1:
                            gates(i, c)
                        dst = (qkvT if group else mixT)[:, bass.ds(i * 4 + c, 1)]
                        evacuate(i * 4 + base, dst.rearrange("p o n -> p (o n)"), c)
                if group:
                    link.end(2)
            for c in range(4):
                if c < 3:
                    split_high((17 + c, 16 * 5), c + 1)
                evacuate(16 + c, qkvT[:, 8 + c], c)

        @block.vector
        def _(dve):
            link = Link(dve, dve_own)
            dve.sem_inc(x_free, 2)
            dve.sem_inc(w_free, 2)
            dve.sem_inc(lru_done, 1)
            dve.wait_ge(chan_t, 1)
            dve.tensor_copy(chan[:, :], ps[0][:, 0, 0:32]).then_inc(chan_ready, 1)
            dve.wait_ge(chan_ready, 1)
            lam = chan[:, 28:32]
            link(dve.tensor_scalar(soft[:, 0, :], lam, -1.0, 0.0, ALU.mult, ALU.max))
            dve.scalar_tensor_tensor(out=soft[:, 1, :], in0=lam, scalar=-1.0, in1=lam, op0=ALU.mult,
                                     op1=ALU.max).then_inc(chan_ready, 1)
            dve.wait_ge(exp_ready, 1)
            link(dve.tensor_scalar(soft[:, 3, :], soft[:, 2, :], 2.0, None, ALU.add))
            link(dve.reciprocal(soft[:, 3, :], soft[:, 3, :]))
            link(dve.tensor_tensor(soft[:, 3, :], soft[:, 3, :], soft[:, 2, :], ALU.mult))
            link(dve.tensor_tensor(soft[:, 4, :], soft[:, 3, :], soft[:, 3, :], ALU.mult))
            link(dve.tensor_scalar(soft[:, 5, :], soft[:, 4, :], 1.0 / 19.0, None, ALU.mult))
            for odd in range(17, 2, -2):
                link(dve.scalar_tensor_tensor(out=soft[:, 5, :], in0=soft[:, 5, :], scalar=1.0 / odd,
                                              in1=soft[:, 4, :], op0=ALU.add, op1=ALU.mult))
            link(dve.scalar_tensor_tensor(out=soft[:, 5, :], in0=soft[:, 5, :], scalar=1.0, in1=soft[:, 3, :],
                                          op0=ALU.add, op1=ALU.mult))
            link(dve.scalar_tensor_tensor(out=soft[:, 5, :], in0=soft[:, 5, :], scalar=2.0, in1=soft[:, 0, :],
                                          op0=ALU.mult, op1=ALU.add))
            link(dve.tensor_scalar(soft[:, 6, :], soft[:, 5, :], 8.0, None, ALU.mult))
            dve.tensor_scalar(soft[:, 7, :], soft[:, 5, :], -8.0, None, ALU.mult).then_inc(soft_ready, 1)

            def scale(i, c):
                dve.wait_ge(root_ready, i * 2 + (c + 1))
                link(dve.reciprocal(stat[:, 2, bass.ds(i * 2 + c, 1)], stat[:, 1, bass.ds(i * 2 + c, 1)]))
                link(dve.scalar_tensor_tensor(out=xn_sb[c][:, :], in0=x_sb[c][:, :],
                                              scalar=stat[:, 2, bass.ds(i * 2 + c, 1)],
                                              in1=norm_w[:, :], op0=ALU.mult, op1=ALU.mult))
                dve.sem_inc(x_free, 1)
                dve.sem_inc(xn_ready, 1)

            def low(i, c):
                dve.wait_ge(hi_out, i * 2 + (c + 1))
                at = bass.ds(i * 2 * P + c * P, P)
                dve.tensor_tensor(hT_lo[:, :, at], ps_t[c][:, :, :].rearrange("p a (k n) -> p (a k) n", n=P),
                                  hT_hi[:, :, at].bitcast(F32), ALU.subtract).then_inc(lo_out, 1)

            dve.wait_ge(norm_w_in, 16)
            with dve.Fori(0, TT // 2) as i:
                link.loop(i, 4)
                scale(i, 0)
                scale(i, 1)
                low(i, 0)
                low(i, 1)
            link.end(TT // 2)

            def split_low(n, c):
                dve.wait_ge(w_hi_ready, n)
                ins = dve.tensor_tensor(w_lo[:, c % 2], w_raw[:, c // 2, :, (c % 2) * P:(c % 2 + 1) * P],
                                        w_hi[:, c % 2].bitcast(F32), ALU.subtract)
                ins.then_inc(w_lo_ready, 1)
                if c % 2 == 1:
                    dve.wait_ge(w_lo_ready, n)
                    dve.sem_inc(w_free, 1)

            def convolve(t):
                x_t = mixT[:, bass.ds(t + 4, 1)].rearrange("p o n -> p (o n)")
                link(dve.tensor_scalar(conv_x[:, :], x_t, chan[:, bass.ds(t + 12, 1)], chan[:, bass.ds(t + 16, 1)],
                                       ALU.mult, ALU.add))
                for back in (1, 2, 3):
                    link(dve.scalar_tensor_tensor(
                        out=conv_x[:, back:], in0=mixT[:, bass.ds(t + 4, 1), 0:SEQ - back].rearrange("p o n -> p (o n)"),
                        scalar=chan[:, bass.ds(t + 4 * (3 - back), 1)],
                        in1=conv_x[:, back:], op0=ALU.mult, op1=ALU.add))
                dve.sem_inc(conv_ready, 1)

            def recur(t):
                dve.wait_ge(tanh_ready, t * 2 + 2)
                link(dve.tensor_tensor(r_sb[:, :], a_sb[:, :], a_sb[:, :], ALU.mult))
                dve.scalar_tensor_tensor(out=t_sb[:, :], in0=r_sb[:, :], scalar=1.0, in1=t_sb[:, :],
                                         op0=ALU.add, op1=ALU.mult).then_inc(ratio_ready, 1)
                link(dve.tensor_tensor(i_sb[:, :], i_sb[:, :], conv_x[:, :], ALU.mult))
                dve.wait_ge(sqrt_ready, t + 1)
                link(dve.tensor_tensor(i_sb[:, :], i_sb[:, :], t_sb[:, :], ALU.mult))
                link(dve.tensor_tensor_scan(r_sb[:, :], a_sb[:, :], i_sb[:, :], 0.0, ALU.mult, ALU.add))
                dve.wait_ge(gelu_ready, t + 1)
                gate = mixT[:, bass.ds(t, 1)].rearrange("p o n -> p (o n)")
                dve.tensor_tensor(gate, gate, r_sb[:, :], ALU.mult).then_inc(lru_done, 1)

            split_low(1, 0)
            with dve.Fori(0, 2) as i:
                for c in range(4):
                    split_low(i * 4 + (c + 2), (c + 1) % 4)
            with dve.Fori(0, 2) as i:
                link.loop(i, 2 * 8)
                for c in range(4):
                    split_low(i * 4 + (c + 10), (c + 1) % 4)
                    if c == 0:
                        dve.wait_ge(proj_out, 10)
                    if c % 2 == 0:
                        convolve(i * 2 + c // 2)
                    else:
                        recur(i * 2 + c // 2)
            link.end(2)
            for c in range(1, 4):
                split_low(17 + c, c)

        @block.tensor
        def _(pe):
            for free, n in ((turned, 2), (lo_out, 2), (proj_done, 2), (proj_out, 2), (gates_done, 1), (gates_read, 1)):
                pe.sem_inc(free, n)
            pe.wait_ge(rows_in, 80)
            pe.wait_ge(consts, 1)
            pe.transpose(ps[0][:, 0, 0:32], rows[:, :], ident[0:32, 0:32]).then_inc(chan_t, 1)

            def turn(i, c):
                pe.wait_ge(xn_ready, i * 2 + (c + 1))
                pe.wait_ge(lo_out, i * 2 + (c + 1))
                for k in range(KT):
                    last = pe.transpose(ps_t[c][:, k // 4, (k % 4) * P:(k % 4 + 1) * P],
                                        xn_sb[c][:, k * P:(k + 1) * P], ident[:, :])
                last.then_inc(turned, 1)

            with pe.Fori(0, TT // 2) as i:
                turn(i, 0)
                turn(i, 1)
            pe.wait_ge(lo_out, TT + 2)

            def tile(n, c):
                pe.wait_ge(w_lo_ready, n)
                pe.wait_ge(proj_out, n)
                for k in range(KT):
                    last = split_products(pe, [ps[c % 2][:, h, :] for h in range(2)],
                                          w_hi[:, c % 2, k, :], w_lo[:, c % 2, k, :],
                                          [hT_hi[:, k, h * HALF:(h + 1) * HALF] for h in range(2)],
                                          [hT_lo[:, k, h * HALF:(h + 1) * HALF] for h in range(2)],
                                          k == 0, k == KT - 1)
                last.then_inc(proj_done, 1)

            def gates(t):
                pe.wait_ge(conv_ready, t + 1)
                pe.wait_ge(cur_ready, t + 1)
                pe.wait_ge(gates_read, t + 1)
                for g in range(2):
                    for h in range(2):
                        last = pe.matmul(ps_t[g][:, h, :], gate_cur[:, g, :], conv_x[:, h * HALF:(h + 1) * HALF],
                                         start=True, stop=True)
                last.then_inc(gates_done, 1)

            with pe.Fori(0, 2) as i:
                for c in range(4):
                    tile(i * 4 + (c + 1), c)
            with pe.Fori(0, 2) as i:
                for c in range(4):
                    tile(i * 4 + (c + 9), c)
                    if c % 2 == 0:
                        gates(i * 2 + c // 2)
            for c in range(4):
                tile(17 + c, c)


def attend(nc, io, persist):
    mixT, qkvT, ident, head_ss = (persist[n] for n in ("mixT", "qkvT", "ident", "head_ss"))
    with ExitStack() as ctx:
        sb = lambda name, shape, dt=F32: ctx.enter_context(nc.sbuf_tensor(name, shape, dt))
        sem = lambda name: ctx.enter_context(nc.semaphore(name))
        q_hi, q_lo, k_hi, k_lo = (sb(n, [P, SEQ], F32R) for n in ("q_hi", "q_lo", "k_hi", "k_lo"))
        vT = sb("vT", [P, SEQ])
        v_nat = sb("v_nat", [P, TT, DH])
        bias8 = sb("bias8", [P, SEQ])
        prob = sb("prob", [P, 2, 2, SEQ])
        attT = sb("attT", [P, 2, SEQ])
        zeros = sb("zeros", [P, D])
        junk = sb("junk", [P, 2, DH])
        lam_in = sb("lam_in", [P, 4, QK])
        lam = sb("lam", [P, 8])
        row_max = sb("row_max", [P, TT, 2])
        neg_max = sb("neg_max", [P, TT, 2])
        row_sum = sb("row_sum", [P, TT, 2])
        inv_sum = sb("inv_sum", [P, TT, 2])
        coef = sb("coef", [P, TT])
        ps_s = [ctx.enter_context(nc.psum_tensor(f"ps_s{c}", [P, SEQ], F32)) for c in range(2)]
        ps_t = ctx.enter_context(nc.psum_tensor("ps_t", [P, SEQ], F32))
        ps_o = [ctx.enter_context(nc.psum_tensor(f"ps_o{n}", [P, HALF], F32)) for n in range(2)]

        zero_set = sem("zero_set")
        zeroed = sem("y_zeroed")
        lam_loaded = sem("lam_loaded")
        lam_sums = sem("lam_sums")
        lam_exp = sem("lam_exp")
        pool_own = sem("pool_own")
        bias_ready = sem("bias_ready")
        v_ready = sem("v_ready")
        qk_high = sem("qk_high")
        qk_split = sem("qk_split")
        scores_done = sem("scores_done")
        scores_read = sem("scores_read")
        max_ready = sem("max_ready")
        exp_done = sem("exp_done")
        att_ready = sem("att_ready")
        turned = sem("turned")
        turned_out = sem("turned_out")
        pv_done = sem("pv_done")
        out_scaled = sem("out_scaled")
        out_squared = sem("out_squared")
        dve_own = sem("dve_own2")
        dve_seen = sem("dve_seen")
        block = ctx.enter_context(nc.Block("attend"))

        width = [(TT - s) * P for s in range(TT)]
        tile_of = [TT - 1 - s for s in range(TT)]

        def heads(eng, body):
            with eng.Fori(0, HEADS - 1) as h:
                body(h, False)
            body(HEADS - 1, True)

        def tile(tensor, n):
            return tensor[:, span(n, 1)].rearrange("p o n -> p (o n)")

        @block.sync
        def _(sp):
            for n, name in enumerate(("lambda_q1", "lambda_k1", "lambda_q2", "lambda_k2")):
                sp.dma_start(lam_in[:, n, :], io[name][0].partition_broadcast(P)).then_inc(lam_loaded, 16)
            sp.wait_ge(zero_set, 1)
            sp.dma_start(persist["y_d"][NE * P:SLOTS, :].rearrange("(j p) n -> p j n", p=P),
                         zeros[:, :].unsqueeze(1).to_broadcast([P, NX, D])).then_inc(zeroed, 16)
            sp.wait_ge(zeroed, 16)

        @block.gpsimd
        def _(pool):
            pool.memset(zeros[:, :], 0.0).then_inc(zero_set, 1)
            pool.iota(bias8[:, :], [[8, SEQ]], base=-8 * (SEQ - P), channel_multiplier=-8,
                      allow_small_or_imprecise_dtypes=True).then_inc(pool_own, 1)
            pool.wait_ge(pool_own, 1)
            pool.affine_select(out=bias8[:, :], in_=bias8[:, :], compare_op=ALU.is_ge, fill=-BIG,
                               base=SEQ - P, pattern=[[-1, SEQ]], channel_multiplier=1).then_inc(pool_own, 1)
            pool.wait_ge(pool_own, 2)
            with pool.Fori(0, HEADS) as h:
                pool.wait_ge(scores_read, h * TT + 1)
                pool.sem_inc(pool_own, 1)
                pool.tensor_scalar(bias8[:, :], bias8[:, :], 2.0 ** (-8.0 / HEADS), 1.0,
                                   ALU.mult, ALU.mult).then_inc(bias_ready, 1)
                pool.tensor_copy(vT[:, :], tile(qkvT, h + 8)).then_inc(v_ready, 1)

        @block.scalar
        def _(act):
            act.wait_ge(lam_sums, 2)
            act.activation(lam[:, 2:4], lam[:, 0:2], ACT.Exp).then_inc(lam_exp, 1)

            def split(h):
                if not isinstance(h, int) or h:
                    act.wait_ge(scores_done, h * TT)
                act.activation(q_hi[:, :], tile(qkvT, h), ACT.Copy).then_inc(qk_high, 1)
                act.activation(k_hi[:, :], tile(qkvT, h + 4), ACT.Copy).then_inc(qk_high, 1)

            def body(h, last):
                for s in range(TT + 3):
                    if s < TT:
                        act.wait_ge(max_ready, h * TT + (s + 1))
                        for c in range(2):
                            ins = act.activation(prob[:, s % 2, c, 0:width[s]], prob[:, s % 2, c, 0:width[s]], ACT.Exp,
                                                 bias=neg_max[:, s, c:c + 1], scale=QK ** -0.5,
                                                 accum_out=row_sum[:, s, c:c + 1])
                        ins.then_inc(exp_done, 1)
                    if s == 0:
                        act.wait_ge(turned, h * (TT + 1) + 1)
                        act.wait_ge(pv_done, h * TT + 2)
                        act.activation(v_nat[:, :, :], ps_t[:, :].rearrange("p (k n) -> p k n", n=P),
                                       ACT.Copy).then_inc(turned_out, 1)
                    if 1 <= s < TT + 1:
                        e = s - 1
                        act.wait_ge(turned, h * (TT + 1) + (e + 2))
                        act.wait_ge(pv_done, h * TT + (e + 1))
                        act.activation(attT[:, e % 2, 0:width[e]], ps_t[:, 0:width[e]], ACT.Copy).then_inc(turned_out, 1)
                    if s == TT - 1 and not last:
                        split(h + 1)
                    if 2 <= s < TT + 2:
                        e = s - 2
                        act.wait_ge(out_scaled, h * TT + (e + 1))
                        act.activation(junk[:, e % 2], ps_o[e % 2][:, 0:DH], ACT.Square, scale=inv_sum[:, e, 0:1],
                                       accum_out=head_ss[:, span(h * TT + tile_of[e], 1)]
                                       ).then_inc(out_squared, 1)

            split(0)
            heads(act, body)

        @block.vector
        def _(dve):
            link = Link(dve, dve_own)
            dve.sem_inc(scores_read, 1)
            dve.wait_ge(lam_loaded, 64)
            for n in range(2):
                dve.tensor_tensor_reduce(lam_in[:, 2 * n, :], lam_in[:, 2 * n, :], lam_in[:, 2 * n + 1, :], 1.0, 0.0,
                                         ALU.mult, ALU.add, lam[:, n:n + 1]).then_inc(lam_sums, 1)
            dve.wait_ge(lam_exp, 1)
            link(dve.tensor_tensor(lam[:, 4:5], lam[:, 3:4], lam[:, 2:3], ALU.subtract))
            link(dve.tensor_scalar(lam[:, 5:6], lam[:, 4:5], -LAM_INIT, None, ALU.add))

            def split(h):
                dve.wait_ge(qk_high, h * 2 + 2)
                dve.tensor_tensor(q_lo[:, :], tile(qkvT, h), q_hi[:, :].bitcast(F32), ALU.subtract).then_inc(qk_split, 1)
                dve.tensor_tensor(k_lo[:, :], tile(qkvT, h + 4), k_hi[:, :].bitcast(F32), ALU.subtract).then_inc(qk_split, 1)

            def body(h, last):
                for s in range(TT + 3):
                    if 1 <= s < TT + 1:
                        e = s - 1
                        dve.wait_ge(exp_done, h * TT + (e + 1))
                        link(dve.reciprocal(inv_sum[:, e, :], row_sum[:, e, :]))
                        link(dve.scalar_tensor_tensor(out=coef[:, e:e + 1], in0=row_sum[:, e, 0:1], scalar=lam[:, 5:6],
                                                      in1=inv_sum[:, e, 1:2], op0=ALU.mult, op1=ALU.mult))
                        dve.scalar_tensor_tensor(out=prob[:, e % 2, 0, 0:width[e]], in0=prob[:, e % 2, 1, 0:width[e]],
                                                 scalar=coef[:, e:e + 1], in1=prob[:, e % 2, 0, 0:width[e]],
                                                 op0=ALU.mult, op1=ALU.add).then_inc(att_ready, 1)
                    if s < TT:
                        if s == 0:
                            dve.wait_ge(bias_ready, h + 1)
                        dve.wait_ge(scores_done, h * TT + (s + 1))
                        dve.sem_inc(dve_seen, 1)
                        b = bias8[:, SEQ - width[s]:SEQ]
                        dve.tensor_tensor_reduce(prob[:, s % 2, 0, 0:width[s]], ps_s[0][:, 0:width[s]], b, 1.0, -3e38,
                                                 ALU.add, ALU.max, row_max[:, s, 0:1])
                        link(dve.tensor_tensor_reduce(prob[:, s % 2, 1, 0:width[s]], ps_s[1][:, 0:width[s]], b, 1.0,
                                                      -3e38, ALU.add, ALU.max, row_max[:, s, 1:2]))
                        dve.sem_inc(scores_read, 1)
                        dve.tensor_scalar(neg_max[:, s, :], row_max[:, s, :], -(QK ** -0.5), None,
                                          ALU.mult).then_inc(max_ready, 1)
                    if s == TT - 1 and not last:
                        split(h + 1)
                    if 2 <= s < TT + 2:
                        e = s - 2
                        dve.wait_ge(pv_done, h * TT + (e + 3))
                        qt = slice(tile_of[e] * P, tile_of[e] * P + P)
                        o = mixT[:, span(h + 4, 1), qt]
                        dve.tensor_scalar(o.rearrange("p o n -> p (o n)"), ps_o[e % 2][:, 0:DH], inv_sum[:, e, 0:1], None,
                                          ALU.mult).then_inc(out_scaled, 1)

            split(0)
            with dve.Fori(0, HEADS - 1) as h:
                link.loop(h, 3 * TT)
                body(h, False)
            link.again(HEADS - 1)
            body(HEADS - 1, True)
            link.end(HEADS)

        @block.tensor
        def _(pe):
            for free, n in ((turned_out, 1), (pv_done, 2), (out_squared, 2)):
                pe.sem_inc(free, n)

            def scores(h, s):
                if s == 0:
                    pe.wait_ge(qk_split, h * 2 + 2)
                pe.wait_ge(scores_read, h * TT + (s + 1))
                qt = slice(tile_of[s] * P, tile_of[s] * P + P)
                for lo in range(0, width[s], HALF):
                    cols = slice(lo, min(lo + HALF, width[s]))
                    for ql, kr, start, stop in ((q_hi, k_hi, True, False), (q_hi, k_lo, False, False), (q_lo, k_hi, False, True)):
                        for c in range(2):
                            half = slice(QK * c, QK * c + QK)
                            mm = pe.matmul(ps_s[c][:, cols], ql[half, qt], kr[half, cols], start=start, stop=stop)
                mm.then_inc(scores_done, 1)

            def body(h, last):
                for s in range(TT + 3):
                    if s < TT:
                        scores(h, s)
                    if s == 0:
                        pe.wait_ge(turned_out, h * (TT + 1) + 1)
                        pe.wait_ge(v_ready, h + 1)
                        for k in range(TT):
                            mm = pe.transpose(ps_t[:, k * P:(k + 1) * P], vT[:, k * P:(k + 1) * P], ident[:, :])
                        mm.then_inc(turned, 1)
                    if 2 <= s < TT + 2:
                        e = s - 2
                        pe.wait_ge(turned_out, h * (TT + 1) + (e + 3))
                        pe.wait_ge(out_squared, h * TT + (e + 1))
                        for k in range(TT - e):
                            mm = pe.matmul(ps_o[e % 2][:, 0:DH], attT[:, e % 2, k * P:(k + 1) * P], v_nat[:, k, :],
                                           start=k == 0, stop=k == TT - e - 1)
                        mm.then_inc(pv_done, 1)
                    if 1 <= s < TT + 1:
                        e = s - 1
                        pe.wait_ge(att_ready, h * TT + (e + 1))
                        pe.wait_ge(turned_out, h * (TT + 1) + (e + 2))
                        for k in range(TT - e):
                            mm = pe.transpose(ps_t[:, k * P:(k + 1) * P], prob[:, e % 2, 0, k * P:(k + 1) * P], ident[:, :])
                        mm.then_inc(turned, 1)

            heads(pe, body)


def stage(a, b, k):
    n, half, par = a * 2 + (b - k), a + (b - k) // 2, (b - k) % 2
    return None if isinstance(a, int) and not 0 <= n < TT else (n, half, par)


def tile_steps(eng, emit, link=None, per=0):
    for b in (-1, 0, 1):
        emit(0, b)
    with eng.Fori(0, 2) as i:
        if link:
            link.loop(i, per)
        emit(i, 2)
        emit(i, 3)
    if link:
        link.end(2)
    for b in (6, 7, 8, 9):
        emit(0, b)


def need(eng, sem, value):
    if not isinstance(value, int) or value > 0:
        eng.wait_ge(sem, value)


def mix_out(nc, io, persist):
    mixT, ident, head_ss, logits = (persist[n] for n in ("mixT", "ident", "head_ss", "logits"))
    with ExitStack() as ctx:
        sb = lambda name, shape, dt=F32: ctx.enter_context(nc.sbuf_tensor(name, shape, dt))
        sem = lambda name: ctx.enter_context(nc.semaphore(name))
        wout_raw = sb("wout_raw", [P, KT, D])
        wout_hi = sb("wout_hi", [P, KT, D], F32R)
        wout_lo = sb("wout_lo", [P, KT, D], F32R)
        c_hi = sb("c_hi", [P, 2, KT, P], F32R)
        c_lo = sb("c_lo", [P, 2, KT, P], F32R)
        heads_n = sb("heads_n", [P, 2, HEADS * DH])
        x_sb = sb("x_sb", [P, 2, D])
        x2_sb = sb("x2_sb", [P, 2, D])
        hn_sb = sb("hn_sb", [P, 2, D])
        hnT = sb("hnT", [P, 2, KT, P])
        norm_w = sb("ffn_w", [P, D])
        head_w = sb("head_w", [P, DH])
        head_r = sb("head_r", [P, HEADS * TT])
        w_rt = sb("w_rt", [P, KT, NG + NE])
        b_rt = sb("b_rt", [P, NG + NE])
        stat = sb("stat3", [P, 3, TT])
        eps = sb("eps3", [P, 2])
        ps_c = [ctx.enter_context(nc.psum_tensor(f"ps_c{n}", [P, HALF], F32)) for n in range(2)]
        ps_y = [ctx.enter_context(nc.psum_tensor(f"ps_y{n}", [P, D], F32)) for n in range(2)]
        ps_h = ctx.enter_context(nc.psum_tensor("ps_h", [P, D], F32))

        small_in = sem("small_in")
        wout_in = [sem(f"wout_in{n}") for n in range(3)]
        x_in = [sem(f"x3_in{n}") for n in range(2)]
        x2_out = [sem(f"x2_out{n}") for n in range(2)]
        hn_out = [sem(f"hn_out{n}") for n in range(2)]
        eps_set = sem("eps_set")
        head_root = sem("head_root")
        wout_high = sem("wout_high")
        wout_split = sem("wout_split")
        heads_ready = sem("heads_ready")
        c_turned = sem("c_turned")
        c_high = sem("c_high")
        c_split = sem("c_split")
        y_done = sem("y_done")
        x2_ready = sem("x2_ready")
        root_ready = sem("root3_ready")
        hn_ready = sem("hn_ready")
        hn_turned = sem("hn_turned")
        hnT_ready = sem("hnT_ready")
        routed = sem("routed")
        logits_ready = sem("logits_ready")
        act_own = sem("act_own3")
        dve_own = sem("dve_own3")
        block = ctx.enter_context(nc.Block("mix"))
        k_order = [4, 5, 6, 7, 0, 1, 2, 3]
        wout_loads = [(4, 5), (5, 8), (0, 4)]

        @block.sync
        def _(sp):
            sp.dma_start(head_w[:, :], io["head_norm_w"][0].partition_broadcast(P)).then_inc(small_in, 16)
            sp.dma_start(norm_w[:, :], io["ffn_norm_w"][0].partition_broadcast(P)).then_inc(small_in, 16)
            sp.dma_start(w_rt[:, :, 0:NG], io["w_router_group"][0].rearrange("(k p) n -> p k n", p=P)).then_inc(small_in, 16)
            sp.dma_start(w_rt[:, :, NG:], io["w_router_expert"][0].rearrange("(k p) n -> p k n", p=P)).then_inc(small_in, 16)
            sp.dma_start(b_rt[:, 0:NG], io["b_router_group"][0].partition_broadcast(P)).then_inc(small_in, 16)
            sp.dma_start(b_rt[:, NG:], io["b_router_expert"][0].partition_broadcast(P)).then_inc(small_in, 16)

            for n, (lo, hi) in enumerate(wout_loads):
                sp.dma_start(wout_raw[:, lo:hi], io["w_out"][0][lo * P:hi * P, :].rearrange("(k p) n -> p k n", p=P)
                             ).then_inc(wout_in[n], 16)

            def emit(a, b):
                if at := stage(a, b, -1):
                    n, half, par = at
                    need(sp, x2_ready, n - 1)
                    sp.dma_start(x_sb[:, par], io["x"][0][span(n * P, P), :]).then_inc(x_in[par], 16)
                if at := stage(a, b, 1):
                    n, half, par = at
                    sp.wait_ge(x2_ready, n + 1)
                    sp.dma_start(persist["x2_d"][span(n * P, P), :], x2_sb[:, par]).then_inc(x2_out[par], 16)
                    sp.wait_ge(hn_ready, n + 1)
                    sp.dma_start(persist["hn_d"][span(n * P, P), :], hn_sb[:, par]).then_inc(hn_out[par], 16)

            tile_steps(sp, emit)
            for par in range(2):
                sp.wait_ge(x2_out[par], 16 * (TT // 2))
                sp.wait_ge(hn_out[par], 16 * (TT // 2))

        @block.gpsimd
        def _(pool):
            pool.memset(eps[:, 0:1], HEAD_EPS).then_inc(eps_set, 1)
            pool.memset(eps[:, 1:2], NORM_EPS).then_inc(eps_set, 1)

        @block.scalar
        def _(act):
            link = Link(act, act_own)
            act.wait_ge(eps_set, 2)
            act.activation(head_r[:, :], head_ss[:, :], ACT.Sqrt, bias=eps[:, 0:1], scale=1.0 / DH).then_inc(head_root, 1)

            def emit(a, b):
                if at := stage(a, b, -1):
                    n, half, par = at
                    need(act, y_done, n - 1)
                    act.wait_ge(c_turned, n + 1)
                    act.activation(c_hi[:, par, 0:4], ps_c[par][:, :].rearrange("p (k n) -> p k n", n=P),
                                   ACT.Copy).then_inc(c_high, 1)
                    act.activation(c_hi[:, par, 4:8], mixT[:, 0:4, span(n * P, P)], ACT.Copy).then_inc(c_high, 1)
                if isinstance(a, int) and b == -1:
                    for k in k_order:
                        for n, (lo, hi) in enumerate(wout_loads):
                            if k == lo:
                                act.wait_ge(wout_in[n], 16)
                        act.activation(wout_hi[:, k], wout_raw[:, k], ACT.Copy).then_inc(wout_high, 1)
                if at := stage(a, b, 0):
                    n, half, par = at
                    act.wait_ge(x2_ready, n + 1)
                    need(act, hn_out[par], half * 16)
                    need(act, hn_turned, n - 1)
                    link(act.activation(hn_sb[:, par], x2_sb[:, par], ACT.Square, accum_out=stat[:, 0, span(n, 1)]))
                    act.activation(stat[:, 1, span(n, 1)], stat[:, 0, span(n, 1)], ACT.Sqrt, bias=eps[:, 1:2],
                                   scale=1.0 / D).then_inc(root_ready, 1)
                if at := stage(a, b, 1):
                    n, half, par = at
                    act.wait_ge(hn_turned, n + 1)
                    act.wait_ge(routed, n)
                    act.activation(hnT[:, par], ps_h[:, :].rearrange("p (k n) -> p k n", n=P), ACT.Copy).then_inc(hnT_ready, 1)

            tile_steps(act, emit, link, 2)

        @block.vector
        def _(dve):
            link = Link(dve, dve_own)
            dve.sem_inc(logits_ready, 1)
            dve.sem_inc(routed, 1)
            dve.wait_ge(small_in, 96)
            link(dve.tensor_scalar(head_w[:, :], head_w[:, :], 1.0 - LAM_INIT, None, ALU.mult))
            dve.wait_ge(head_root, 1)
            link(dve.reciprocal(head_r[:, :], head_r[:, :]))

            def emit(a, b):
                if at := stage(a, b, -1):
                    n, half, par = at
                    need(dve, c_turned, n - 1)
                    for h in range(HEADS):
                        ins = dve.scalar_tensor_tensor(out=heads_n[:, par, h * DH:(h + 1) * DH],
                                                       in0=mixT[:, 4 + h, span(n * P, P)],
                                                       scalar=head_r[:, span(n + h * TT, 1)], in1=head_w[:, :],
                                                       op0=ALU.mult, op1=ALU.mult)
                    ins.then_inc(heads_ready, 1)
                    dve.wait_ge(c_high, n * 2 + 2)
                    dve.tensor_tensor(c_lo[:, par, 0:4], ps_c[par][:, :].rearrange("p (k n) -> p k n", n=P),
                                      c_hi[:, par, 0:4].bitcast(F32), ALU.subtract)
                    dve.tensor_tensor(c_lo[:, par, 4:8], mixT[:, 0:4, span(n * P, P)],
                                      c_hi[:, par, 4:8].bitcast(F32), ALU.subtract).then_inc(c_split, 1)
                if isinstance(a, int) and b == -1:
                    for j, k in enumerate(k_order):
                        dve.wait_ge(wout_high, j + 1)
                        dve.tensor_tensor(wout_lo[:, k], wout_raw[:, k], wout_hi[:, k].bitcast(F32),
                                          ALU.subtract).then_inc(wout_split, 1)
                if at := stage(a, b, 0):
                    n, half, par = at
                    dve.wait_ge(y_done, n + 1)
                    dve.wait_ge(x_in[par], half * 16 + 16)
                    need(dve, x2_out[par], half * 16)
                    dve.tensor_tensor(x2_sb[:, par], ps_y[par][:, :], x_sb[:, par], ALU.add).then_inc(x2_ready, 1)
                    dve.wait_ge(root_ready, n + 1)
                    link(dve.reciprocal(stat[:, 2, span(n, 1)], stat[:, 1, span(n, 1)]))
                    dve.scalar_tensor_tensor(out=hn_sb[:, par], in0=x2_sb[:, par], scalar=stat[:, 2, span(n, 1)],
                                             in1=norm_w[:, :], op0=ALU.mult, op1=ALU.mult).then_inc(hn_ready, 1)
                if at := stage(a, b, 2):
                    n, half, par = at
                    dve.wait_ge(routed, n + 2)
                    dve.tensor_tensor(logits[:, span(n, 1)].rearrange("p o n -> p (o n)"), ps_c[par][:, 0:NG + NE],
                                      b_rt[:, :], ALU.add).then_inc(logits_ready, 1)

            tile_steps(dve, emit, link, 2)

        @block.tensor
        def _(pe):
            def emit(a, b):
                if at := stage(a, b, -1):
                    n, half, par = at
                    pe.wait_ge(heads_ready, n + 1)
                    need(pe, c_split, n - 1)
                    need(pe, logits_ready, n - 2)
                    for h in range(HEADS):
                        mm = pe.transpose(ps_c[par][:, h * DH:(h + 1) * DH], heads_n[:, par, h * DH:(h + 1) * DH], ident[:, :])
                    mm.then_inc(c_turned, 1)
                if at := stage(a, b, 0):
                    n, half, par = at
                    pe.wait_ge(c_split, n + 1)
                    need(pe, x2_ready, n - 1)
                    for j, k in enumerate(k_order):
                        if isinstance(n, int) and n == 0:
                            pe.wait_ge(wout_split, j + 1)
                        mm = split_products(pe, [ps_y[par][:, h * HALF:(h + 1) * HALF] for h in range(2)],
                                            c_hi[:, par, k], c_lo[:, par, k],
                                            [wout_hi[:, k, h * HALF:(h + 1) * HALF] for h in range(2)],
                                            [wout_lo[:, k, h * HALF:(h + 1) * HALF] for h in range(2)],
                                            j == 0, j == KT - 1)
                    mm.then_inc(y_done, 1)
                if at := stage(a, b, 2):
                    n, half, par = at
                    pe.wait_ge(hnT_ready, n + 1)
                    if isinstance(n, int):
                        need(pe, logits_ready, n)
                    for k in range(KT):
                        mm = pe.matmul(ps_c[par][:, 0:NG + NE], hnT[:, par, k], w_rt[:, k], start=k == 0, stop=k == KT - 1)
                    mm.then_inc(routed, 1)
                if at := stage(a, b, 1):
                    n, half, par = at
                    pe.wait_ge(hn_ready, n + 1)
                    need(pe, hnT_ready, n)
                    for k in range(KT):
                        mm = pe.transpose(ps_h[:, k * P:(k + 1) * P], hn_sb[:, par, k * P:(k + 1) * P], ident[:, :])
                    mm.then_inc(hn_turned, 1)

            tile_steps(pe, emit)


def route(nc, io, persist):
    ident, logits, gates, slots, extra = (persist[n] for n in ("ident", "logits", "gates", "slots", "extra"))
    with ExitStack() as ctx:
        sb = lambda name, shape, dt=F32: ctx.enter_context(nc.sbuf_tensor(name, shape, dt))
        sem = lambda name: ctx.enter_context(nc.semaphore(name))
        gmax = sb("gmax", [P, TT])
        gcand = sb("gcand", [P, TT, NG])
        gidx = sb("gidx", [P, TT])
        gexp = sb("gexp", [P, TT, NG])
        gsum = sb("gsum", [P, TT])
        masked = sb("masked", [P, TT, NE])
        cand = sb("cand", [P, TT, NE])
        top = sb("top", [P, 2, TT])
        idx = sb("idx", [P, TT])
        hot = sb("hot", [P, 2, TT, NE])
        both = sb("both", [P, TT, NE])
        diff = sb("diff", [P, 4, TT])
        cum = sb("cum", [P, TT + 1, NE])
        pos = sb("pos", [P, TT + 1, NE])
        more = sb("more", [P, NE])
        upto = sb("upto", [P, NE])
        base = sb("base", [P, NE])
        slot_e = sb("slot_e", [P, TT, NE])
        slot_f = sb("slot_f", [P, 2, TT])
        before = sb("before", [P, NX, NE])
        extra_f = sb("extra_f", [P, NX + 1])
        iota_g = sb("iota_g", [P, TT, NG])
        iota_e = sb("iota_e", [P, TT, NE])
        iota_s = sb("iota_s", [P, NE])
        iota_x = sb("iota_x", [P, NX, NE])
        ones = sb("ones", [P, P])
        earlier = sb("earlier", [P, P])
        token = sb("token", [P, TT], I32)
        zero = sb("zero", [P, SLOTS // P], I32)
        ps = ctx.enter_context(nc.psum_tensor("ps_pos", [P, HALF], F32))

        set_up = sem("set_up")
        zeroed = sem("zeroed")
        exp_asked = sem("exp_asked")
        exp_given = sem("exp_given")
        counts_asked = sem("counts_asked")
        counted = sem("counted")
        slots_ready = sem("slots_ready")
        scattered = sem("scattered")
        dve_own = sem("dve_own4")
        block = ctx.enter_context(nc.Block("route"))

        @block.sync
        def _(sp):
            sp.wait_ge(set_up, 7)
            sp.dma_start(persist["slot_token"].rearrange("(p n) o -> p (n o)", p=P), zero[:, :]).then_inc(zeroed, 16)

        @block.gpsimd
        def _(pool):
            f = dict(allow_small_or_imprecise_dtypes=True)
            pool.iota(iota_g[:, :, :], [[0, TT], [1, NG]], base=-NG, channel_multiplier=0, **f).then_inc(set_up, 1)
            pool.iota(iota_e[:, :, :], [[0, TT], [1, NE]], base=-NE, channel_multiplier=0, **f).then_inc(set_up, 1)
            pool.iota(iota_s[:, :], [[P, NE]], base=0, channel_multiplier=0, **f).then_inc(set_up, 1)
            pool.iota(iota_x[:, :, :], [[1, NX], [0, NE]], base=0, channel_multiplier=0, **f).then_inc(set_up, 1)
            pool.iota(token[:, :], [[P, TT]], base=0, channel_multiplier=1).then_inc(set_up, 1)
            pool.memset(zero[:, :], 0).then_inc(set_up, 1)
            pool.memset(ones[:, :], 1.0).then_inc(set_up, 1)
            pool.wait_ge(set_up, 7)
            pool.affine_select(out=earlier[:, :], in_=ones[:, :], compare_op=ALU.is_gt, fill=0.0, base=0,
                               pattern=[[1, P]], channel_multiplier=-1).then_inc(set_up, 1)
            pool.wait_ge(zeroed, 16)
            pool.wait_ge(slots_ready, 1)
            for which in range(2):
                for t in range(TT):
                    pool.indirect_dma_start(
                        out=persist["slot_token"], in_=token[:, t:t + 1], in_offset=None,
                        out_offset=bass.IndirectOffsetOnAxis(ap=slots[:, which, t:t + 1], axis=0)).then_inc(scattered, 16)
            pool.wait_ge(scattered, 16 * 2 * TT)

        @block.scalar
        def _(act):
            act.wait_ge(exp_asked, 1)
            act.activation(gexp[:, :, :], gexp[:, :, :], ACT.Exp).then_inc(exp_given, 1)
            act.wait_ge(exp_asked, 2)
            act.activation(diff[:, 1, :], diff[:, 0, :], ACT.Exp).then_inc(exp_given, 1)

        @block.vector
        def _(dve):
            link = Link(dve, dve_own)
            lg, le = logits[:, :, 0:NG], logits[:, :, NG:]
            wide_g = lambda x: x.unsqueeze(2).to_broadcast([P, TT, NG])
            wide_e = lambda x: x.unsqueeze(2).to_broadcast([P, TT, NE])
            per_tile = lambda x: x.unsqueeze(1).to_broadcast([P, TT, NE])
            dve.wait_ge(set_up, 8)

            def first_max(value, number, where, index, values, wide, one_hot):
                link(dve.tensor_reduce(values, value, AX.X, ALU.max))
                link(dve.tensor_tensor(where, value, wide(values), ALU.is_equal))
                link(dve.tensor_tensor(where, where, number, ALU.mult))
                link(dve.tensor_reduce(index, where, AX.X, ALU.min))
                link(dve.tensor_tensor(one_hot, number, wide(index), ALU.is_equal))

            first_max(lg, iota_g[:, :, :], gcand[:, :, :], gidx[:, :], gmax[:, :], wide_g, gcand[:, :, :])
            dve.tensor_tensor(gexp[:, :, :], lg, wide_g(gmax[:, :]), ALU.subtract).then_inc(exp_asked, 1)
            link(dve.tensor_scalar(gcand[:, :, :], gcand[:, :, :], -1.0, BIG, ALU.add, ALU.mult))
            link(dve.tensor_tensor(masked[:, :, :].rearrange("p t (g e) -> p t g e", g=NG),
                                   le.rearrange("p t (g e) -> p t g e", g=NG),
                                   gcand[:, :, :].unsqueeze(3).to_broadcast([P, TT, NG, EPG]), ALU.add))
            first_max(masked[:, :, :], iota_e[:, :, :], cand[:, :, :], idx[:, :], top[:, 0, :], wide_e, hot[:, 0])
            link(dve.scalar_tensor_tensor(out=masked[:, :, :].rearrange("p t e -> p (t e)"),
                                          in0=hot[:, 0].rearrange("p t e -> p (t e)"), scalar=-BIG,
                                          in1=masked[:, :, :].rearrange("p t e -> p (t e)"), op0=ALU.mult, op1=ALU.add))
            first_max(masked[:, :, :], iota_e[:, :, :], cand[:, :, :], idx[:, :], top[:, 1, :], wide_e, hot[:, 1])
            dve.tensor_tensor(diff[:, 0, :], top[:, 1, :], top[:, 0, :], ALU.subtract).then_inc(exp_asked, 1)
            link(dve.tensor_tensor(both[:, :, :], hot[:, 0], hot[:, 1], ALU.add))
            link(dve.memset(cum[:, 0, :], 0.0))
            for t in range(TT):
                link(dve.tensor_tensor(cum[:, t + 1, :], cum[:, t, :], both[:, t, :], ALU.add))
            dve.sem_inc(counts_asked, 1)
            dve.wait_ge(exp_given, 1)
            link(dve.tensor_reduce(gsum[:, :], gexp[:, :, :], AX.X, ALU.add))
            link(dve.reciprocal(gsum[:, :], gsum[:, :]))
            dve.wait_ge(exp_given, 2)
            link(dve.tensor_scalar(diff[:, 2, :], diff[:, 1, :], 1.0, None, ALU.add))
            link(dve.reciprocal(diff[:, 2, :], diff[:, 2, :]))
            link(dve.tensor_tensor(gates[:, 0, :], diff[:, 2, :], gsum[:, :], ALU.mult))
            link(dve.tensor_tensor(gates[:, 1, :], gates[:, 0, :], diff[:, 1, :], ALU.mult))
            dve.wait_ge(counted, 1)
            link(dve.tensor_copy(pos[:, :, :].rearrange("p t e -> p (t e)"), ps[:, 0:(TT + 1) * NE]))
            count = pos[:, TT, :]
            link(dve.tensor_scalar(more[:, :], count, float(P), None, ALU.is_gt))
            for n in range(2, SEQ // P):
                link(dve.scalar_tensor_tensor(out=more[:, :], in0=count, scalar=float(n * P), in1=more[:, :],
                                              op0=ALU.is_gt, op1=ALU.add))
            link(dve.tensor_tensor_scan(upto[:, :], ones[:, 0:NE], more[:, :], 0.0, ALU.mult, ALU.add))
            link(dve.tensor_tensor(base[:, :], upto[:, :], more[:, :], ALU.subtract))
            link(dve.tensor_scalar(base[:, :], base[:, :], float(P), float((NE - 1) * P), ALU.mult, ALU.add))
            link(dve.tensor_tensor(base[:, :], base[:, :], iota_s[:, :], ALU.subtract))
            link(dve.tensor_scalar(slot_e[:, :, :], pos[:, 0:TT, :], float(P), None, ALU.is_ge))
            link(dve.tensor_tensor(slot_e[:, :, :], slot_e[:, :, :], per_tile(base[:, :]), ALU.mult))
            link(dve.tensor_tensor(slot_e[:, :, :], slot_e[:, :, :], pos[:, 0:TT, :], ALU.add))
            link(dve.tensor_tensor(slot_e[:, :, :], slot_e[:, :, :], per_tile(iota_s[:, :]), ALU.add))
            for which in range(2):
                link(dve.tensor_tensor(cand[:, :, :], slot_e[:, :, :], hot[:, which], ALU.mult))
                link(dve.tensor_reduce(slot_f[:, which, :], cand[:, :, :], AX.X, ALU.add))
            link(dve.tensor_copy(slots[:, :, :], slot_f[:, :, :]))
            dve.sem_inc(slots_ready, 1)
            link(dve.tensor_tensor(before[:, :, :], upto[:, :].unsqueeze(1).to_broadcast([P, NX, NE]),
                                   iota_x[:, :, :], ALU.is_le))
            link(dve.tensor_reduce(extra_f[:, 0:NX], before[:, :, :], AX.X, ALU.add))
            link(dve.tensor_scalar(extra_f[:, 0:NX], extra_f[:, 0:NX], float(NE - 1), None, ALU.min))
            link(dve.tensor_copy(extra_f[:, NX:], upto[:, NE - 1:]))
            link(dve.tensor_copy(extra[:, :], extra_f[:, :]))

        @block.tensor
        def _(pe):
            pe.wait_ge(counts_asked, 1)
            pe.matmul(ps[:, 0:(TT + 1) * NE], ones[:, :], cum[:, :, :].rearrange("p t e -> p (t e)"), start=True,
                      stop=False, skip_group_check=True)
            pe.matmul(ps[:, 0:TT * NE], earlier[:, :], both[:, :, :].rearrange("p t e -> p (t e)"), start=False,
                      stop=True, skip_group_check=True).then_inc(counted, 1)


RING = 6
UNITS = KT + FT


def unit_number(s, u):
    if isinstance(s, int) and s in (0, NE):
        return u if s == 0 else s * UNITS - UNITS + u
    return s * UNITS + (u - FT)


class StepSems:

    def __init__(self, sem, tag, buffers):
        self.gu_in = [sem(f"{tag}_gu_in{p}") for p in range(buffers)]
        self.d_in = [sem(f"{tag}_d_in{p}") for p in range(buffers)]
        self.token_in = [sem(f"{tag}_token_in{p}") for p in range(buffers)]
        self.x_in = [sem(f"{tag}_x_in{p}") for p in range(buffers)]
        self.y_out = [sem(f"{tag}_y_out{p}") for p in range(buffers)]
        self.split_high = sem(f"{tag}_split_high")
        self.split_low = sem(f"{tag}_split_low")
        self.units_done = sem(f"{tag}_units_done")
        self.x_turned = sem(f"{tag}_x_turned")
        self.x_high = sem(f"{tag}_x_high")
        self.x_ready = sem(f"{tag}_x_ready")
        self.h_act_ready = sem(f"{tag}_h_act_ready")
        self.h_ready = sem(f"{tag}_h_ready")
        self.h_turned = sem(f"{tag}_h_turned")
        self.h_high = sem(f"{tag}_h_high")
        self.h_split = sem(f"{tag}_h_split")
        self.y_ready = sem(f"{tag}_y_ready")
        self.y_free = sem(f"{tag}_y_free")


def experts(nc, io, persist):
    ident, extra = persist["ident"], persist["extra"]
    slot_token, hn_d, y_d = (persist[n] for n in ("slot_token", "hn_d", "y_d"))
    with ExitStack() as ctx:
        sb = lambda name, shape, dt=F32: ctx.enter_context(nc.sbuf_tensor(name, shape, dt))
        sem = lambda name: ctx.enter_context(nc.semaphore(name))
        gu_raw = sb("gu_raw", [P, 2, 2, KT, FF])
        d_raw = sb("d_raw", [P, 2, FT, D])
        w_hi = sb("w5_hi", [P, RING, D], F32R)
        w_lo = sb("w5_lo", [P, RING, D], F32R)
        token = sb("token5", [P, 2], I32)
        x_sb = sb("x5_sb", [P, 2, D])
        x_hi = sb("x5_hi", [P, 2, KT, P], F32R)
        x_lo = sb("x5_lo", [P, 2, KT, P], F32R)
        h_act = sb("h_act", [P, FF])
        h_sb = sb("h_sb", [P, FF])
        h_hi = sb("h_hi", [P, FT, P], F32R)
        h_lo = sb("h_lo", [P, FT, P], F32R)
        y_sb = sb("y_sb", [P, 2, D])
        ps_gu = [ctx.enter_context(nc.psum_tensor(f"ps_gu{n}", [P, 2, HALF], F32)) for n in range(2)]
        ps_y = ctx.enter_context(nc.psum_tensor("ps_y5", [P, 2, HALF], F32))
        ps_t = ctx.enter_context(nc.psum_tensor("ps_t5", [P, 2, HALF], F32))

        m, x = StepSems(sem, "main", 2), StepSems(sem, "more", 1)
        pool_seen = sem("pool_seen")
        block = ctx.enter_context(nc.Block("experts"))


        def load_gate_up(sp, q, e, par):
            for which, name in enumerate(("w_exp_gate", "w_exp_up")):
                sp.dma_start(gu_raw[:, par, which],
                             io[name][0][span(e, 1)].rearrange("o (k p) n -> p (o k) n", p=P)).then_inc(q.gu_in[par], 16)

        def load_down(sp, q, e, par):
            sp.dma_start(d_raw[:, par],
                         io["w_exp_down"][0][span(e, 1)].rearrange("o (f p) n -> p (o f) n", p=P)).then_inc(q.d_in[par], 16)

        def raw_unit(u, par):
            return gu_raw[:, par, :, u] if u < KT else d_raw[:, par, u - KT].rearrange("p (a n) -> p a n", a=2)

        def two(tensor, r):
            return tensor[:, r].rearrange("p (a n) -> p a n", a=2)

        def turned_rows(bank):
            return bank.rearrange("p a (k n) -> p (a k) n", n=P)


        def high(act, q, n, r, u, par):
            if n is not None:
                need(act, q.units_done, n - (RING - 1))
            act.activation(two(w_hi, r), raw_unit(u, par), ACT.Copy).then_inc(q.split_high, 1)

        def low(dve, q, n, r, u, par):
            dve.wait_ge(q.split_high, n + 1)
            dve.tensor_tensor(two(w_lo, r), raw_unit(u, par), two(w_hi, r).bitcast(F32),
                              ALU.subtract).then_inc(q.split_low, 1)

        def products(pe, q, n, r, outs, lh, ll, start, stop):
            pe.wait_ge(q.split_low, n + 1)
            split_products(pe, outs, lh, ll, [two(w_hi, r)[:, a] for a in range(2)],
                           [two(w_lo, r)[:, a] for a in range(2)], start, stop).then_inc(q.units_done, 1)


        def gather(pool, q, n, half, par, rows):
            pool.dma_start(token[:, par:par + 1], slot_token[span(rows, P), :]).then_inc(q.token_in[par], 16)
            pool.wait_ge(q.token_in[par], half * 16 + 16)
            pool.sem_inc(pool_seen, 1)
            pool.indirect_dma_start(out=x_sb[:, par], out_offset=None, in_=hn_d,
                                    in_offset=bass.IndirectOffsetOnAxis(ap=token[:, par:par + 1], axis=0)
                                    ).then_inc(q.x_in[par], 16)

        def turn_x(pe, q, par):
            for k in range(KT):
                mm = pe.transpose(ps_t[:, k // 4, (k % 4) * P:(k % 4 + 1) * P], x_sb[:, par, k * P:(k + 1) * P], ident[:, :])
            mm.then_inc(q.x_turned, 1)

        def x_high(act, q, n, par):
            act.wait_ge(q.x_turned, n + 1)
            act.activation(x_hi[:, par], turned_rows(ps_t[:, :, :]), ACT.Copy).then_inc(q.x_high, 1)

        def x_low(dve, q, n, par):
            dve.wait_ge(q.x_high, n + 1)
            dve.tensor_tensor(x_lo[:, par], turned_rows(ps_t[:, :, :]), x_hi[:, par].bitcast(F32),
                              ALU.subtract).then_inc(q.x_ready, 1)

        def silu(act, q, par):
            act.activation(h_act[:, :], ps_gu[par][:, 0], ACT.Silu).then_inc(q.h_act_ready, 1)

        def hidden(dve, q, n, par):
            dve.wait_ge(q.h_act_ready, n + 1)
            dve.tensor_tensor(h_sb[:, :], ps_gu[par][:, 1], h_act[:, :], ALU.mult).then_inc(q.h_ready, 1)

        def turn_h(pe, q, n):
            pe.wait_ge(q.h_ready, n + 1)
            for f in range(FT):
                mm = pe.transpose(ps_t[:, 0, f * P:(f + 1) * P], h_sb[:, f * P:(f + 1) * P], ident[:, :])
            mm.then_inc(q.h_turned, 1)

        def h_high(act, q, n):
            act.wait_ge(q.h_turned, n + 1)
            act.activation(h_hi[:, :, :], ps_t[:, 0].rearrange("p (f n) -> p f n", n=P), ACT.Copy).then_inc(q.h_high, 1)

        def h_low(dve, q, n):
            dve.wait_ge(q.h_high, n + 1)
            dve.tensor_tensor(h_lo[:, :, :], ps_t[:, 0].rearrange("p (f n) -> p f n", n=P),
                              h_hi[:, :, :].bitcast(F32), ALU.subtract).then_inc(q.h_split, 1)

        def take_y(dve, q, par):
            dve.tensor_copy(two(y_sb, par), ps_y[:, :, :]).then_inc(q.y_ready, 1)

        def store_y(sp, q, n, half, par, rows):
            sp.wait_ge(q.y_ready, n + 1)
            sp.dma_start(y_d[span(rows, P), :], y_sb[:, par]).then_inc(q.y_out[par], 16)
            sp.wait_ge(q.y_out[par], half * 16 + 16)
            sp.sem_inc(q.y_free, 1)

        gate_up, rows_y = [[ps_gu[p][:, a] for a in range(2)] for p in range(2)], [ps_y[:, a] for a in range(2)]

        def steps(eng, emit):
            emit(0, 0, 0)
            emit(1, 0, 1)
            with eng.Fori(0, (NE - 4) // 2) as i:
                emit(i * 2 + 2, i + 1, 0)
                emit(i * 2 + 3, i + 1, 1)
            for s in range(NE - 2, NE + 1):
                emit(s, s // 2, s % 2)

        def slot(s, u):
            return (u if isinstance(s, int) and s in (0, NE) else u - FT) % RING

        def more_chunks(eng, body):
            count = eng.value_load(extra[0:1, NX:NX + 1], min_val=0, max_val=NX)
            with eng.If(count > 0):
                with eng.Fori(0, count) as j:
                    body(j)

        def has(s, k=0):
            return not isinstance(s, int) or 0 <= s - k < NE

        @block.sync
        def _(sp):
            load_gate_up(sp, m, 0, 0)
            load_down(sp, m, 0, 0)
            load_gate_up(sp, m, 1, 1)

            def emit(s, half, par):
                if has(s, 2):
                    store_y(sp, m, s - 2, half - 1, par, (s - 2) * P)
                if has(s, -2):
                    sp.wait_ge(m.split_low, unit_number(s, KT))
                    load_gate_up(sp, m, s + 2, par)
                if has(s, -1):
                    if not isinstance(s, int) or s:
                        sp.wait_ge(m.split_low, unit_number(s, UNITS))
                    load_down(sp, m, s + 1, 1 - par)

            steps(sp, emit)
            emit(NE + 1, NE // 2, 1)
            sp.wait_ge(m.split_low, NE * UNITS)

            def chunk(j):
                e = sp.value_load(extra[0:1, bass.ds(j, 1)], min_val=0, max_val=NE - 1)
                load_gate_up(sp, x, e, 0)
                load_down(sp, x, e, 0)
                store_y(sp, x, j, j, 0, (j + NE) * P)

            more_chunks(sp, chunk)

        @block.gpsimd
        def _(pool):
            gather(pool, m, 0, 0, 0, 0)
            gather(pool, m, 1, 0, 1, P)
            with pool.Fori(1, NE // 2) as i:
                for par in range(2):
                    pool.wait_ge(m.x_turned, i * 2 + (par - 1))
                    gather(pool, m, i * 2 + par, i, par, (i * 2 + par) * P)
            pool.wait_ge(m.x_turned, NE)

            def chunk(j):
                gather(pool, x, j, j, 0, (j + NE) * P)
                pool.wait_ge(x.x_turned, j + 1)

            more_chunks(pool, chunk)

        @block.scalar
        def _(act):
            def emit(s, half, par):
                for u in range(UNITS):
                    if u == 1 and has(s):
                        x_high(act, m, s, par)
                    if u == 1 and has(s, 1):
                        act.wait_ge(m.units_done, unit_number(s - 1, KT))
                        need(act, m.h_ready, s - 1)
                        silu(act, m, 1 - par)
                    if u == KT + 1 and has(s, 1):
                        h_high(act, m, s - 1)
                    if u < KT and has(s):
                        if u == 0:
                            act.wait_ge(m.gu_in[par], half * 32 + 32)
                        high(act, m, unit_number(s, u), slot(s, u), u, par)
                    if u >= KT and has(s, 1):
                        if u == KT:
                            act.wait_ge(m.d_in[1 - par], (half + par) * 16)
                        high(act, m, unit_number(s, u), slot(s, u), u, 1 - par)

            steps(act, emit)
            act.wait_ge(m.units_done, NE * UNITS)

            def chunk(j):
                x_high(act, x, j, 0)
                act.wait_ge(x.gu_in[0], j * 32 + 32)
                for u in range(UNITS):
                    if u == KT:
                        act.wait_ge(x.units_done, j * UNITS + KT)
                        silu(act, x, 0)
                        h_high(act, x, j)
                        act.wait_ge(x.d_in[0], j * 16 + 16)
                    high(act, x, None if u < RING else j * UNITS + u, u % RING, u, 0)
                act.wait_ge(x.units_done, j * UNITS + UNITS)

            more_chunks(act, chunk)

        @block.vector
        def _(dve):
            dve.sem_inc(m.y_free, 2)

            def take(n, par):
                dve.wait_ge(m.units_done, unit_number(n + 1, UNITS))
                dve.wait_ge(m.y_free, n + 1)
                take_y(dve, m, par)

            def emit(s, half, par):
                for u in range(UNITS):
                    if u == 1 and has(s):
                        x_low(dve, m, s, par)
                    if u == 1 and has(s, 1):
                        hidden(dve, m, s - 1, 1 - par)
                    if u == 5 and has(s, 2):
                        take(s - 2, par)
                    if u == KT + 1 and has(s, 1):
                        h_low(dve, m, s - 1)
                    if (u < KT and has(s)) or (u >= KT and has(s, 1)):
                        low(dve, m, unit_number(s, u), slot(s, u), u, par if u < KT else 1 - par)

            steps(dve, emit)
            take(NE - 1, 1)
            dve.wait_ge(m.y_free, NE + 2)

            def chunk(j):
                x_low(dve, x, j, 0)
                for u in range(UNITS):
                    if u == KT:
                        hidden(dve, x, j, 0)
                        h_low(dve, x, j)
                    low(dve, x, j * UNITS + u, u % RING, u, 0)
                dve.wait_ge(x.units_done, j * UNITS + UNITS)
                take_y(dve, x, 0)
                dve.wait_ge(x.y_free, j + 1)

            more_chunks(dve, chunk)

        @block.tensor
        def _(pe):
            def turn_next(n, half, par):
                pe.wait_ge(m.x_in[par], half * 16 + 16)
                need(pe, m.x_ready, n)
                need(pe, m.h_split, n - 1)
                turn_x(pe, m, par)

            def emit(s, half, par):
                if isinstance(s, int) and s == 0:
                    turn_next(0, 0, 0)
                for u in range(KT):
                    if u == KT // 2 and has(s, 1):
                        turn_h(pe, m, s - 1)
                    if has(s):
                        if u == 0:
                            pe.wait_ge(m.x_ready, s + 1)
                            need(pe, m.h_ready, s - 1)
                        products(pe, m, unit_number(s, u), slot(s, u), gate_up[par], x_hi[:, par, u], x_lo[:, par, u],
                                 u == 0, u == KT - 1)
                if has(s, -1):
                    turn_next(s + 1, half + par, 1 - par)
                if has(s, 1):
                    pe.wait_ge(m.h_split, s)
                    need(pe, m.y_ready, s - 1)
                    for f in range(FT):
                        products(pe, m, unit_number(s, KT + f), slot(s, KT + f), rows_y, h_hi[:, f], h_lo[:, f],
                                 f == 0, f == FT - 1)

            steps(pe, emit)
            pe.wait_ge(m.y_ready, NE)

            def chunk(j):
                pe.wait_ge(x.x_in[0], j * 16 + 16)
                turn_x(pe, x, 0)
                pe.wait_ge(x.x_ready, j + 1)
                for u in range(KT):
                    products(pe, x, j * UNITS + u, u % RING, gate_up[0], x_hi[:, 0, u], x_lo[:, 0, u], u == 0, u == KT - 1)
                turn_h(pe, x, j)
                pe.wait_ge(x.h_split, j + 1)
                for f in range(FT):
                    products(pe, x, j * UNITS + KT + f, (KT + f) % RING, rows_y, h_hi[:, f], h_lo[:, f], f == 0, f == FT - 1)
                pe.wait_ge(x.y_ready, j + 1)

            more_chunks(pe, chunk)


def combine(nc, io, persist, out):
    gates, slots = persist["gates"], persist["slots"]
    with ExitStack() as ctx:
        sb = lambda name, shape, dt=F32: ctx.enter_context(nc.sbuf_tensor(name, shape, dt))
        sem = lambda name: ctx.enter_context(nc.semaphore(name))
        x2_sb = sb("x2_6", [P, TT, D])
        y_sb = sb("y_6", [P, 2, TT, D])
        o_sb = sb("o_6", [P, 2, D])
        norm_w = sb("final_w", [P, D])
        stat = sb("stat6", [P, 3, TT])
        eps = sb("eps6", [P, 1])
        norm_w_in = sem("final_w_in")
        x2_in = sem("x2_in")
        y_in = [sem(f"y_in{t}") for t in range(TT)]
        o_out = [sem(f"o_out{n}") for n in range(2)]
        eps_set = sem("eps_set6")
        sum_ready = sem("sum_ready")
        root_ready = sem("root6_ready")
        o_ready = sem("o_ready")
        act_own = sem("act_own6")
        dve_own = sem("dve_own6")
        block = ctx.enter_context(nc.Block("combine"))

        @block.sync
        def _(sp):
            for t in range(TT):
                sp.dma_start(x2_sb[:, t], persist["x2_d"][t * P:(t + 1) * P, :]).then_inc(x2_in, 16)
                if t == 0:
                    sp.dma_start(norm_w[:, :], io["final_norm_w"].partition_broadcast(P)).then_inc(norm_w_in, 16)
            for t in range(TT):
                sp.wait_ge(o_ready, t + 1)
                sp.dma_start(out[0][t * P:(t + 1) * P, :], o_sb[:, t % 2]).then_inc(o_out[t % 2], 16)
            for par in range(2):
                sp.wait_ge(o_out[par], 16 * (TT // 2))

        @block.gpsimd
        def _(pool):
            pool.memset(eps[:, :], NORM_EPS).then_inc(eps_set, 1)
            for t in range(TT):
                for which in range(2):
                    pool.indirect_dma_start(
                        out=y_sb[:, which, t], out_offset=None, in_=persist["y_d"],
                        in_offset=bass.IndirectOffsetOnAxis(ap=slots[:, which, t:t + 1], axis=0)).then_inc(y_in[t], 16)

        @block.vector
        def _(dve):
            link = Link(dve, dve_own)

            def add(t):
                dve.wait_ge(x2_in, 16 * TT)
                dve.wait_ge(y_in[t], 32)
                link(dve.scalar_tensor_tensor(out=x2_sb[:, t], in0=y_sb[:, 0, t], scalar=gates[:, 0, t:t + 1],
                                              in1=x2_sb[:, t], op0=ALU.mult, op1=ALU.add))
                dve.scalar_tensor_tensor(out=x2_sb[:, t], in0=y_sb[:, 1, t], scalar=gates[:, 1, t:t + 1],
                                         in1=x2_sb[:, t], op0=ALU.mult, op1=ALU.add).then_inc(sum_ready, 1)

            def norm(t):
                dve.wait_ge(root_ready, t + 1)
                link(dve.reciprocal(stat[:, 2, t:t + 1], stat[:, 1, t:t + 1]))
                need(dve, o_out[t % 2], 16 * (t // 2))
                dve.scalar_tensor_tensor(out=o_sb[:, t % 2], in0=x2_sb[:, t], scalar=stat[:, 2, t:t + 1],
                                         in1=norm_w[:, :], op0=ALU.mult, op1=ALU.mult).then_inc(o_ready, 1)

            dve.wait_ge(norm_w_in, 16)
            add(0)
            for t in range(TT):
                if t + 1 < TT:
                    add(t + 1)
                norm(t)

        @block.scalar
        def _(act):
            link = Link(act, act_own)
            act.wait_ge(eps_set, 1)
            for t in range(TT):
                act.wait_ge(sum_ready, t + 1)
                link(act.activation(y_sb[:, 0, t], x2_sb[:, t], ACT.Square, accum_out=stat[:, 0, t:t + 1]))
                act.activation(stat[:, 1, t:t + 1], stat[:, 0, t:t + 1], ACT.Sqrt, bias=eps[:, 0:1],
                               scale=1.0 / D).then_inc(root_ready, 1)


def build(nc, io, out):
    with ExitStack() as ctx:
        persist = {
            "ident": ctx.enter_context(nc.sbuf_tensor("ident", [P, P], F32)),
        }
        persist["head_ss"] = ctx.enter_context(nc.sbuf_tensor("head_ss", [P, HEADS * TT], F32))
        persist["logits"] = ctx.enter_context(nc.sbuf_tensor("logits", [P, TT, NG + NE], F32))
        persist["gates"] = ctx.enter_context(nc.sbuf_tensor("gates", [P, 2, TT], F32))
        persist["slots"] = ctx.enter_context(nc.sbuf_tensor("slots", [P, 2, TT], U32))
        persist["extra"] = ctx.enter_context(nc.sbuf_tensor("extra", [P, NX + 1], I32))
        persist["x2_d"] = nc.dram_tensor("x2_d", (SEQ, D), F32).ap()
        persist["hn_d"] = nc.dram_tensor("hn_d", (SEQ, D), F32).ap()
        persist["y_d"] = nc.dram_tensor("y_d", (SLOTS, D), F32).ap()
        persist["slot_token"] = nc.dram_tensor("slot_token", (SLOTS, 1), I32).ap()
        with nc.sbuf_tensor("mixT", [P, 2 * CT, SEQ], F32) as mixT:
            persist["mixT"] = mixT
            with nc.sbuf_tensor("qkvT", [P, 12, SEQ], F32) as qkvT:
                persist["qkvT"] = qkvT
                project_and_recur(nc, io, persist)
                attend(nc, io, persist)
            mix_out(nc, io, persist)
        route(nc, io, persist)
        experts(nc, io, persist)
        combine(nc, io, persist, out)


_INS = ["x", "mix_norm_w", "w_in", "lambda_q1", "lambda_k1", "lambda_q2", "lambda_k2", "head_norm_w", "conv_w",
        "conv_b", "w_rgate", "b_rgate", "w_igate", "b_igate", "lru_lambda", "w_out", "ffn_norm_w",
        "w_router_group", "b_router_group", "w_router_expert", "b_router_expert", "w_exp_gate", "w_exp_up",
        "w_exp_down", "final_norm_w"]


def kernel(**inputs):
    import numpy as _np
    import concourse.bacc as _bacc
    from concourse.bass_utils import run_bass_kernel_spmd as _run

    nc = _bacc.Bacc("TRN2", target_bir_lowering=False, num_devices=1)
    arrays, io = {}, {}
    for name in _INS:
        a = _np.ascontiguousarray(inputs[name])
        arrays[f"in_{name}"] = a
        io[name] = nc.dram_tensor(f"in_{name}", a.shape, mybir.dt.from_np(a.dtype), kind="ExternalInput").ap()
    out = nc.dram_tensor("out_0", (1, SEQ, D), F32, kind="ExternalOutput").ap()
    build(nc, io, out)
    r = _run(nc, [arrays], core_ids=[0])
    return r.results[0]["out_0"]
```

```python
from contextlib import ExitStack

import concourse.bass as bass
from concourse import mybir

P = 128
F32 = mybir.dt.float32
F32R = mybir.dt.float32r
I32 = mybir.dt.int32
U32 = mybir.dt.uint32
ALU = mybir.AluOpType
ACT = mybir.ActivationFunctionType
AX = mybir.AxisListType
SEQ = 1024
D = 1024
KT = D // P
TT = SEQ // P
HALF = 512
HEADS = 4
DH = 128
QK = 64
CT = 4
NORM_EPS = 1e-6
HEAD_EPS = 1e-5
LAM_INIT = 0.2
NG = 4
EPG = 8
NE = NG * EPG
FF = D // 2
FT = FF // P
NX = SEQ * 2 // P - 1
CHUNKS = NE + NX
BIG = 1e30


class Link:

    def __init__(self, eng, sem):
        self.eng, self.sem, self.n, self.i, self.per, self.mark = eng, sem, 0, None, 0, 0

    def loop(self, i, per):
        self.i, self.per, self.mark = i, per, self.n

    def again(self, i):
        assert self.n - self.mark == self.per, (self.n - self.mark, self.per)
        self.n, self.i = self.mark, i

    def end(self, times):
        assert self.n - self.mark == self.per, (self.n - self.mark, self.per)
        self.n, self.i = self.mark + self.per * times, None

    def __call__(self, ins):
        self.n += 1
        ins.then_inc(self.sem, 1)
        self.eng.wait_ge(self.sem, self.n if self.i is None else self.i * self.per + self.n)


def span(start, n):
    return slice(start, start + n) if isinstance(start, int) else bass.ds(start, n)


def split_products(pe, out, lh, ll, rh, rl, start, stop):
    nc_mm = pe.matmul
    for o, h in zip(out, range(len(out))):
        nc_mm(o, lh, rh[h], start=start, stop=False)
    for o, h in zip(out, range(len(out))):
        nc_mm(o, lh, rl[h], start=False, stop=False)
    for o, h in zip(out, range(len(out))):
        last = nc_mm(o, ll, rh[h], start=False, stop=stop)
    return last


def project_and_recur(nc, io, persist):
    mixT, qkvT, ident = persist["mixT"], persist["qkvT"], persist["ident"]
    with ExitStack() as ctx:
        sb = lambda name, shape, dt=F32: ctx.enter_context(nc.sbuf_tensor(name, shape, dt))
        sem = lambda name: ctx.enter_context(nc.semaphore(name))
        hT_hi = sb("hT_hi", [P, KT, SEQ], F32R)
        hT_lo = sb("hT_lo", [P, KT, SEQ], F32R)
        w_raw = sb("w_raw", [P, 2, KT, 2 * P])
        w_hi = sb("w_hi", [P, 2, KT, P], F32R)
        w_lo = sb("w_lo", [P, 2, KT, P], F32R)
        tmp = [sb(f"tmp{n}", [P, SEQ]) for n in range(5)]
        gate_w = sb("gate_w", [P, CT, 2, P])
        gate_cur = sb("gate_cur", [P, 2, P])
        rows = sb("rows", [32, P])
        chan = sb("chan", [P, 32])
        soft = sb("soft", [P, 8, CT])
        stat = sb("stat", [P, 3, TT])
        eps = sb("eps", [P, 1])
        ps = [ctx.enter_context(nc.psum_tensor(f"ps_proj{n}", [P, 2, HALF], F32)) for n in range(2)]
        ps_t = [ctx.enter_context(nc.psum_tensor(f"ps_turn{n}", [P, 2, HALF], F32)) for n in range(2)]
        x_sb, xn_sb, norm_w = tmp[0:2], tmp[2:4], tmp[4]
        conv_x, r_sb, i_sb, a_sb, t_sb = tmp

        rows_in = sem("rows_in")
        norm_w_in = sem("norm_w_in")
        gates_in = sem("gates_in")
        x_in = [sem(f"x_in{n}") for n in range(2)]
        w_in = [sem(f"w_in{n}") for n in range(2)]
        consts = sem("consts")
        ident0 = sem("ident0")
        chan_t = sem("chan_t")
        chan_ready = sem("chan_ready")
        exp_ready = sem("exp_ready")
        soft_ready = sem("soft_ready")
        x_free = sem("x_free")
        root_ready = sem("root_ready")
        xn_ready = sem("xn_ready")
        turned = sem("turned")
        hi_out = sem("hi_out")
        lo_out = sem("lo_out")
        w_free = sem("w_free")
        w_hi_ready = sem("w_hi_ready")
        w_lo_ready = sem("w_lo_ready")
        proj_done = sem("proj_done")
        proj_out = sem("proj_out")
        cur_ready = sem("cur_ready")
        conv_ready = sem("conv_ready")
        gates_done = sem("gates_done")
        gates_read = sem("gates_read")
        tanh_ready = sem("tanh_ready")
        ratio_ready = sem("ratio_ready")
        sqrt_ready = sem("sqrt_ready")
        gelu_ready = sem("gelu_ready")
        lru_done = sem("lru_done")
        act_own = sem("act_own")
        dve_own = sem("dve_own")
        block = ctx.enter_context(nc.Block("project"))

        w_cols = io["w_in"][0].rearrange("(k p) n -> p k n", p=P)

        @block.sync
        def _(sp):
            for src, at, n in ((io["conv_w"], 0, 16), (io["conv_b"], 16, 4), (io["b_rgate"], 20, 4),
                               (io["b_igate"], 24, 4), (io["lru_lambda"], 28, 4)):
                flat = src.rearrange("l w (t p) -> (l w t) p", p=P) if n == 16 else \
                    src.rearrange("l (t p) -> (l t) p", p=P)
                sp.dma_start(rows[at:at + n, :], flat).then_inc(rows_in, 16)
            sp.dma_start(norm_w[:, :], io["mix_norm_w"][0].partition_broadcast(P)).then_inc(norm_w_in, 16)
            with sp.Fori(0, TT // 2) as i:
                for c in range(2):
                    sp.wait_ge(x_free, i * 2 + (c + 1))
                    sp.dma_start(x_sb[c][:, :], io["x"][0][bass.ds(i * (2 * P) + c * P, P), :]).then_inc(x_in[c], 16)

            def load(col, n, c):
                sp.wait_ge(w_free, n)
                sp.dma_start(w_raw[:, c], w_cols[:, :, bass.ds(col, 2 * P)]).then_inc(w_in[c], 16)

            with sp.Fori(0, 2) as i:
                for c in range(2):
                    load((i * -HALF) + (4 * HALF + c * 2 * P), i * 2 + (c + 1), c)
            with sp.Fori(0, 2) as i:
                for c in range(2):
                    load(i * HALF + c * 2 * P, i * 2 + (c + 5), c)
            for c in range(2):
                load(2 * HALF + c * 2 * P, c + 9, c)

        @block.gpsimd
        def _(pool):
            pool.memset(ident[:, :], 0.0).then_inc(ident0, 1)
            pool.memset(eps[:, :], NORM_EPS).then_inc(ident0, 1)
            pool.memset(gate_w[:, :, :, :], 0.0).then_inc(ident0, 1)
            pool.wait_ge(ident0, 3)
            pool.affine_select(out=ident[:, :], in_=ident[:, :], compare_op=ALU.not_equal, fill=1.0, base=0,
                               pattern=[[-1, P]], channel_multiplier=1).then_inc(consts, 1)
            for g, src in enumerate((io["w_rgate"], io["w_igate"])):
                for b in range(2):
                    half = slice(64 * b, 64 * b + 64)
                    pool.dma_start(gate_w[half, :, g, half],
                                   src[0].rearrange("(t b) i j -> b i t j", b=2)[b]).then_inc(gates_in, 16)
            pool.wait_ge(gates_in, 64)
            with pool.Fori(0, CT) as t:
                pool.wait_ge(gates_done, t + 1)
                pool.tensor_copy(gate_cur[:, :, :], gate_w[:, bass.ds(t, 1)].rearrange("p o g j -> p (o g) j")).then_inc(cur_ready, 1)

        @block.scalar
        def _(act):
            link = Link(act, act_own)
            act.wait_ge(chan_ready, 2)
            act.activation(soft[:, 2, :], soft[:, 1, :], ACT.Exp, scale=-1.0).then_inc(exp_ready, 1)
            act.wait_ge(consts, 1)

            def square(i, c):
                act.wait_ge(x_in[c], i * 16 + 16)
                act.wait_ge(turned, i * 2 + (c + 1))
                link(act.activation(xn_sb[c][:, :], x_sb[c][:, :], ACT.Square,
                                    accum_out=stat[:, 0, bass.ds(i * 2 + c, 1)]))
                act.activation(stat[:, 1, bass.ds(i * 2 + c, 1)], stat[:, 0, bass.ds(i * 2 + c, 1)], ACT.Sqrt,
                               bias=eps[:, 0:1], scale=1.0 / D).then_inc(root_ready, 1)

            def high(i, c):
                act.wait_ge(turned, i * 2 + (c + 3))
                act.activation(hT_hi[:, :, bass.ds(i * 2 * P + c * P, P)],
                               ps_t[c][:, :, :].rearrange("p a (k n) -> p (a k) n", n=P), ACT.Copy).then_inc(hi_out, 1)

            with act.Fori(0, TT // 2) as i:
                link.loop(i, 2)
                square(i, 0)
                square(i, 1)
                high(i, 0)
                high(i, 1)
            link.end(TT // 2)

            def split_high(n, c):
                if c % 2 == 0:
                    act.wait_ge(w_in[c // 2], n[1])
                act.wait_ge(proj_done, n[0] + 1)
                act.activation(w_hi[:, c % 2], w_raw[:, c // 2, :, (c % 2) * P:(c % 2 + 1) * P],
                               ACT.Copy).then_inc(w_hi_ready, 1)

            def evacuate(n, dst, c):
                act.wait_ge(proj_done, n + 3)
                act.activation(dst, ps[c % 2][:, :, :].rearrange("p a n -> p (a n)"), ACT.Copy).then_inc(proj_out, 1)

            def gates(i, c):
                t = i * 2 + c // 2
                act.wait_ge(gates_done, t + 2)
                act.wait_ge(lru_done, t + 1)
                link(act.activation(r_sb[:, :], ps_t[0][:, :, :].rearrange("p a n -> p (a n)"), ACT.Sigmoid,
                                    bias=chan[:, bass.ds(t + 20, 1)]))
                act.activation(i_sb[:, :], ps_t[1][:, :, :].rearrange("p a n -> p (a n)"), ACT.Sigmoid,
                               bias=chan[:, bass.ds(t + 24, 1)]).then_inc(gates_read, 1)
                act.activation(t_sb[:, :], r_sb[:, :], ACT.Tanh, scale=soft[:, 6, bass.ds(t, 1)]).then_inc(tanh_ready, 1)
                act.activation(a_sb[:, :], r_sb[:, :], ACT.Exp, scale=soft[:, 7, bass.ds(t, 1)]).then_inc(tanh_ready, 1)
                act.wait_ge(ratio_ready, t + 1)
                act.activation(t_sb[:, :], t_sb[:, :], ACT.Sqrt).then_inc(sqrt_ready, 1)
                act.activation(mixT[:, bass.ds(t, 1)], mixT[:, bass.ds(t, 1)], ACT.Gelu_apprx_tanh).then_inc(gelu_ready, 1)

            split_high((0, 16), 0)
            for group in range(2):
                with act.Fori(0, 2) as i:
                    if group:
                        link.loop(i, 2)
                    for c in range(4):
                        base = 8 * group + c
                        nxt = (c + 1) % 4
                        nth = 2 * group + 1 + (c == 3)
                        split_high((i * 4 + (base + 1), i * 16 + 16 * nth), nxt)
                        if group and c == 0:
                            act.wait_ge(soft_ready, 1)
                            act.wait_ge(proj_out, 10)
                        if group and c % 2 == 1:
                            gates(i, c)
                        dst = (qkvT if group else mixT)[:, bass.ds(i * 4 + c, 1)]
                        evacuate(i * 4 + base, dst.rearrange("p o n -> p (o n)"), c)
                if group:
                    link.end(2)
            for c in range(4):
                if c < 3:
                    split_high((17 + c, 16 * 5), c + 1)
                evacuate(16 + c, qkvT[:, 8 + c], c)

        @block.vector
        def _(dve):
            link = Link(dve, dve_own)
            dve.sem_inc(x_free, 2)
            dve.sem_inc(w_free, 2)
            dve.sem_inc(lru_done, 1)
            dve.wait_ge(chan_t, 1)
            dve.tensor_copy(chan[:, :], ps[0][:, 0, 0:32]).then_inc(chan_ready, 1)
            dve.wait_ge(chan_ready, 1)
            lam = chan[:, 28:32]
            link(dve.tensor_scalar(soft[:, 0, :], lam, -1.0, 0.0, ALU.mult, ALU.max))
            dve.scalar_tensor_tensor(out=soft[:, 1, :], in0=lam, scalar=-1.0, in1=lam, op0=ALU.mult,
                                     op1=ALU.max).then_inc(chan_ready, 1)
            dve.wait_ge(exp_ready, 1)
            link(dve.tensor_scalar(soft[:, 3, :], soft[:, 2, :], 2.0, None, ALU.add))
            link(dve.reciprocal(soft[:, 3, :], soft[:, 3, :]))
            link(dve.tensor_tensor(soft[:, 3, :], soft[:, 3, :], soft[:, 2, :], ALU.mult))
            link(dve.tensor_tensor(soft[:, 4, :], soft[:, 3, :], soft[:, 3, :], ALU.mult))
            link(dve.tensor_scalar(soft[:, 5, :], soft[:, 4, :], 1.0 / 19.0, None, ALU.mult))
            for odd in range(17, 2, -2):
                link(dve.scalar_tensor_tensor(out=soft[:, 5, :], in0=soft[:, 5, :], scalar=1.0 / odd,
                                              in1=soft[:, 4, :], op0=ALU.add, op1=ALU.mult))
            link(dve.scalar_tensor_tensor(out=soft[:, 5, :], in0=soft[:, 5, :], scalar=1.0, in1=soft[:, 3, :],
                                          op0=ALU.add, op1=ALU.mult))
            link(dve.scalar_tensor_tensor(out=soft[:, 5, :], in0=soft[:, 5, :], scalar=2.0, in1=soft[:, 0, :],
                                          op0=ALU.mult, op1=ALU.add))
            link(dve.tensor_scalar(soft[:, 6, :], soft[:, 5, :], 8.0, None, ALU.mult))
            dve.tensor_scalar(soft[:, 7, :], soft[:, 5, :], -8.0, None, ALU.mult).then_inc(soft_ready, 1)

            def scale(i, c):
                dve.wait_ge(root_ready, i * 2 + (c + 1))
                link(dve.reciprocal(stat[:, 2, bass.ds(i * 2 + c, 1)], stat[:, 1, bass.ds(i * 2 + c, 1)]))
                link(dve.scalar_tensor_tensor(out=xn_sb[c][:, :], in0=x_sb[c][:, :],
                                              scalar=stat[:, 2, bass.ds(i * 2 + c, 1)],
                                              in1=norm_w[:, :], op0=ALU.mult, op1=ALU.mult))
                dve.sem_inc(x_free, 1)
                dve.sem_inc(xn_ready, 1)

            def low(i, c):
                dve.wait_ge(hi_out, i * 2 + (c + 1))
                at = bass.ds(i * 2 * P + c * P, P)
                dve.tensor_tensor(hT_lo[:, :, at], ps_t[c][:, :, :].rearrange("p a (k n) -> p (a k) n", n=P),
                                  hT_hi[:, :, at].bitcast(F32), ALU.subtract).then_inc(lo_out, 1)

            dve.wait_ge(norm_w_in, 16)
            with dve.Fori(0, TT // 2) as i:
                link.loop(i, 4)
                scale(i, 0)
                scale(i, 1)
                low(i, 0)
                low(i, 1)
            link.end(TT // 2)

            def split_low(n, c):
                dve.wait_ge(w_hi_ready, n)
                ins = dve.tensor_tensor(w_lo[:, c % 2], w_raw[:, c // 2, :, (c % 2) * P:(c % 2 + 1) * P],
                                        w_hi[:, c % 2].bitcast(F32), ALU.subtract)
                ins.then_inc(w_lo_ready, 1)
                if c % 2 == 1:
                    dve.wait_ge(w_lo_ready, n)
                    dve.sem_inc(w_free, 1)

            def convolve(t):
                x_t = mixT[:, bass.ds(t + 4, 1)].rearrange("p o n -> p (o n)")
                link(dve.tensor_scalar(conv_x[:, :], x_t, chan[:, bass.ds(t + 12, 1)], chan[:, bass.ds(t + 16, 1)],
                                       ALU.mult, ALU.add))
                for back in (1, 2, 3):
                    link(dve.scalar_tensor_tensor(
                        out=conv_x[:, back:], in0=mixT[:, bass.ds(t + 4, 1), 0:SEQ - back].rearrange("p o n -> p (o n)"),
                        scalar=chan[:, bass.ds(t + 4 * (3 - back), 1)],
                        in1=conv_x[:, back:], op0=ALU.mult, op1=ALU.add))
                dve.sem_inc(conv_ready, 1)

            def recur(t):
                dve.wait_ge(tanh_ready, t * 2 + 2)
                link(dve.tensor_tensor(r_sb[:, :], a_sb[:, :], a_sb[:, :], ALU.mult))
                dve.scalar_tensor_tensor(out=t_sb[:, :], in0=r_sb[:, :], scalar=1.0, in1=t_sb[:, :],
                                         op0=ALU.add, op1=ALU.mult).then_inc(ratio_ready, 1)
                link(dve.tensor_tensor(i_sb[:, :], i_sb[:, :], conv_x[:, :], ALU.mult))
                dve.wait_ge(sqrt_ready, t + 1)
                link(dve.tensor_tensor(i_sb[:, :], i_sb[:, :], t_sb[:, :], ALU.mult))
                link(dve.tensor_tensor_scan(r_sb[:, :], a_sb[:, :], i_sb[:, :], 0.0, ALU.mult, ALU.add))
                dve.wait_ge(gelu_ready, t + 1)
                gate = mixT[:, bass.ds(t, 1)].rearrange("p o n -> p (o n)")
                dve.tensor_tensor(gate, gate, r_sb[:, :], ALU.mult).then_inc(lru_done, 1)

            split_low(1, 0)
            with dve.Fori(0, 2) as i:
                for c in range(4):
                    split_low(i * 4 + (c + 2), (c + 1) % 4)
            with dve.Fori(0, 2) as i:
                link.loop(i, 2 * 8)
                for c in range(4):
                    split_low(i * 4 + (c + 10), (c + 1) % 4)
                    if c == 0:
                        dve.wait_ge(proj_out, 10)
                    if c % 2 == 0:
                        convolve(i * 2 + c // 2)
                    else:
                        recur(i * 2 + c // 2)
            link.end(2)
            for c in range(1, 4):
                split_low(17 + c, c)

        @block.tensor
        def _(pe):
            for free, n in ((turned, 2), (lo_out, 2), (proj_done, 2), (proj_out, 2), (gates_done, 1), (gates_read, 1)):
                pe.sem_inc(free, n)
            pe.wait_ge(rows_in, 80)
            pe.wait_ge(consts, 1)
            pe.transpose(ps[0][:, 0, 0:32], rows[:, :], ident[0:32, 0:32]).then_inc(chan_t, 1)

            def turn(i, c):
                pe.wait_ge(xn_ready, i * 2 + (c + 1))
                pe.wait_ge(lo_out, i * 2 + (c + 1))
                for k in range(KT):
                    last = pe.transpose(ps_t[c][:, k // 4, (k % 4) * P:(k % 4 + 1) * P],
                                        xn_sb[c][:, k * P:(k + 1) * P], ident[:, :])
                last.then_inc(turned, 1)

            with pe.Fori(0, TT // 2) as i:
                turn(i, 0)
                turn(i, 1)
            pe.wait_ge(lo_out, TT + 2)

            def tile(n, c):
                pe.wait_ge(w_lo_ready, n)
                pe.wait_ge(proj_out, n)
                for k in range(KT):
                    last = split_products(pe, [ps[c % 2][:, h, :] for h in range(2)],
                                          w_hi[:, c % 2, k, :], w_lo[:, c % 2, k, :],
                                          [hT_hi[:, k, h * HALF:(h + 1) * HALF] for h in range(2)],
                                          [hT_lo[:, k, h * HALF:(h + 1) * HALF] for h in range(2)],
                                          k == 0, k == KT - 1)
                last.then_inc(proj_done, 1)

            def gates(t):
                pe.wait_ge(conv_ready, t + 1)
                pe.wait_ge(cur_ready, t + 1)
                pe.wait_ge(gates_read, t + 1)
                for g in range(2):
                    for h in range(2):
                        last = pe.matmul(ps_t[g][:, h, :], gate_cur[:, g, :], conv_x[:, h * HALF:(h + 1) * HALF],
                                         start=True, stop=True)
                last.then_inc(gates_done, 1)

            with pe.Fori(0, 2) as i:
                for c in range(4):
                    tile(i * 4 + (c + 1), c)
            with pe.Fori(0, 2) as i:
                for c in range(4):
                    tile(i * 4 + (c + 9), c)
                    if c % 2 == 0:
                        gates(i * 2 + c // 2)
            for c in range(4):
                tile(17 + c, c)


def attend(nc, io, persist):
    mixT, qkvT, ident, head_ss = (persist[n] for n in ("mixT", "qkvT", "ident", "head_ss"))
    with ExitStack() as ctx:
        sb = lambda name, shape, dt=F32: ctx.enter_context(nc.sbuf_tensor(name, shape, dt))
        sem = lambda name: ctx.enter_context(nc.semaphore(name))
        q_parts = sb("q_parts", [P, 2, SEQ], F32R)
        k_parts = sb("k_parts", [P, 2, SEQ], F32R)
        qq = sb("qq", [P, 2, SEQ], F32R)
        kk = sb("kk", [P, 2, 2, SEQ], F32R)
        vT = sb("vT", [P, SEQ])
        v_nat = sb("v_nat", [P, HEADS, TT, DH])
        bias8 = sb("bias8", [P, SEQ])
        prob = sb("prob", [P, 4, 2, SEQ])
        attT = sb("attT", [P, 2, SEQ])
        junk = sb("junk", [P, 2, DH])
        lam_in = sb("lam_in", [P, 4, QK])
        lam = sb("lam", [P, 8])
        row_max = sb("row_max", [P, TT, 2])
        neg_max = sb("neg_max", [P, TT, 2])
        row_sum = sb("row_sum", [P, TT, 2])
        inv_sum = sb("inv_sum", [P, TT, 2])
        coef = sb("coef", [P, TT])
        ps_s = [ctx.enter_context(nc.psum_tensor(f"ps_s{c}", [P, SEQ], F32)) for c in range(2)]
        ps_t = ctx.enter_context(nc.psum_tensor("ps_t", [P, SEQ], F32))
        ps_o = [ctx.enter_context(nc.psum_tensor(f"ps_o{n}", [P, HALF], F32)) for n in range(2)]

        lam_loaded = sem("lam_loaded")
        lam_sums = sem("lam_sums")
        lam_exp = sem("lam_exp")
        pool_own = sem("pool_own")
        bias_ready = sem("bias_ready")
        v_ready = sem("v_ready")
        qk_high = sem("qk_high")
        qk_split = sem("qk_split")
        qk_in = [sem(f"qk_in{n}") for n in range(3)]
        scores_done = sem("scores_done")
        scores_read = sem("scores_read")
        max_ready = sem("max_ready")
        exp_done = sem("exp_done")
        att_ready = sem("att_ready")
        turned = sem("turned")
        turned_out = sem("turned_out")
        pv_done = sem("pv_done")
        out_scaled = sem("out_scaled")
        out_squared = sem("out_squared")
        dve_own = sem("dve_own2")
        dve_seen = sem("dve_seen")
        block = ctx.enter_context(nc.Block("attend"))

        loads = [(0, TT // 2, slice(HALF, SEQ), True, True), (1, TT - 1, slice(P, HALF), False, True),
                 (1, TT, slice(0, P), False, True), (2, TT, slice(0, HALF), True, False)]
        dmas = [8, 8, 4]
        width = [(TT - s) * P for s in range(TT)]
        tile_of = [TT - 1 - s for s in range(TT)]

        def pipeline(eng, emit, link=None, per=0):
            for s in range(TT):
                emit(0, s)
            with eng.Fori(1, HEADS - 1) as h:
                if link:
                    link.loop(h - 1, per)
                for s in range(TT):
                    emit(h, s)
            if link:
                link.end(HEADS - 2)
            for s in range(TT):
                emit(HEADS - 1, s)
            for s in range(4):
                emit(HEADS, s)

        def behind(h, s, k):
            head, e = (h, s - k) if s >= k else (h - 1, s - k + TT)
            return None if isinstance(h, int) and not 0 <= head < HEADS else (h * TT + (s - k), head, e)

        def last(h):
            return isinstance(h, int) and h >= HEADS - 1

        def turn_number(h, s):
            return h * (TT + 1) + (s - 1 if s == 0 or isinstance(h, int) and h == HEADS else s)

        def v_number(h):
            return 1 if isinstance(h, int) and h == 0 else h * (TT + 1)

        def tile(tensor, n):
            return tensor[:, span(n, 1)].rearrange("p o n -> p (o n)")

        @block.sync
        def _(sp):
            for n, name in enumerate(("lambda_q1", "lambda_k1", "lambda_q2", "lambda_k2")):
                sp.dma_start(lam_in[:, n, :], io[name][0].partition_broadcast(P)).then_inc(lam_loaded, 16)

            def arrange(n, cols, want_q, want_k):
                for c in range(2):
                    src = slice(QK * c, QK * c + QK)
                    for row in range(2):
                        dst = slice(QK * row, QK * row + QK)
                        if want_k:
                            sp.dma_start(kk[dst, :, c, cols].bitcast(F32), k_parts[src, :, cols].bitcast(F32)
                                         ).then_inc(qk_in[n], 16)
                        if want_q:
                            sp.dma_start(qq[dst, c, cols].bitcast(F32), q_parts[src, row, cols].bitcast(F32)
                                         ).then_inc(qk_in[n], 16)

            sp.wait_ge(qk_split, 2)
            arrange(0, slice(0, SEQ), True, True)
            with sp.Fori(1, HEADS) as h:
                sp.wait_ge(qk_split, h * 2 + 2)
                for n, used, cols, want_q, want_k in loads:
                    sp.wait_ge(scores_done, h * TT + (used - TT))
                    arrange(n, cols, want_q, want_k)

        @block.gpsimd
        def _(pool):
            pool.iota(bias8[:, :], [[8, SEQ]], base=-8 * (SEQ - P), channel_multiplier=-8,
                      allow_small_or_imprecise_dtypes=True).then_inc(pool_own, 1)
            pool.wait_ge(pool_own, 1)
            pool.affine_select(out=bias8[:, :], in_=bias8[:, :], compare_op=ALU.is_ge, fill=-BIG,
                               base=SEQ - P, pattern=[[-1, SEQ]], channel_multiplier=1).then_inc(pool_own, 1)
            pool.wait_ge(pool_own, 2)
            with pool.Fori(0, HEADS) as h:
                pool.wait_ge(scores_read, h * TT + 1)
                pool.sem_inc(pool_own, 1)
                pool.tensor_scalar(bias8[:, :], bias8[:, :], 2.0 ** (-8.0 / HEADS), 1.0,
                                   ALU.mult, ALU.mult).then_inc(bias_ready, 1)
                pool.tensor_copy(vT[:, :], tile(qkvT, h + 8)).then_inc(v_ready, 1)

        @block.scalar
        def _(act):
            act.wait_ge(lam_sums, 2)
            act.activation(lam[:, 2:4], lam[:, 0:2], ACT.Exp).then_inc(lam_exp, 1)

            def split(h):
                if not isinstance(h, int) or h:
                    act.wait_ge(qk_in[2], h * (16 * dmas[2]))
                act.activation(q_parts[:, 0], tile(qkvT, h), ACT.Copy).then_inc(qk_high, 1)
                act.activation(k_parts[:, 0], tile(qkvT, h + 4), ACT.Copy).then_inc(qk_high, 1)

            def emit(h, s):
                if s == 1 and not (isinstance(h, int) and h == HEADS):
                    act.wait_ge(turned, v_number(h))
                    act.activation(v_nat[:, span(h, 1)].rearrange("p o k n -> p (o k) n"),
                                   ps_t[:, :].rearrange("p (k n) -> p k n", n=P), ACT.Copy).then_inc(turned_out, 1)
                if at := behind(h, s, 2):
                    n, head, e = at
                    act.wait_ge(turned, turn_number(h, s))
                    act.wait_ge(pv_done, n + 1)
                    act.activation(attT[:, e % 2, 0:width[e]], ps_t[:, 0:width[e]], ACT.Copy).then_inc(turned_out, 1)
                if at := behind(h, s, 0):
                    n, head, e = at
                    act.wait_ge(max_ready, n + 1)
                    for c in range(2):
                        ins = act.activation(prob[:, e % 4, c, 0:width[e]], prob[:, e % 4, c, 0:width[e]], ACT.Exp,
                                             bias=neg_max[:, e, c:c + 1], scale=QK ** -0.5,
                                             accum_out=row_sum[:, e, c:c + 1])
                    ins.then_inc(exp_done, 1)
                if s == 2 and not last(h):
                    split(h + 1)
                if at := behind(h, s, 4):
                    n, head, e = at
                    act.wait_ge(out_scaled, n + 1)
                    act.activation(junk[:, e % 2], ps_o[e % 2][:, 0:DH], ACT.Square, scale=inv_sum[:, e, 0:1],
                                   accum_out=head_ss[:, span(head * TT + tile_of[e], 1)]).then_inc(out_squared, 1)

            split(0)
            pipeline(act, emit)

        @block.vector
        def _(dve):
            link = Link(dve, dve_own)
            dve.sem_inc(scores_read, 1)
            dve.wait_ge(lam_loaded, 64)
            for n in range(2):
                dve.tensor_tensor_reduce(lam_in[:, 2 * n, :], lam_in[:, 2 * n, :], lam_in[:, 2 * n + 1, :], 1.0, 0.0,
                                         ALU.mult, ALU.add, lam[:, n:n + 1]).then_inc(lam_sums, 1)
            dve.wait_ge(lam_exp, 1)
            link(dve.tensor_tensor(lam[:, 4:5], lam[:, 3:4], lam[:, 2:3], ALU.subtract))
            link(dve.tensor_scalar(lam[:, 5:6], lam[:, 4:5], -LAM_INIT, None, ALU.add))

            def split(h):
                dve.wait_ge(qk_high, h * 2 + 2)
                dve.tensor_tensor(q_parts[:, 1], tile(qkvT, h), q_parts[:, 0].bitcast(F32), ALU.subtract).then_inc(qk_split, 1)
                dve.tensor_tensor(k_parts[:, 1], tile(qkvT, h + 4), k_parts[:, 0].bitcast(F32), ALU.subtract).then_inc(qk_split, 1)

            def emit(h, s):
                if at := behind(h, s, 0):
                    n, head, e = at
                    if s == 0:
                        dve.wait_ge(bias_ready, h + 1)
                    dve.wait_ge(scores_done, n + 1)
                    dve.sem_inc(dve_seen, 1)
                    b = bias8[:, SEQ - width[e]:SEQ]
                    dve.tensor_tensor_reduce(prob[:, e % 4, 0, 0:width[e]], ps_s[0][:, 0:width[e]], b, 1.0, -3e38,
                                             ALU.add, ALU.max, row_max[:, e, 0:1])
                    link(dve.tensor_tensor_reduce(prob[:, e % 4, 1, 0:width[e]], ps_s[1][:, 0:width[e]], b, 1.0,
                                                  -3e38, ALU.add, ALU.max, row_max[:, e, 1:2]))
                    dve.sem_inc(scores_read, 1)
                    dve.tensor_scalar(neg_max[:, e, :], row_max[:, e, :], -(QK ** -0.5), None,
                                      ALU.mult).then_inc(max_ready, 1)
                if at := behind(h, s, 1):
                    n, head, e = at
                    dve.wait_ge(exp_done, n + 1)
                    link(dve.reciprocal(inv_sum[:, e, :], row_sum[:, e, :]))
                    link(dve.scalar_tensor_tensor(out=coef[:, e:e + 1], in0=row_sum[:, e, 0:1], scalar=lam[:, 5:6],
                                                  in1=inv_sum[:, e, 1:2], op0=ALU.mult, op1=ALU.mult))
                    dve.scalar_tensor_tensor(out=prob[:, e % 4, 0, 0:width[e]], in0=prob[:, e % 4, 1, 0:width[e]],
                                             scalar=coef[:, e:e + 1], in1=prob[:, e % 4, 0, 0:width[e]],
                                             op0=ALU.mult, op1=ALU.add).then_inc(att_ready, 1)
                if s == 2 and not last(h):
                    split(h + 1)
                if at := behind(h, s, 4):
                    n, head, e = at
                    dve.wait_ge(pv_done, n + 3)
                    o = mixT[:, span(head + 4, 1), tile_of[e] * P:tile_of[e] * P + P]
                    dve.tensor_scalar(o.rearrange("p o n -> p (o n)"), ps_o[e % 2][:, 0:DH], inv_sum[:, e, 0:1], None,
                                      ALU.mult).then_inc(out_scaled, 1)

            split(0)
            pipeline(dve, emit, link, per=3 * TT)

        @block.tensor
        def _(pe):
            for free, n in ((turned_out, 1), (pv_done, 2), (out_squared, 2)):
                pe.sem_inc(free, n)
            for n in range(1, 3):
                pe.sem_inc(qk_in[n], 16 * dmas[n])

            def scores(h, s):
                if s == 0:
                    for n in range(2):
                        pe.wait_ge(qk_in[n], h * (16 * dmas[n]) + 16 * dmas[n])
                if s == TT // 2:
                    pe.wait_ge(qk_in[2], h * (16 * dmas[2]) + 16 * dmas[2])
                pe.wait_ge(scores_read, h * TT + (s + 1))
                qt = slice(tile_of[s] * P, tile_of[s] * P + P)
                for c in range(2):
                    for part in range(2):
                        for lo in range(0, width[s], HALF):
                            cols = slice(lo, min(lo + HALF, width[s]))
                            mm = pe.matmul(ps_s[c][:, cols], qq[:, c, qt], kk[:, part, c, cols], start=part == 0,
                                           stop=part == 1)
                mm.then_inc(scores_done, 1)

            def emit(h, s):
                if behind(h, s, 0):
                    scores(h, s)
                if s == 1 and not (isinstance(h, int) and h == HEADS):
                    pe.wait_ge(turned_out, v_number(h))
                    pe.wait_ge(v_ready, h + 1)
                    for k in range(TT):
                        mm = pe.transpose(ps_t[:, k * P:(k + 1) * P], vT[:, k * P:(k + 1) * P], ident[:, :])
                    mm.then_inc(turned, 1)
                if at := behind(h, s, 2):
                    n, head, e = at
                    pe.wait_ge(att_ready, n + 1)
                    pe.wait_ge(turned_out, turn_number(h, s))
                    for k in range(TT - e):
                        mm = pe.transpose(ps_t[:, k * P:(k + 1) * P], prob[:, e % 4, 0, k * P:(k + 1) * P], ident[:, :])
                    mm.then_inc(turned, 1)
                if at := behind(h, s, 3):
                    n, head, e = at
                    pe.wait_ge(turned_out, (turn_number(h, s - 1) if s else turn_number(h - 1, TT - 1)) + 1)
                    pe.wait_ge(out_squared, n + 1)
                    for k in range(TT - e):
                        mm = pe.matmul(ps_o[e % 2][:, 0:DH], attT[:, e % 2, k * P:(k + 1) * P],
                                       v_nat[:, span(head, 1), k, :].rearrange("p o n -> p (o n)"),
                                       start=k == 0, stop=k == TT - e - 1)
                    mm.then_inc(pv_done, 1)

            pipeline(pe, emit)


def stage(a, b, k):
    n, half, par = a * 2 + (b - k), a + (b - k) // 2, (b - k) % 2
    return None if isinstance(a, int) and not 0 <= n < TT else (n, half, par)


def tile_steps(eng, emit, link=None, per=0):
    for b in (-1, 0, 1):
        emit(0, b)
    with eng.Fori(0, 2) as i:
        if link:
            link.loop(i, per)
        emit(i, 2)
        emit(i, 3)
    if link:
        link.end(2)
    for b in (6, 7, 8, 9):
        emit(0, b)


def need(eng, sem, value):
    if not isinstance(value, int) or value > 0:
        eng.wait_ge(sem, value)


def mix_out(nc, io, persist):
    mixT, ident, head_ss, logits = (persist[n] for n in ("mixT", "ident", "head_ss", "logits"))
    with ExitStack() as ctx:
        sb = lambda name, shape, dt=F32: ctx.enter_context(nc.sbuf_tensor(name, shape, dt))
        sem = lambda name: ctx.enter_context(nc.semaphore(name))
        wout_raw = sb("wout_raw", [P, KT, D])
        wout_hi = sb("wout_hi", [P, KT, D], F32R)
        wout_lo = sb("wout_lo", [P, KT, D], F32R)
        c_hi = sb("c_hi", [P, 2, KT, P], F32R)
        c_lo = sb("c_lo", [P, 2, KT, P], F32R)
        heads_n = sb("heads_n", [P, 2, HEADS * DH])
        x_sb = sb("x_sb", [P, 2, D])
        x2_sb = sb("x2_sb", [P, 2, D])
        hn_sb = sb("hn_sb", [P, 2, D])
        hnT = sb("hnT", [P, 2, KT, P])
        norm_w = sb("ffn_w", [P, D])
        head_w = sb("head_w", [P, DH])
        head_r = sb("head_r", [P, HEADS * TT])
        w_rt = sb("w_rt", [P, KT, NG + NE])
        b_rt = sb("b_rt", [P, NG + NE])
        stat = sb("stat3", [P, 3, TT])
        eps = sb("eps3", [P, 2])
        ps_c = [ctx.enter_context(nc.psum_tensor(f"ps_c{n}", [P, HALF], F32)) for n in range(2)]
        ps_y = [ctx.enter_context(nc.psum_tensor(f"ps_y{n}", [P, D], F32)) for n in range(2)]
        ps_h = ctx.enter_context(nc.psum_tensor("ps_h", [P, D], F32))

        small_in = sem("small_in")
        wout_in = [sem(f"wout_in{n}") for n in range(3)]
        x_in = [sem(f"x3_in{n}") for n in range(2)]
        x2_out = [sem(f"x2_out{n}") for n in range(2)]
        hn_out = [sem(f"hn_out{n}") for n in range(2)]
        eps_set = sem("eps_set")
        head_root = sem("head_root")
        wout_high = sem("wout_high")
        wout_split = sem("wout_split")
        heads_ready = sem("heads_ready")
        c_turned = sem("c_turned")
        c_high = sem("c_high")
        c_split = sem("c_split")
        y_done = sem("y_done")
        x2_ready = sem("x2_ready")
        root_ready = sem("root3_ready")
        hn_ready = sem("hn_ready")
        hn_turned = sem("hn_turned")
        hnT_ready = sem("hnT_ready")
        routed = sem("routed")
        logits_ready = sem("logits_ready")
        act_own = sem("act_own3")
        dve_own = sem("dve_own3")
        block = ctx.enter_context(nc.Block("mix"))
        k_order = [4, 5, 6, 7, 0, 1, 2, 3]
        wout_loads = [(4, 5), (5, 8), (0, 4)]

        @block.sync
        def _(sp):
            sp.dma_start(head_w[:, :], io["head_norm_w"][0].partition_broadcast(P)).then_inc(small_in, 16)
            sp.dma_start(norm_w[:, :], io["ffn_norm_w"][0].partition_broadcast(P)).then_inc(small_in, 16)
            sp.dma_start(w_rt[:, :, 0:NG], io["w_router_group"][0].rearrange("(k p) n -> p k n", p=P)).then_inc(small_in, 16)
            sp.dma_start(w_rt[:, :, NG:], io["w_router_expert"][0].rearrange("(k p) n -> p k n", p=P)).then_inc(small_in, 16)
            sp.dma_start(b_rt[:, 0:NG], io["b_router_group"][0].partition_broadcast(P)).then_inc(small_in, 16)
            sp.dma_start(b_rt[:, NG:], io["b_router_expert"][0].partition_broadcast(P)).then_inc(small_in, 16)

            for n, (lo, hi) in enumerate(wout_loads):
                sp.dma_start(wout_raw[:, lo:hi], io["w_out"][0][lo * P:hi * P, :].rearrange("(k p) n -> p k n", p=P)
                             ).then_inc(wout_in[n], 16)

            def emit(a, b):
                if at := stage(a, b, -1):
                    n, half, par = at
                    need(sp, x2_ready, n - 1)
                    sp.dma_start(x_sb[:, par], io["x"][0][span(n * P, P), :]).then_inc(x_in[par], 16)
                if at := stage(a, b, 1):
                    n, half, par = at
                    sp.wait_ge(x2_ready, n + 1)
                    sp.dma_start(persist["x2_d"][span(n * P, P), :], x2_sb[:, par]).then_inc(x2_out[par], 16)
                    sp.wait_ge(hn_ready, n + 1)
                    for copy in range(2):
                        sp.dma_start(persist["hn_d"][copy][span(n * P, P), :], hn_sb[:, par]).then_inc(hn_out[par], 16)

            tile_steps(sp, emit)
            for par in range(2):
                sp.wait_ge(x2_out[par], 16 * (TT // 2))
                sp.wait_ge(hn_out[par], 32 * (TT // 2))

        @block.gpsimd
        def _(pool):
            pool.memset(eps[:, 0:1], HEAD_EPS).then_inc(eps_set, 1)
            pool.memset(eps[:, 1:2], NORM_EPS).then_inc(eps_set, 1)

        @block.scalar
        def _(act):
            link = Link(act, act_own)
            act.wait_ge(eps_set, 2)
            act.activation(head_r[:, :], head_ss[:, :], ACT.Sqrt, bias=eps[:, 0:1], scale=1.0 / DH).then_inc(head_root, 1)

            def emit(a, b):
                if at := stage(a, b, -1):
                    n, half, par = at
                    need(act, y_done, n - 1)
                    act.wait_ge(c_turned, n + 1)
                    act.activation(c_hi[:, par, 0:4], ps_c[par][:, :].rearrange("p (k n) -> p k n", n=P),
                                   ACT.Copy).then_inc(c_high, 1)
                    act.activation(c_hi[:, par, 4:8], mixT[:, 0:4, span(n * P, P)], ACT.Copy).then_inc(c_high, 1)
                if isinstance(a, int) and b == -1:
                    for k in k_order:
                        for n, (lo, hi) in enumerate(wout_loads):
                            if k == lo:
                                act.wait_ge(wout_in[n], 16)
                        act.activation(wout_hi[:, k], wout_raw[:, k], ACT.Copy).then_inc(wout_high, 1)
                if at := stage(a, b, 0):
                    n, half, par = at
                    act.wait_ge(x2_ready, n + 1)
                    need(act, hn_out[par], half * 32)
                    need(act, hn_turned, n - 1)
                    link(act.activation(hn_sb[:, par], x2_sb[:, par], ACT.Square, accum_out=stat[:, 0, span(n, 1)]))
                    act.activation(stat[:, 1, span(n, 1)], stat[:, 0, span(n, 1)], ACT.Sqrt, bias=eps[:, 1:2],
                                   scale=1.0 / D).then_inc(root_ready, 1)
                if at := stage(a, b, 1):
                    n, half, par = at
                    act.wait_ge(hn_turned, n + 1)
                    act.wait_ge(routed, n)
                    act.activation(hnT[:, par], ps_h[:, :].rearrange("p (k n) -> p k n", n=P), ACT.Copy).then_inc(hnT_ready, 1)

            tile_steps(act, emit, link, 2)

        @block.vector
        def _(dve):
            link = Link(dve, dve_own)
            dve.sem_inc(logits_ready, 1)
            dve.sem_inc(routed, 1)
            dve.wait_ge(small_in, 96)
            link(dve.tensor_scalar(head_w[:, :], head_w[:, :], 1.0 - LAM_INIT, None, ALU.mult))
            dve.wait_ge(head_root, 1)
            link(dve.reciprocal(head_r[:, :], head_r[:, :]))

            def emit(a, b):
                if at := stage(a, b, -1):
                    n, half, par = at
                    need(dve, c_turned, n - 1)
                    for h in range(HEADS):
                        ins = dve.scalar_tensor_tensor(out=heads_n[:, par, h * DH:(h + 1) * DH],
                                                       in0=mixT[:, 4 + h, span(n * P, P)],
                                                       scalar=head_r[:, span(n + h * TT, 1)], in1=head_w[:, :],
                                                       op0=ALU.mult, op1=ALU.mult)
                    ins.then_inc(heads_ready, 1)
                    dve.wait_ge(c_high, n * 2 + 2)
                    dve.tensor_tensor(c_lo[:, par, 0:4], ps_c[par][:, :].rearrange("p (k n) -> p k n", n=P),
                                      c_hi[:, par, 0:4].bitcast(F32), ALU.subtract)
                    dve.tensor_tensor(c_lo[:, par, 4:8], mixT[:, 0:4, span(n * P, P)],
                                      c_hi[:, par, 4:8].bitcast(F32), ALU.subtract).then_inc(c_split, 1)
                if isinstance(a, int) and b == -1:
                    for j, k in enumerate(k_order):
                        dve.wait_ge(wout_high, j + 1)
                        dve.tensor_tensor(wout_lo[:, k], wout_raw[:, k], wout_hi[:, k].bitcast(F32),
                                          ALU.subtract).then_inc(wout_split, 1)
                if at := stage(a, b, 0):
                    n, half, par = at
                    dve.wait_ge(y_done, n + 1)
                    dve.wait_ge(x_in[par], half * 16 + 16)
                    need(dve, x2_out[par], half * 16)
                    dve.tensor_tensor(x2_sb[:, par], ps_y[par][:, :], x_sb[:, par], ALU.add).then_inc(x2_ready, 1)
                    dve.wait_ge(root_ready, n + 1)
                    link(dve.reciprocal(stat[:, 2, span(n, 1)], stat[:, 1, span(n, 1)]))
                    dve.scalar_tensor_tensor(out=hn_sb[:, par], in0=x2_sb[:, par], scalar=stat[:, 2, span(n, 1)],
                                             in1=norm_w[:, :], op0=ALU.mult, op1=ALU.mult).then_inc(hn_ready, 1)
                if at := stage(a, b, 2):
                    n, half, par = at
                    dve.wait_ge(routed, n + 2)
                    dve.tensor_tensor(logits[:, span(n, 1)].rearrange("p o n -> p (o n)"), ps_c[par][:, 0:NG + NE],
                                      b_rt[:, :], ALU.add).then_inc(logits_ready, 1)

            tile_steps(dve, emit, link, 2)

        @block.tensor
        def _(pe):
            def mix(n, par, js):
                for j in js:
                    k = k_order[j]
                    if isinstance(n, int) and n == 0:
                        pe.wait_ge(wout_split, j + 1)
                    mm = split_products(pe, [ps_y[par][:, h * HALF:(h + 1) * HALF] for h in range(2)],
                                        c_hi[:, par, k], c_lo[:, par, k],
                                        [wout_hi[:, k, h * HALF:(h + 1) * HALF] for h in range(2)],
                                        [wout_lo[:, k, h * HALF:(h + 1) * HALF] for h in range(2)],
                                        j == 0, j == KT - 1)
                return mm

            def emit(a, b):
                own = stage(a, b, 0)
                if own:
                    pe.wait_ge(c_split, own[0] + 1)
                    need(pe, x2_ready, own[0] - 1)
                    mix(own[0], own[2], range(KT // 2))
                if at := stage(a, b, -1):
                    n, half, par = at
                    pe.wait_ge(heads_ready, n + 1)
                    need(pe, c_split, n - 1)
                    need(pe, logits_ready, n - 2)
                    for h in range(HEADS):
                        mm = pe.transpose(ps_c[par][:, h * DH:(h + 1) * DH], heads_n[:, par, h * DH:(h + 1) * DH], ident[:, :])
                    mm.then_inc(c_turned, 1)
                if at := stage(a, b, 2):
                    n, half, par = at
                    pe.wait_ge(hnT_ready, n + 1)
                    if isinstance(n, int):
                        need(pe, logits_ready, n)
                    for k in range(KT):
                        mm = pe.matmul(ps_c[par][:, 0:NG + NE], hnT[:, par, k], w_rt[:, k], start=k == 0, stop=k == KT - 1)
                    mm.then_inc(routed, 1)
                if own:
                    mix(own[0], own[2], range(KT // 2, KT)).then_inc(y_done, 1)
                if at := stage(a, b, 1):
                    n, half, par = at
                    pe.wait_ge(hn_ready, n + 1)
                    need(pe, hnT_ready, n)
                    for k in range(KT):
                        mm = pe.transpose(ps_h[:, k * P:(k + 1) * P], hn_sb[:, par, k * P:(k + 1) * P], ident[:, :])
                    mm.then_inc(hn_turned, 1)

            tile_steps(pe, emit)


RING = 6
UNITS = KT + FT


def unit_number(s, u):
    if isinstance(s, int) and s in (0, NE):
        return u if s == 0 else s * UNITS - UNITS + u
    return s * UNITS + (u - FT)


class StepSems:

    def __init__(self, sem, tag, buffers):
        self.gu_in = [sem(f"{tag}_gu_in{p}") for p in range(buffers)]
        self.d_in = [sem(f"{tag}_d_in{p}") for p in range(buffers)]
        self.entry_ready = sem(f"{tag}_entry_ready")
        self.y_entry_ready = sem(f"{tag}_y_entry_ready")
        self.x_in = [sem(f"{tag}_x_in{p}") for p in range(buffers)]
        self.y_out = [sem(f"{tag}_y_out{p}") for p in range(buffers)]
        self.split_high = sem(f"{tag}_split_high")
        self.split_low = sem(f"{tag}_split_low")
        self.units_done = sem(f"{tag}_units_done")
        self.x_turned = sem(f"{tag}_x_turned")
        self.x_high = sem(f"{tag}_x_high")
        self.x_ready = sem(f"{tag}_x_ready")
        self.h_act_ready = sem(f"{tag}_h_act_ready")
        self.h_ready = sem(f"{tag}_h_ready")
        self.h_turned = sem(f"{tag}_h_turned")
        self.h_high = sem(f"{tag}_h_high")
        self.h_split = sem(f"{tag}_h_split")
        self.y_ready = sem(f"{tag}_y_ready")
        self.y_free = sem(f"{tag}_y_free")


def load_gate_up(sp, io, persist, q, e, par):
    for which, name in enumerate(("w_exp_gate", "w_exp_up")):
        sp.dma_start(persist["gu_raw"][:, par, which],
                     io[name][0][span(e, 1)].rearrange("o (k p) n -> p (o k) n", p=P)).then_inc(q.gu_in[par], 16)


def load_down(sp, io, persist, q, e, par):
    sp.dma_start(persist["d_raw"][:, par],
                 io["w_exp_down"][0][span(e, 1)].rearrange("o (f p) n -> p (o f) n", p=P)).then_inc(q.d_in[par], 16)


def route(nc, io, persist):
    logits, gates, extra = (persist[n] for n in ("logits", "gates", "extra"))
    with ExitStack() as ctx:
        sb = lambda name, shape, dt=F32: ctx.enter_context(nc.sbuf_tensor(name, shape, dt))
        sem = lambda name: ctx.enter_context(nc.semaphore(name))
        gmax = sb("gmax", [P, TT])
        gcand = sb("gcand", [P, TT, NG])
        gidx = sb("gidx", [P, TT])
        gexp = sb("gexp", [P, TT, NG])
        gsum = sb("gsum", [P, TT])
        masked = sb("masked", [P, TT, NE])
        cand = sb("cand", [P, TT, NE])
        top = sb("top", [P, 2, TT])
        idx = sb("idx", [P, TT])
        hot = sb("hot", [P, 2, TT, NE])
        both = sb("both", [P, TT, NE])
        diff = sb("diff", [P, 4, TT])
        cum = sb("cum", [P, TT + 1, NE])
        pos = sb("pos", [P, TT + 1, NE])
        more = sb("more", [P, NE])
        upto = sb("upto", [P, NE])
        base = sb("base", [P, NE])
        slot_e = sb("slot_e", [P, TT, NE])
        slot_f = sb("slot_f", [P, 2, TT])
        before = sb("before", [P, NX, NE])
        extra_f = sb("extra_f", [P, NX + 1])
        iota_g = sb("iota_g", [P, TT, NG])
        iota_e = sb("iota_e", [P, TT, NE])
        iota_s = sb("iota_s", [P, NE])
        iota_x = sb("iota_x", [P, NX, NE])
        ones = sb("ones", [P, P])
        earlier = sb("earlier", [P, P])
        slots = sb("slots", [P, 2, 2 * TT], I32)
        entry = sb("entry", [P, 2 * TT])
        place = sb("place", [P, 2, 2 * TT])
        iota_p = sb("iota_p", [P, 2 * TT, P])
        iota_c = sb("iota_c", [P, 2 * TT, CHUNKS])
        at_place = sb("at_place", [P, 2 * TT, P])
        in_chunk = sb("in_chunk", [P, 2 * TT, CHUNKS])
        found = sb("found", [P, 2, CHUNKS])
        ps = ctx.enter_context(nc.psum_tensor("ps_pos", [P, HALF], F32))
        ps_e = ctx.enter_context(nc.psum_tensor("ps_entry", [P, HALF], F32))

        set_up = sem("set_up")
        exp_asked = sem("exp_asked")
        exp_given = sem("exp_given")
        counts_asked = sem("counts_asked")
        counted = sem("counted")
        slots_ready = sem("slots_ready")
        found_sums = sem("found_sums")
        dve_own = sem("dve_own4")
        block = ctx.enter_context(nc.Block("route"))

        @block.sync
        def _(sp):
            m = persist["main_sems"]
            load_gate_up(sp, io, persist, m, 0, 0)
            load_down(sp, io, persist, m, 0, 0)
            load_gate_up(sp, io, persist, m, 1, 1)
            load_down(sp, io, persist, m, 1, 1)

        @block.gpsimd
        def _(pool):
            f = dict(allow_small_or_imprecise_dtypes=True)
            pool.iota(iota_g[:, :, :], [[0, TT], [1, NG]], base=-NG, channel_multiplier=0, **f).then_inc(set_up, 1)
            pool.iota(iota_e[:, :, :], [[0, TT], [1, NE]], base=-NE, channel_multiplier=0, **f).then_inc(set_up, 1)
            pool.iota(iota_s[:, :], [[P, NE]], base=0, channel_multiplier=0, **f).then_inc(set_up, 1)
            pool.iota(iota_x[:, :, :], [[1, NX], [0, NE]], base=0, channel_multiplier=0, **f).then_inc(set_up, 1)
            pool.iota(entry[:, :], [[SEQ, 2], [P, TT]], base=1, channel_multiplier=1, **f).then_inc(set_up, 1)
            pool.memset(ones[:, :], 1.0).then_inc(set_up, 1)
            pool.iota(iota_p[:, :, :], [[0, 2 * TT], [1, P]], base=0, channel_multiplier=0, **f).then_inc(set_up, 1)
            pool.iota(iota_c[:, :, :], [[0, 2 * TT], [1, CHUNKS]], base=0, channel_multiplier=0, **f).then_inc(set_up, 1)
            pool.wait_ge(set_up, 8)
            pool.affine_select(out=earlier[:, :], in_=ones[:, :], compare_op=ALU.is_gt, fill=0.0, base=0,
                               pattern=[[1, P]], channel_multiplier=-1).then_inc(set_up, 1)

        @block.scalar
        def _(act):
            act.wait_ge(exp_asked, 1)
            act.activation(gexp[:, :, :], gexp[:, :, :], ACT.Exp).then_inc(exp_given, 1)
            act.wait_ge(exp_asked, 2)
            act.activation(diff[:, 1, :], diff[:, 0, :], ACT.Exp).then_inc(exp_given, 1)

        @block.vector
        def _(dve):
            link = Link(dve, dve_own)
            lg, le = logits[:, :, 0:NG], logits[:, :, NG:]
            wide_g = lambda x: x.unsqueeze(2).to_broadcast([P, TT, NG])
            wide_e = lambda x: x.unsqueeze(2).to_broadcast([P, TT, NE])
            per_tile = lambda x: x.unsqueeze(1).to_broadcast([P, TT, NE])
            dve.wait_ge(set_up, 9)

            def first_max(value, number, where, index, values, wide, one_hot):
                link(dve.tensor_reduce(values, value, AX.X, ALU.max))
                link(dve.tensor_tensor(where, value, wide(values), ALU.is_equal))
                link(dve.tensor_tensor(where, where, number, ALU.mult))
                link(dve.tensor_reduce(index, where, AX.X, ALU.min))
                link(dve.tensor_tensor(one_hot, number, wide(index), ALU.is_equal))

            first_max(lg, iota_g[:, :, :], gcand[:, :, :], gidx[:, :], gmax[:, :], wide_g, gcand[:, :, :])
            dve.tensor_tensor(gexp[:, :, :], lg, wide_g(gmax[:, :]), ALU.subtract).then_inc(exp_asked, 1)
            link(dve.tensor_scalar(gcand[:, :, :], gcand[:, :, :], -1.0, BIG, ALU.add, ALU.mult))
            link(dve.tensor_tensor(masked[:, :, :].rearrange("p t (g e) -> p t g e", g=NG),
                                   le.rearrange("p t (g e) -> p t g e", g=NG),
                                   gcand[:, :, :].unsqueeze(3).to_broadcast([P, TT, NG, EPG]), ALU.add))
            first_max(masked[:, :, :], iota_e[:, :, :], cand[:, :, :], idx[:, :], top[:, 0, :], wide_e, hot[:, 0])
            link(dve.scalar_tensor_tensor(out=masked[:, :, :].rearrange("p t e -> p (t e)"),
                                          in0=hot[:, 0].rearrange("p t e -> p (t e)"), scalar=-BIG,
                                          in1=masked[:, :, :].rearrange("p t e -> p (t e)"), op0=ALU.mult, op1=ALU.add))
            first_max(masked[:, :, :], iota_e[:, :, :], cand[:, :, :], idx[:, :], top[:, 1, :], wide_e, hot[:, 1])
            dve.tensor_tensor(diff[:, 0, :], top[:, 1, :], top[:, 0, :], ALU.subtract).then_inc(exp_asked, 1)
            link(dve.tensor_tensor(both[:, :, :], hot[:, 0], hot[:, 1], ALU.add))
            link(dve.memset(cum[:, 0, :], 0.0))
            for t in range(TT):
                link(dve.tensor_tensor(cum[:, t + 1, :], cum[:, t, :], both[:, t, :], ALU.add))
            dve.sem_inc(counts_asked, 1)
            dve.wait_ge(exp_given, 1)
            link(dve.tensor_reduce(gsum[:, :], gexp[:, :, :], AX.X, ALU.add))
            link(dve.reciprocal(gsum[:, :], gsum[:, :]))
            dve.wait_ge(exp_given, 2)
            link(dve.tensor_scalar(diff[:, 2, :], diff[:, 1, :], 1.0, None, ALU.add))
            link(dve.reciprocal(diff[:, 2, :], diff[:, 2, :]))
            link(dve.tensor_tensor(gates[:, 0, :], diff[:, 2, :], gsum[:, :], ALU.mult))
            link(dve.tensor_tensor(gates[:, 1, :], gates[:, 0, :], diff[:, 1, :], ALU.mult))
            dve.wait_ge(counted, 1)
            link(dve.tensor_copy(pos[:, :, :].rearrange("p t e -> p (t e)"), ps[:, 0:(TT + 1) * NE]))
            count = pos[:, TT, :]
            link(dve.tensor_scalar(more[:, :], count, float(P), None, ALU.is_gt))
            for n in range(2, SEQ // P):
                link(dve.scalar_tensor_tensor(out=more[:, :], in0=count, scalar=float(n * P), in1=more[:, :],
                                              op0=ALU.is_gt, op1=ALU.add))
            link(dve.tensor_tensor_scan(upto[:, :], ones[:, 0:NE], more[:, :], 0.0, ALU.mult, ALU.add))
            link(dve.tensor_tensor(base[:, :], upto[:, :], more[:, :], ALU.subtract))
            link(dve.tensor_scalar(base[:, :], base[:, :], float(P), float((NE - 1) * P), ALU.mult, ALU.add))
            link(dve.tensor_tensor(base[:, :], base[:, :], iota_s[:, :], ALU.subtract))
            link(dve.tensor_scalar(slot_e[:, :, :], pos[:, 0:TT, :], float(P), None, ALU.is_ge))
            link(dve.tensor_tensor(slot_e[:, :, :], slot_e[:, :, :], per_tile(base[:, :]), ALU.mult))
            link(dve.tensor_tensor(slot_e[:, :, :], slot_e[:, :, :], pos[:, 0:TT, :], ALU.add))
            link(dve.tensor_tensor(slot_e[:, :, :], slot_e[:, :, :], per_tile(iota_s[:, :]), ALU.add))
            for which in range(2):
                link(dve.tensor_tensor(cand[:, :, :], slot_e[:, :, :], hot[:, which], ALU.mult))
                link(dve.tensor_reduce(slot_f[:, which, :], cand[:, :, :], AX.X, ALU.add))
            link(dve.tensor_copy(slots[:, 0, :], slot_f[:, :, :].rearrange("p w t -> p (w t)")))
            link(dve.tensor_scalar(slots[:, 1, :], slots[:, 0, :], 7, None, ALU.logical_shift_right))
            link(dve.tensor_scalar(slots[:, 0, :], slots[:, 0, :], P - 1, None, ALU.bitwise_and))
            link(dve.tensor_copy(place[:, :, :], slots[:, :, :]))
            dve.tensor_tensor(at_place[:, :, :], iota_p[:, :, :],
                              place[:, 0, :].unsqueeze(2).to_broadcast([P, 2 * TT, P]), ALU.is_equal)
            link(dve.tensor_tensor(in_chunk[:, :, :], iota_c[:, :, :],
                                   place[:, 1, :].unsqueeze(2).to_broadcast([P, 2 * TT, CHUNKS]), ALU.is_equal))
            dve.tensor_tensor(in_chunk[:, :, :], in_chunk[:, :, :],
                              entry[:, :].unsqueeze(2).to_broadcast([P, 2 * TT, CHUNKS]), ALU.mult).then_inc(slots_ready, 1)
            link(dve.tensor_tensor(before[:, :, :], upto[:, :].unsqueeze(1).to_broadcast([P, NX, NE]),
                                   iota_x[:, :, :], ALU.is_le))
            link(dve.tensor_reduce(extra_f[:, 0:NX], before[:, :, :], AX.X, ALU.add))
            link(dve.tensor_scalar(extra_f[:, 0:NX], extra_f[:, 0:NX], float(NE - 1), None, ALU.min))
            link(dve.tensor_copy(extra_f[:, NX:], upto[:, NE - 1:]))
            link(dve.tensor_copy(extra[:, :], extra_f[:, :]))
            dve.wait_ge(found_sums, 1)
            link(dve.tensor_scalar(found[:, 0, :], ps_e[:, 0:CHUNKS], 0.0, float(4 * SEQ), ALU.is_equal, ALU.mult))
            link(dve.tensor_tensor(found[:, 0, :], found[:, 0, :], ps_e[:, 0:CHUNKS], ALU.add))
            link(dve.tensor_scalar(found[:, 1, :], found[:, 0, :], -1.0, None, ALU.add))
            link(dve.tensor_copy(persist["entries"][:, :], found[:, 1, :]))

        @block.tensor
        def _(pe):
            pe.wait_ge(counts_asked, 1)
            pe.matmul(ps[:, 0:(TT + 1) * NE], ones[:, :], cum[:, :, :].rearrange("p t e -> p (t e)"), start=True,
                      stop=False, skip_group_check=True)
            pe.matmul(ps[:, 0:TT * NE], earlier[:, :], both[:, :, :].rearrange("p t e -> p (t e)"), start=False,
                      stop=True, skip_group_check=True).then_inc(counted, 1)
            pe.wait_ge(slots_ready, 1)
            for n in range(2 * TT):
                mm = pe.matmul(ps_e[:, 0:CHUNKS], at_place[:, n, :], in_chunk[:, n, :], start=n == 0, stop=n == 2 * TT - 1)
            mm.then_inc(found_sums, 1)
def x2_all(persist):
    return persist["gu_raw"][:, 1].rearrange("p a k n -> p (a k n)").rearrange("p (t n) -> p t n", n=D)


def experts(nc, io, persist):
    ident, extra = persist["ident"], persist["extra"]
    entries, hn_d, y_d = (persist[n] for n in ("entries", "hn_d", "y_d"))
    gu_raw, d_raw, m = (persist[n] for n in ("gu_raw", "d_raw", "main_sems"))
    hn_rows = hn_d.rearrange("c t d -> (c t) d")
    with ExitStack() as ctx:
        sb = lambda name, shape, dt=F32: ctx.enter_context(nc.sbuf_tensor(name, shape, dt))
        sem = lambda name: ctx.enter_context(nc.semaphore(name))
        w_hi = sb("w5_hi", [P, RING, D], F32R)
        w_lo = sb("w5_lo", [P, RING, D], F32R)
        entry = sb("entry5", [P, 2], I32)
        y_entry = sb("y_entry5", [P, 2], I32)
        x_sb = sb("x5_sb", [P, 2, D])
        x_hi = sb("x5_hi", [P, 2, KT, P], F32R)
        x_lo = sb("x5_lo", [P, 2, KT, P], F32R)
        h_act = sb("h_act", [P, FF])
        h_sb = sb("h_sb", [P, FF])
        h_hi = sb("h_hi", [P, FT, P], F32R)
        h_lo = sb("h_lo", [P, FT, P], F32R)
        y_sb = sb("y_sb", [P, 2, D])
        ps_gu = [ctx.enter_context(nc.psum_tensor(f"ps_gu{n}", [P, 2, HALF], F32)) for n in range(2)]
        ps_y = ctx.enter_context(nc.psum_tensor("ps_y5", [P, 2, HALF], F32))
        ps_t = ctx.enter_context(nc.psum_tensor("ps_t5", [P, 2, HALF], F32))

        x = StepSems(sem, "more", 1)
        x_cleared = sem("x_cleared")
        pool_seen = sem("pool_seen")
        block = ctx.enter_context(nc.Block("experts"))


        def raw_unit(u, par):
            return gu_raw[:, par, :, u] if u < KT else d_raw[:, par, u - KT].rearrange("p (a n) -> p a n", a=2)

        def two(tensor, r):
            return tensor[:, r].rearrange("p (a n) -> p a n", a=2)

        def turned_rows(bank):
            return bank.rearrange("p a (k n) -> p (a k) n", n=P)


        def high(act, q, n, r, u, par):
            if n is not None:
                need(act, q.units_done, n - (RING - 1))
            act.activation(two(w_hi, r), raw_unit(u, par), ACT.Copy).then_inc(q.split_high, 1)

        def low(dve, q, n, r, u, par):
            dve.wait_ge(q.split_high, n + 1)
            dve.tensor_tensor(two(w_lo, r), raw_unit(u, par), two(w_hi, r).bitcast(F32),
                              ALU.subtract).then_inc(q.split_low, 1)

        def products(pe, q, n, r, outs, lh, ll, start, stop):
            pe.wait_ge(q.split_low, n + 1)
            split_products(pe, outs, lh, ll, [two(w_hi, r)[:, a] for a in range(2)],
                           [two(w_lo, r)[:, a] for a in range(2)], start, stop).then_inc(q.units_done, 1)


        def take_entries(pool, copy, ready, n, par, chunk):
            pool.sem_inc(pool_seen, 1)
            pool.tensor_copy(copy[:, par:par + 1], entries[:, span(chunk, 1)]).then_inc(ready, 1)
            pool.wait_ge(ready, n + 1)
            pool.sem_inc(pool_seen, 1)

        def gather(pool, q, n, par, chunk):
            take_entries(pool, entry, q.entry_ready, n, par, chunk)
            pool.indirect_dma_start(out=x_sb[:, par], out_offset=None, in_=hn_rows,
                                    in_offset=bass.IndirectOffsetOnAxis(ap=entry[:, par:par + 1], axis=0),
                                    bounds_check=2 * SEQ - 1, oob_is_err=False).then_inc(q.x_in[par], 16)

        def scatter_y(pool, q, n, par, chunk):
            pool.wait_ge(q.y_ready, n + 1)
            take_entries(pool, y_entry, q.y_entry_ready, n, par, chunk)
            pool.indirect_dma_start(out=y_d, in_=y_sb[:, par], in_offset=None,
                                    out_offset=bass.IndirectOffsetOnAxis(ap=y_entry[:, par:par + 1], axis=0),
                                    bounds_check=2 * SEQ - 1, oob_is_err=False).then_inc(q.y_out[par], 16)

        def turn_x(pe, q, par):
            for k in range(KT):
                mm = pe.transpose(ps_t[:, k // 4, (k % 4) * P:(k % 4 + 1) * P], x_sb[:, par, k * P:(k + 1) * P], ident[:, :])
            mm.then_inc(q.x_turned, 1)

        def x_high(act, q, n, par):
            act.wait_ge(q.x_turned, n + 1)
            act.activation(x_hi[:, par], turned_rows(ps_t[:, :, :]), ACT.Copy).then_inc(q.x_high, 1)

        def x_low(dve, q, n, par):
            dve.wait_ge(q.x_high, n + 1)
            dve.tensor_tensor(x_lo[:, par], turned_rows(ps_t[:, :, :]), x_hi[:, par].bitcast(F32),
                              ALU.subtract).then_inc(q.x_ready, 1)

        def silu(act, q, par):
            act.activation(h_act[:, :], ps_gu[par][:, 0], ACT.Silu).then_inc(q.h_act_ready, 1)

        def hidden(dve, q, n, par):
            dve.wait_ge(q.h_act_ready, n + 1)
            dve.tensor_tensor(h_sb[:, :], ps_gu[par][:, 1], h_act[:, :], ALU.mult).then_inc(q.h_ready, 1)

        def turn_h(pe, q, n):
            pe.wait_ge(q.h_ready, n + 1)
            for f in range(FT):
                mm = pe.transpose(ps_t[:, 0, f * P:(f + 1) * P], h_sb[:, f * P:(f + 1) * P], ident[:, :])
            mm.then_inc(q.h_turned, 1)

        def h_high(act, q, n):
            act.wait_ge(q.h_turned, n + 1)
            act.activation(h_hi[:, :, :], ps_t[:, 0].rearrange("p (f n) -> p f n", n=P), ACT.Copy).then_inc(q.h_high, 1)

        def h_low(dve, q, n):
            dve.wait_ge(q.h_high, n + 1)
            dve.tensor_tensor(h_lo[:, :, :], ps_t[:, 0].rearrange("p (f n) -> p f n", n=P),
                              h_hi[:, :, :].bitcast(F32), ALU.subtract).then_inc(q.h_split, 1)

        def take_y(dve, q, par):
            dve.tensor_copy(two(y_sb, par), ps_y[:, :, :]).then_inc(q.y_ready, 1)

        def await_y(sp, q, half, par):
            sp.wait_ge(q.y_out[par], half * 16 + 16)
            sp.sem_inc(q.y_free, 1)

        gate_up, rows_y = [[ps_gu[p][:, a] for a in range(2)] for p in range(2)], [ps_y[:, a] for a in range(2)]

        def steps(eng, emit):
            emit(0, 0, 0)
            emit(1, 0, 1)
            with eng.Fori(0, (NE - 4) // 2) as i:
                emit(i * 2 + 2, i + 1, 0)
                emit(i * 2 + 3, i + 1, 1)
            for s in range(NE - 2, NE + 1):
                emit(s, s // 2, s % 2)

        def slot(s, u):
            return (u if isinstance(s, int) and s in (0, NE) else u - FT) % RING

        def more_chunks(eng, body):
            count = eng.value_load(extra[0:1, NX:NX + 1], min_val=0, max_val=NX)
            with eng.If(count > 0):
                with eng.Fori(0, count) as j:
                    body(j)

        def has(s, k=0):
            return not isinstance(s, int) or 0 <= s - k < NE

        @block.sync
        def _(sp):
            def emit(s, half, par):
                if has(s, -2):
                    sp.wait_ge(m.split_low, unit_number(s, KT))
                    load_gate_up(sp, io, persist, m, s + 2, par)
                if has(s, 2):
                    await_y(sp, m, half - 1, par)
                if has(s, -1) and not (isinstance(s, int) and s == 0):
                    sp.wait_ge(m.split_low, unit_number(s, UNITS))
                    load_down(sp, io, persist, m, s + 1, 1 - par)
                if isinstance(s, int) and s == NE - 1:
                    sp.wait_ge(m.split_low, unit_number(s, KT))
                    sp.dma_start(x2_all(persist), persist["x2_d"].rearrange("(t p) n -> p t n", p=P)
                                 ).then_inc(persist["x2_in"], 16)

            steps(sp, emit)
            await_y(sp, m, NE // 2 - 1, 1)
            sp.wait_ge(m.split_low, NE * UNITS)

            def chunk(j):
                e = sp.value_load(extra[0:1, bass.ds(j, 1)], min_val=0, max_val=NE - 1)
                load_gate_up(sp, io, persist, x, e, 0)
                load_down(sp, io, persist, x, e, 0)
                await_y(sp, x, j, 0)

            more_chunks(sp, chunk)

        @block.gpsimd
        def _(pool):
            pool.memset(x_sb[:, :, :], 0.0).then_inc(x_cleared, 1)
            pool.wait_ge(x_cleared, 1)
            gather(pool, m, 0, 0, 0)
            gather(pool, m, 1, 1, 1)
            with pool.Fori(1, NE // 2) as i:
                for par in range(2):
                    pool.wait_ge(m.x_turned, i * 2 + (par - 1))
                    gather(pool, m, i * 2 + par, par, i * 2 + par)
                    scatter_y(pool, m, i * 2 + (par - 2), par, i * 2 + (par - 2))
            for par in range(2):
                scatter_y(pool, m, NE - 2 + par, par, NE - 2 + par)
            pool.wait_ge(m.x_turned, NE)

            def chunk(j):
                gather(pool, x, j, 0, j + NE)
                pool.wait_ge(x.x_turned, j + 1)
                scatter_y(pool, x, j, 0, j + NE)

            more_chunks(pool, chunk)

        @block.scalar
        def _(act):
            def emit(s, half, par):
                for u in range(UNITS):
                    if u == 1 and has(s):
                        x_high(act, m, s, par)
                    if u == 1 and has(s, 1):
                        act.wait_ge(m.units_done, unit_number(s - 1, KT))
                        need(act, m.h_ready, s - 1)
                        silu(act, m, 1 - par)
                    if u == KT + 1 and has(s, 1):
                        h_high(act, m, s - 1)
                    if u < KT and has(s):
                        if u == 0:
                            act.wait_ge(m.gu_in[par], half * 32 + 32)
                        high(act, m, unit_number(s, u), slot(s, u), u, par)
                    if u >= KT and has(s, 1):
                        if u == KT:
                            act.wait_ge(m.d_in[1 - par], (half + par) * 16)
                        high(act, m, unit_number(s, u), slot(s, u), u, 1 - par)

            steps(act, emit)
            act.wait_ge(m.units_done, NE * UNITS)

            def chunk(j):
                x_high(act, x, j, 0)
                act.wait_ge(x.gu_in[0], j * 32 + 32)
                for u in range(UNITS):
                    if u == KT:
                        act.wait_ge(x.units_done, j * UNITS + KT)
                        silu(act, x, 0)
                        h_high(act, x, j)
                        act.wait_ge(x.d_in[0], j * 16 + 16)
                    high(act, x, None if u < RING else j * UNITS + u, u % RING, u, 0)
                act.wait_ge(x.units_done, j * UNITS + UNITS)

            more_chunks(act, chunk)

        @block.vector
        def _(dve):
            dve.sem_inc(m.y_free, 2)

            def take(n, par):
                dve.wait_ge(m.units_done, unit_number(n + 1, UNITS))
                dve.wait_ge(m.y_free, n + 1)
                take_y(dve, m, par)

            def emit(s, half, par):
                for u in range(UNITS):
                    if u == 1 and has(s):
                        x_low(dve, m, s, par)
                    if u == 1 and has(s, 1):
                        hidden(dve, m, s - 1, 1 - par)
                    if u == 5 and has(s, 2):
                        take(s - 2, par)
                    if u == KT + 1 and has(s, 1):
                        h_low(dve, m, s - 1)
                    if (u < KT and has(s)) or (u >= KT and has(s, 1)):
                        low(dve, m, unit_number(s, u), slot(s, u), u, par if u < KT else 1 - par)

            steps(dve, emit)
            take(NE - 1, 1)
            dve.wait_ge(m.y_free, NE + 2)

            def chunk(j):
                x_low(dve, x, j, 0)
                for u in range(UNITS):
                    if u == KT:
                        hidden(dve, x, j, 0)
                        h_low(dve, x, j)
                    low(dve, x, j * UNITS + u, u % RING, u, 0)
                dve.wait_ge(x.units_done, j * UNITS + UNITS)
                take_y(dve, x, 0)
                dve.wait_ge(x.y_free, j + 1)

            more_chunks(dve, chunk)

        @block.tensor
        def _(pe):
            def turn_next(n, half, par):
                pe.wait_ge(m.x_in[par], half * 16 + 16)
                need(pe, m.x_ready, n)
                need(pe, m.h_split, n - 1)
                turn_x(pe, m, par)

            def emit(s, half, par):
                if isinstance(s, int) and s == 0:
                    turn_next(0, 0, 0)
                for u in range(KT):
                    if u == KT // 2 and has(s, 1):
                        turn_h(pe, m, s - 1)
                    if has(s):
                        if u == 0:
                            pe.wait_ge(m.x_ready, s + 1)
                            need(pe, m.h_ready, s - 1)
                        products(pe, m, unit_number(s, u), slot(s, u), gate_up[par], x_hi[:, par, u], x_lo[:, par, u],
                                 u == 0, u == KT - 1)
                if has(s, -1):
                    turn_next(s + 1, half + par, 1 - par)
                if has(s, 1):
                    pe.wait_ge(m.h_split, s)
                    need(pe, m.y_ready, s - 1)
                    for f in range(FT):
                        products(pe, m, unit_number(s, KT + f), slot(s, KT + f), rows_y, h_hi[:, f], h_lo[:, f],
                                 f == 0, f == FT - 1)

            steps(pe, emit)
            pe.wait_ge(m.y_ready, NE)

            def chunk(j):
                pe.wait_ge(x.x_in[0], j * 16 + 16)
                turn_x(pe, x, 0)
                pe.wait_ge(x.x_ready, j + 1)
                for u in range(KT):
                    products(pe, x, j * UNITS + u, u % RING, gate_up[0], x_hi[:, 0, u], x_lo[:, 0, u], u == 0, u == KT - 1)
                turn_h(pe, x, j)
                pe.wait_ge(x.h_split, j + 1)
                for f in range(FT):
                    products(pe, x, j * UNITS + KT + f, (KT + f) % RING, rows_y, h_hi[:, f], h_lo[:, f], f == 0, f == FT - 1)
                pe.wait_ge(x.y_ready, j + 1)

            more_chunks(pe, chunk)


def combine(nc, io, persist, out):
    gates, x2_in, x2_sb = persist["gates"], persist["x2_in"], x2_all(persist)
    with ExitStack() as ctx:
        sb = lambda name, shape, dt=F32: ctx.enter_context(nc.sbuf_tensor(name, shape, dt))
        sem = lambda name: ctx.enter_context(nc.semaphore(name))
        y_sb = sb("y_6", [P, 2, TT, D])
        o_sb = sb("o_6", [P, 2, D])
        norm_w = sb("final_w", [P, D])
        stat = sb("stat6", [P, 3, TT])
        eps = sb("eps6", [P, 1])
        norm_w_in = sem("final_w_in")
        y_in = [sem(f"y_in{t}") for t in range(TT)]
        o_out = [sem(f"o_out{n}") for n in range(2)]
        eps_set = sem("eps_set6")
        sum_ready = sem("sum_ready")
        root_ready = sem("root6_ready")
        o_ready = sem("o_ready")
        act_own = sem("act_own6")
        dve_own = sem("dve_own6")
        block = ctx.enter_context(nc.Block("combine"))

        @block.sync
        def _(sp):
            for t in range(TT):
                for which in range(2):
                    row = which * SEQ + t * P
                    sp.dma_start(y_sb[:, which, t], persist["y_d"][row:row + P, :]).then_inc(y_in[t], 16)
                if t == 0:
                    sp.dma_start(norm_w[:, :], io["final_norm_w"].partition_broadcast(P)).then_inc(norm_w_in, 16)
            for t in range(TT):
                sp.wait_ge(o_ready, t + 1)
                sp.dma_start(out[0][t * P:(t + 1) * P, :], o_sb[:, t % 2]).then_inc(o_out[t % 2], 16)
            for par in range(2):
                sp.wait_ge(o_out[par], 16 * (TT // 2))

        @block.gpsimd
        def _(pool):
            pool.memset(eps[:, :], NORM_EPS).then_inc(eps_set, 1)

        @block.vector
        def _(dve):
            link = Link(dve, dve_own)

            def add(t):
                dve.wait_ge(x2_in, 16)
                dve.wait_ge(y_in[t], 32)
                link(dve.scalar_tensor_tensor(out=x2_sb[:, t], in0=y_sb[:, 0, t], scalar=gates[:, 0, t:t + 1],
                                              in1=x2_sb[:, t], op0=ALU.mult, op1=ALU.add))
                dve.scalar_tensor_tensor(out=x2_sb[:, t], in0=y_sb[:, 1, t], scalar=gates[:, 1, t:t + 1],
                                         in1=x2_sb[:, t], op0=ALU.mult, op1=ALU.add).then_inc(sum_ready, 1)

            def norm(t):
                dve.wait_ge(root_ready, t + 1)
                link(dve.reciprocal(stat[:, 2, t:t + 1], stat[:, 1, t:t + 1]))
                need(dve, o_out[t % 2], 16 * (t // 2))
                dve.scalar_tensor_tensor(out=o_sb[:, t % 2], in0=x2_sb[:, t], scalar=stat[:, 2, t:t + 1],
                                         in1=norm_w[:, :], op0=ALU.mult, op1=ALU.mult).then_inc(o_ready, 1)

            dve.wait_ge(norm_w_in, 16)
            add(0)
            for t in range(TT):
                if t + 1 < TT:
                    add(t + 1)
                norm(t)

        @block.scalar
        def _(act):
            link = Link(act, act_own)
            act.wait_ge(eps_set, 1)
            for t in range(TT):
                act.wait_ge(sum_ready, t + 1)
                link(act.activation(y_sb[:, 0, t], x2_sb[:, t], ACT.Square, accum_out=stat[:, 0, t:t + 1]))
                act.activation(stat[:, 1, t:t + 1], stat[:, 0, t:t + 1], ACT.Sqrt, bias=eps[:, 0:1],
                               scale=1.0 / D).then_inc(root_ready, 1)


def build(nc, io, out):
    with ExitStack() as ctx:
        persist = {
            "ident": ctx.enter_context(nc.sbuf_tensor("ident", [P, P], F32)),
        }
        persist["head_ss"] = ctx.enter_context(nc.sbuf_tensor("head_ss", [P, HEADS * TT], F32))
        persist["logits"] = ctx.enter_context(nc.sbuf_tensor("logits", [P, TT, NG + NE], F32))
        persist["gates"] = ctx.enter_context(nc.sbuf_tensor("gates", [P, 2, TT], F32))
        persist["extra"] = ctx.enter_context(nc.sbuf_tensor("extra", [P, NX + 1], I32))
        persist["x2_d"] = nc.dram_tensor("x2_d", (SEQ, D), F32).ap()
        persist["hn_d"] = nc.dram_tensor("hn_d", (2, SEQ, D), F32).ap()
        persist["y_d"] = nc.dram_tensor("y_d", (2 * SEQ, D), F32).ap()
        persist["entries"] = ctx.enter_context(nc.sbuf_tensor("entries", [P, CHUNKS], I32))
        with nc.sbuf_tensor("mixT", [P, 2 * CT, SEQ], F32) as mixT:
            persist["mixT"] = mixT
            with nc.sbuf_tensor("qkvT", [P, 12, SEQ], F32) as qkvT:
                persist["qkvT"] = qkvT
                project_and_recur(nc, io, persist)
                attend(nc, io, persist)
            mix_out(nc, io, persist)
        persist["x2_in"] = ctx.enter_context(nc.semaphore("x2_in"))
        with ExitStack() as moe:
            persist["gu_raw"] = moe.enter_context(nc.sbuf_tensor("gu_raw", [P, 2, 2, KT, FF], F32))
            persist["d_raw"] = moe.enter_context(nc.sbuf_tensor("d_raw", [P, 2, FT, D], F32))
            persist["main_sems"] = StepSems(lambda name: moe.enter_context(nc.semaphore(name)), "main", 2)
            route(nc, io, persist)
            experts(nc, io, persist)
            combine(nc, io, persist, out)


_INS = ["x", "mix_norm_w", "w_in", "lambda_q1", "lambda_k1", "lambda_q2", "lambda_k2", "head_norm_w", "conv_w",
        "conv_b", "w_rgate", "b_rgate", "w_igate", "b_igate", "lru_lambda", "w_out", "ffn_norm_w",
        "w_router_group", "b_router_group", "w_router_expert", "b_router_expert", "w_exp_gate", "w_exp_up",
        "w_exp_down", "final_norm_w"]


def kernel(**inputs):
    import numpy as _np
    import concourse.bacc as _bacc
    from concourse.bass_utils import run_bass_kernel_spmd as _run

    nc = _bacc.Bacc("TRN2", target_bir_lowering=False, num_devices=1)
    arrays, io = {}, {}
    for name in _INS:
        a = _np.ascontiguousarray(inputs[name])
        arrays[f"in_{name}"] = a
        io[name] = nc.dram_tensor(f"in_{name}", a.shape, mybir.dt.from_np(a.dtype), kind="ExternalInput").ap()
    out = nc.dram_tensor("out_0", (1, SEQ, D), F32, kind="ExternalOutput").ap()
    build(nc, io, out)
    r = _run(nc, [arrays], core_ids=[0])
    return r.results[0]["out_0"]
```

```python
from contextlib import ExitStack

import concourse.bass as bass
from concourse import mybir

P = 128
F32 = mybir.dt.float32
F32R = mybir.dt.float32r
I32 = mybir.dt.int32
U32 = mybir.dt.uint32
ALU = mybir.AluOpType
ACT = mybir.ActivationFunctionType
AX = mybir.AxisListType
SEQ = 1024
D = 1024
KT = D // P
TT = SEQ // P
HALF = 512
HEADS = 4
DH = 128
QK = 64
CT = 4
NORM_EPS = 1e-6
HEAD_EPS = 1e-5
LAM_INIT = 0.2
NG = 4
EPG = 8
NE = NG * EPG
FF = D // 2
FT = FF // P
NX = SEQ * 2 // P - 1
CHUNKS = NE + NX
BIG = 1e30


class Link:

    def __init__(self, eng, sem):
        self.eng, self.sem, self.n, self.i, self.per, self.mark = eng, sem, 0, None, 0, 0

    def loop(self, i, per):
        self.i, self.per, self.mark = i, per, self.n

    def end(self, times):
        assert self.n - self.mark == self.per, (self.n - self.mark, self.per)
        self.n, self.i = self.mark + self.per * times, None

    def __call__(self, ins):
        self.n += 1
        ins.then_inc(self.sem, 1)
        self.eng.wait_ge(self.sem, self.n if self.i is None else self.i * self.per + self.n)


def span(start, n):
    return slice(start, start + n) if isinstance(start, int) else bass.ds(start, n)


def split_products(pe, out, lh, ll, rh, rl, start, stop):
    nc_mm = pe.matmul
    for o, h in zip(out, range(len(out))):
        nc_mm(o, lh, rh[h], start=start, stop=False)
    for o, h in zip(out, range(len(out))):
        nc_mm(o, lh, rl[h], start=False, stop=False)
    for o, h in zip(out, range(len(out))):
        last = nc_mm(o, ll, rh[h], start=False, stop=stop)
    return last


def project_and_recur(nc, io, persist):
    mixT, qkvT, ident = persist["mixT"], persist["qkvT"], persist["ident"]
    with ExitStack() as ctx:
        sb = lambda name, shape, dt=F32: ctx.enter_context(nc.sbuf_tensor(name, shape, dt))
        sem = lambda name: ctx.enter_context(nc.semaphore(name))
        hT_hi = sb("hT_hi", [P, KT, SEQ], F32R)
        hT_lo = sb("hT_lo", [P, KT, SEQ], F32R)
        w_raw = sb("w_raw", [P, 2, KT, 2 * P])
        w_hi = sb("w_hi", [P, 2, KT, P], F32R)
        w_lo = sb("w_lo", [P, 2, KT, P], F32R)
        q_parts, k_parts = persist["q_parts"], persist["k_parts"]
        tmp = [parts[:, n].bitcast(F32) for parts in (q_parts, k_parts) for n in range(2)] + [sb("tmp", [P, SEQ])]
        gate_w = sb("gate_w", [P, CT, 2, P])
        gate_cur = sb("gate_cur", [P, 2, P])
        rows = sb("rows", [32, P])
        chan = sb("chan", [P, 32])
        soft = sb("soft", [P, 8, CT])
        stat = sb("stat", [P, 3, TT])
        eps = sb("eps", [P, 1])
        ps = [ctx.enter_context(nc.psum_tensor(f"ps_proj{n}", [P, 2, HALF], F32)) for n in range(2)]
        ps_t = [ctx.enter_context(nc.psum_tensor(f"ps_turn{n}", [P, 2, HALF], F32)) for n in range(2)]
        junk, xn_sb, norm_w = tmp[0:2], tmp[2:4], tmp[4]
        x_sb = lambda n: qkvT[:, span(n, 1)].rearrange("p o n -> p (o n)")
        conv_x, r_sb, i_sb, a_sb, t_sb = tmp

        rows_in = sem("rows_in")
        norm_w_in = sem("norm_w_in")
        gates_in = sem("gates_in")
        x_in = [sem(f"x_in{n}") for n in range(2)]
        w_in = [sem(f"w_in{n}") for n in range(2)]
        consts = sem("consts")
        ident0 = sem("ident0")
        chan_t = sem("chan_t")
        chan_ready = sem("chan_ready")
        exp_ready = sem("exp_ready")
        soft_ready = sem("soft_ready")
        root_ready = sem("root_ready")
        xn_ready = sem("xn_ready")
        turned = sem("turned")
        hi_out = sem("hi_out")
        lo_out = sem("lo_out")
        w_free = sem("w_free")
        w_hi_ready = sem("w_hi_ready")
        w_lo_ready = sem("w_lo_ready")
        proj_done = sem("proj_done")
        proj_out = sem("proj_out")
        cur_ready = sem("cur_ready")
        conv_ready = sem("conv_ready")
        gates_done = sem("gates_done")
        gates_read = sem("gates_read")
        tanh_ready = sem("tanh_ready")
        ratio_ready = sem("ratio_ready")
        sqrt_ready = sem("sqrt_ready")
        gelu_ready = sem("gelu_ready")
        lru_done = sem("lru_done")
        act_own = sem("act_own")
        dve_own = sem("dve_own")
        block = ctx.enter_context(nc.Block("project"))

        w_cols = io["w_in"][0].rearrange("(k p) n -> p k n", p=P)

        @block.sync
        def _(sp):
            for c in range(2):
                sp.dma_start(x_sb(c), io["x"][0][c * P:(c + 1) * P, :]).then_inc(x_in[c], 16)
            sp.dma_start(norm_w[:, :], io["mix_norm_w"][0].partition_broadcast(P)).then_inc(norm_w_in, 16)
            with sp.Fori(1, TT // 2) as i:
                for c in range(2):
                    sp.wait_ge(x_in[c], i * 16)
                    sp.dma_start(x_sb(i * 2 + c), io["x"][0][bass.ds(i * (2 * P) + c * P, P), :]).then_inc(x_in[c], 16)
            for src, at, n in ((io["conv_w"], 0, 16), (io["conv_b"], 16, 4), (io["b_rgate"], 20, 4),
                               (io["b_igate"], 24, 4), (io["lru_lambda"], 28, 4)):
                flat = src.rearrange("l w (t p) -> (l w t) p", p=P) if n == 16 else \
                    src.rearrange("l (t p) -> (l t) p", p=P)
                sp.dma_start(rows[at:at + n, :], flat).then_inc(rows_in, 16)

            def load(col, n, c):
                sp.wait_ge(w_free, n)
                sp.dma_start(w_raw[:, c], w_cols[:, :, bass.ds(col, 2 * P)]).then_inc(w_in[c], 16)

            with sp.Fori(0, 2) as i:
                for c in range(2):
                    load((i * -HALF) + (4 * HALF + c * 2 * P), i * 2 + (c + 1), c)
            with sp.Fori(0, 2) as i:
                for c in range(2):
                    load(i * HALF + c * 2 * P, i * 2 + (c + 5), c)
            for c in range(2):
                load(2 * HALF + c * 2 * P, c + 9, c)

        @block.gpsimd
        def _(pool):
            pool.memset(ident[:, :], 0.0).then_inc(ident0, 1)
            pool.memset(eps[:, :], NORM_EPS).then_inc(ident0, 1)
            pool.memset(gate_w[:, :, :, :], 0.0).then_inc(ident0, 1)
            pool.wait_ge(ident0, 3)
            pool.affine_select(out=ident[:, :], in_=ident[:, :], compare_op=ALU.not_equal, fill=1.0, base=0,
                               pattern=[[-1, P]], channel_multiplier=1).then_inc(consts, 1)
            for g, src in enumerate((io["w_rgate"], io["w_igate"])):
                for b in range(2):
                    half = slice(64 * b, 64 * b + 64)
                    pool.dma_start(gate_w[half, :, g, half],
                                   src[0].rearrange("(t b) i j -> b i t j", b=2)[b]).then_inc(gates_in, 16)
            pool.wait_ge(gates_in, 64)
            with pool.Fori(0, CT) as t:
                pool.wait_ge(gates_done, t + 1)
                pool.tensor_copy(gate_cur[:, :, :], gate_w[:, bass.ds(t, 1)].rearrange("p o g j -> p (o g) j")).then_inc(cur_ready, 1)

        @block.scalar
        def _(act):
            link = Link(act, act_own)
            act.wait_ge(ident0, 3)

            def square(i, c):
                act.wait_ge(x_in[c], i * 16 + 16)
                link(act.activation(junk[c][:, :], x_sb(i * 2 + c), ACT.Square,
                                    accum_out=stat[:, 0, span(i * 2 + c, 1)]))
                act.activation(stat[:, 1, span(i * 2 + c, 1)], stat[:, 0, span(i * 2 + c, 1)], ACT.Sqrt,
                               bias=eps[:, 0:1], scale=1.0 / D).then_inc(root_ready, 1)

            def high(i, c):
                act.wait_ge(turned, i * 2 + (c + 3))
                act.activation(hT_hi[:, :, span(i * 2 * P + c * P, P)],
                               ps_t[c][:, :, :].rearrange("p a (k n) -> p (a k) n", n=P), ACT.Copy).then_inc(hi_out, 1)

            def split_high(n, c):
                if c % 2 == 0:
                    act.wait_ge(w_in[c // 2], n[1])
                act.wait_ge(proj_done, n[0] + 1)
                act.activation(w_hi[:, c % 2], w_raw[:, c // 2, :, (c % 2) * P:(c % 2 + 1) * P],
                               ACT.Copy).then_inc(w_hi_ready, 1)

            def evacuate(n, dst, c):
                act.wait_ge(proj_done, n + 3)
                act.activation(dst, ps[c % 2][:, :, :].rearrange("p a n -> p (a n)"), ACT.Copy).then_inc(proj_out, 1)

            def gates(i, c):
                t = i * 2 + c // 2
                act.wait_ge(gates_done, t + 2)
                act.wait_ge(lru_done, t + 1)
                link(act.activation(r_sb[:, :], ps_t[0][:, :, :].rearrange("p a n -> p (a n)"), ACT.Sigmoid,
                                    bias=chan[:, bass.ds(t + 20, 1)]))
                act.activation(i_sb[:, :], ps_t[1][:, :, :].rearrange("p a n -> p (a n)"), ACT.Sigmoid,
                               bias=chan[:, bass.ds(t + 24, 1)]).then_inc(gates_read, 1)
                act.activation(t_sb[:, :], r_sb[:, :], ACT.Tanh, scale=soft[:, 6, bass.ds(t, 1)]).then_inc(tanh_ready, 1)
                act.activation(a_sb[:, :], r_sb[:, :], ACT.Exp, scale=soft[:, 7, bass.ds(t, 1)]).then_inc(tanh_ready, 1)
                act.wait_ge(ratio_ready, t + 1)
                act.activation(t_sb[:, :], t_sb[:, :], ACT.Sqrt).then_inc(sqrt_ready, 1)
                act.activation(mixT[:, bass.ds(t, 1)], mixT[:, bass.ds(t, 1)], ACT.Gelu_apprx_tanh).then_inc(gelu_ready, 1)

            square(0, 0)
            square(0, 1)
            with act.Fori(0, TT // 2 - 1) as i:
                link.loop(i, 2)
                for c in range(2):
                    square(i + 1, c)
                    high(i, c)
            link.end(TT // 2 - 1)
            split_high((0, 16), 0)
            high(TT // 2 - 1, 0)
            high(TT // 2 - 1, 1)
            act.wait_ge(chan_ready, 2)
            act.activation(soft[:, 2, :], soft[:, 1, :], ACT.Exp, scale=-1.0).then_inc(exp_ready, 1)
            for group in range(2):
                with act.Fori(0, 2) as i:
                    if group:
                        link.loop(i, 2)
                    for c in range(4):
                        base = 8 * group + c
                        nxt = (c + 1) % 4
                        nth = 2 * group + 1 + (c == 3)
                        split_high((i * 4 + (base + 1), i * 16 + 16 * nth), nxt)
                        if group and c == 0:
                            act.wait_ge(soft_ready, 1)
                            act.wait_ge(proj_out, 10)
                        if group and c % 2 == 1:
                            gates(i, c)
                        dst = (qkvT if group else mixT)[:, bass.ds(i * 4 + c, 1)]
                        evacuate(i * 4 + base, dst.rearrange("p o n -> p (o n)"), c)
                if group:
                    link.end(2)
            for c in range(4):
                if c < 3:
                    split_high((17 + c, 16 * 5), c + 1)
                if c == 3:
                    act.wait_ge(lru_done, CT + 1)
                    act.activation(q_parts[:, 0], qkvT[:, 0], ACT.Copy).then_inc(hi_out, 1)
                    act.activation(k_parts[:, 0], qkvT[:, 4], ACT.Copy).then_inc(hi_out, 1)
                evacuate(16 + c, qkvT[:, 8 + c], c)

        @block.vector
        def _(dve):
            link = Link(dve, dve_own)
            dve.sem_inc(w_free, 2)
            dve.sem_inc(lru_done, 1)
            def scale(i, c):
                dve.wait_ge(root_ready, i * 2 + (c + 1))
                link(dve.reciprocal(stat[:, 2, span(i * 2 + c, 1)], stat[:, 1, span(i * 2 + c, 1)]))
                dve.wait_ge(turned, i * 2 + (c + 1))
                dve.scalar_tensor_tensor(out=xn_sb[c][:, :], in0=x_sb(i * 2 + c),
                                         scalar=stat[:, 2, span(i * 2 + c, 1)],
                                         in1=norm_w[:, :], op0=ALU.mult, op1=ALU.mult).then_inc(xn_ready, 1)

            def low(i, c):
                dve.wait_ge(hi_out, i * 2 + (c + 1))
                at = span(i * 2 * P + c * P, P)
                dve.tensor_tensor(hT_lo[:, :, at], ps_t[c][:, :, :].rearrange("p a (k n) -> p (a k) n", n=P),
                                  hT_hi[:, :, at].bitcast(F32), ALU.subtract).then_inc(lo_out, 1)

            dve.wait_ge(norm_w_in, 16)
            scale(0, 0)
            scale(0, 1)
            with dve.Fori(0, TT // 2 - 1) as i:
                link.loop(i, 2)
                for c in range(2):
                    scale(i + 1, c)
                    low(i, c)
            link.end(TT // 2 - 1)

            def split_low(n, c):
                dve.wait_ge(w_hi_ready, n)
                ins = dve.tensor_tensor(w_lo[:, c % 2], w_raw[:, c // 2, :, (c % 2) * P:(c % 2 + 1) * P],
                                        w_hi[:, c % 2].bitcast(F32), ALU.subtract)
                ins.then_inc(w_lo_ready, 1)
                if c % 2 == 1:
                    dve.wait_ge(w_lo_ready, n)
                    dve.sem_inc(w_free, 1)

            def convolve(t):
                x_t = mixT[:, bass.ds(t + 4, 1)].rearrange("p o n -> p (o n)")
                link(dve.tensor_scalar(conv_x[:, :], x_t, chan[:, bass.ds(t + 12, 1)], chan[:, bass.ds(t + 16, 1)],
                                       ALU.mult, ALU.add))
                for back in (1, 2, 3):
                    link(dve.scalar_tensor_tensor(
                        out=conv_x[:, back:], in0=mixT[:, bass.ds(t + 4, 1), 0:SEQ - back].rearrange("p o n -> p (o n)"),
                        scalar=chan[:, bass.ds(t + 4 * (3 - back), 1)],
                        in1=conv_x[:, back:], op0=ALU.mult, op1=ALU.add))
                dve.sem_inc(conv_ready, 1)

            def recur(t):
                dve.wait_ge(tanh_ready, t * 2 + 2)
                link(dve.tensor_tensor(r_sb[:, :], a_sb[:, :], a_sb[:, :], ALU.mult))
                dve.scalar_tensor_tensor(out=t_sb[:, :], in0=r_sb[:, :], scalar=1.0, in1=t_sb[:, :],
                                         op0=ALU.add, op1=ALU.mult).then_inc(ratio_ready, 1)
                link(dve.tensor_tensor(i_sb[:, :], i_sb[:, :], conv_x[:, :], ALU.mult))
                dve.wait_ge(sqrt_ready, t + 1)
                link(dve.tensor_tensor(i_sb[:, :], i_sb[:, :], t_sb[:, :], ALU.mult))
                link(dve.tensor_tensor_scan(r_sb[:, :], a_sb[:, :], i_sb[:, :], 0.0, ALU.mult, ALU.add))
                dve.wait_ge(gelu_ready, t + 1)
                gate = mixT[:, bass.ds(t, 1)].rearrange("p o n -> p (o n)")
                dve.tensor_tensor(gate, gate, r_sb[:, :], ALU.mult).then_inc(lru_done, 1)

            split_low(1, 0)
            low(TT // 2 - 1, 0)
            low(TT // 2 - 1, 1)
            dve.wait_ge(chan_t, 1)
            dve.tensor_copy(chan[:, :], ps_t[0][:, 0, 0:32]).then_inc(chan_ready, 1)
            dve.wait_ge(chan_ready, 1)
            lam = chan[:, 28:32]
            link(dve.tensor_scalar(soft[:, 0, :], lam, -1.0, 0.0, ALU.mult, ALU.max))
            dve.scalar_tensor_tensor(out=soft[:, 1, :], in0=lam, scalar=-1.0, in1=lam, op0=ALU.mult,
                                     op1=ALU.max).then_inc(chan_ready, 1)
            dve.wait_ge(exp_ready, 1)
            link(dve.tensor_scalar(soft[:, 3, :], soft[:, 2, :], 2.0, None, ALU.add))
            link(dve.reciprocal(soft[:, 3, :], soft[:, 3, :]))
            link(dve.tensor_tensor(soft[:, 3, :], soft[:, 3, :], soft[:, 2, :], ALU.mult))
            link(dve.tensor_tensor(soft[:, 4, :], soft[:, 3, :], soft[:, 3, :], ALU.mult))
            link(dve.tensor_scalar(soft[:, 5, :], soft[:, 4, :], 1.0 / 19.0, None, ALU.mult))
            for odd in range(17, 2, -2):
                link(dve.scalar_tensor_tensor(out=soft[:, 5, :], in0=soft[:, 5, :], scalar=1.0 / odd,
                                              in1=soft[:, 4, :], op0=ALU.add, op1=ALU.mult))
            link(dve.scalar_tensor_tensor(out=soft[:, 5, :], in0=soft[:, 5, :], scalar=1.0, in1=soft[:, 3, :],
                                          op0=ALU.add, op1=ALU.mult))
            link(dve.scalar_tensor_tensor(out=soft[:, 5, :], in0=soft[:, 5, :], scalar=2.0, in1=soft[:, 0, :],
                                          op0=ALU.mult, op1=ALU.add))
            link(dve.tensor_scalar(soft[:, 6, :], soft[:, 5, :], 8.0, None, ALU.mult))
            dve.tensor_scalar(soft[:, 7, :], soft[:, 5, :], -8.0, None, ALU.mult).then_inc(soft_ready, 1)
            with dve.Fori(0, 2) as i:
                for c in range(4):
                    split_low(i * 4 + (c + 2), (c + 1) % 4)
            with dve.Fori(0, 2) as i:
                link.loop(i, 2 * 8)
                for c in range(4):
                    split_low(i * 4 + (c + 10), (c + 1) % 4)
                    if c == 0:
                        dve.wait_ge(proj_out, 10)
                    if c % 2 == 0:
                        convolve(i * 2 + c // 2)
                    else:
                        recur(i * 2 + c // 2)
            link.end(2)
            for c in range(1, 4):
                split_low(17 + c, c)
            dve.wait_ge(proj_out, 16)
            for n, parts in enumerate((q_parts, k_parts)):
                dve.wait_ge(hi_out, TT + 1 + n)
                dve.tensor_tensor(parts[:, 1], qkvT[:, 4 * n], parts[:, 0].bitcast(F32), ALU.subtract)

        @block.tensor
        def _(pe):
            for free, n in ((turned, 2), (lo_out, 2), (proj_done, 2), (proj_out, 2), (gates_done, 1), (gates_read, 1)):
                pe.sem_inc(free, n)
            pe.wait_ge(consts, 1)

            def turn(i, c):
                pe.wait_ge(xn_ready, i * 2 + (c + 1))
                pe.wait_ge(lo_out, i * 2 + (c + 1))
                for k in range(KT):
                    last = pe.transpose(ps_t[c][:, k // 4, (k % 4) * P:(k % 4 + 1) * P],
                                        xn_sb[c][:, k * P:(k + 1) * P], ident[:, :])
                last.then_inc(turned, 1)

            with pe.Fori(0, TT // 2) as i:
                turn(i, 0)
                turn(i, 1)
            pe.wait_ge(lo_out, TT + 2)
            pe.wait_ge(rows_in, 80)
            pe.transpose(ps_t[0][:, 0, 0:32], rows[:, :], ident[0:32, 0:32]).then_inc(chan_t, 1)

            def tile(n, c):
                pe.wait_ge(w_lo_ready, n)
                pe.wait_ge(proj_out, n)
                for k in range(KT):
                    last = split_products(pe, [ps[c % 2][:, h, :] for h in range(2)],
                                          w_hi[:, c % 2, k, :], w_lo[:, c % 2, k, :],
                                          [hT_hi[:, k, h * HALF:(h + 1) * HALF] for h in range(2)],
                                          [hT_lo[:, k, h * HALF:(h + 1) * HALF] for h in range(2)],
                                          k == 0, k == KT - 1)
                last.then_inc(proj_done, 1)

            def gates(t):
                pe.wait_ge(conv_ready, t + 1)
                pe.wait_ge(cur_ready, t + 1)
                pe.wait_ge(gates_read, t + 1)
                for g in range(2):
                    for h in range(2):
                        last = pe.matmul(ps_t[g][:, h, :], gate_cur[:, g, :], conv_x[:, h * HALF:(h + 1) * HALF],
                                         start=True, stop=True)
                last.then_inc(gates_done, 1)

            with pe.Fori(0, 2) as i:
                for c in range(4):
                    tile(i * 4 + (c + 1), c)
            with pe.Fori(0, 2) as i:
                for c in range(4):
                    tile(i * 4 + (c + 9), c)
                    if c % 2 == 0:
                        gates(i * 2 + c // 2)
            for c in range(4):
                tile(17 + c, c)


def attend(nc, io, persist):
    mixT, qkvT, ident, head_ss = (persist[n] for n in ("mixT", "qkvT", "ident", "head_ss"))
    with ExitStack() as ctx:
        sb = lambda name, shape, dt=F32: ctx.enter_context(nc.sbuf_tensor(name, shape, dt))
        sem = lambda name: ctx.enter_context(nc.semaphore(name))
        q_parts, k_parts = persist["q_parts"], persist["k_parts"]
        qq = sb("qq", [P, 2, SEQ], F32R)
        kk = sb("kk", [P, 2, 2, 2, SEQ], F32R)
        vT = sb("vT", [P, SEQ])
        v_nat = sb("v_nat", [P, HEADS, TT, DH])
        bias8 = sb("bias8", [P, SEQ])
        prob = sb("prob", [P, 4, 2, SEQ])
        attT = sb("attT", [P, 2, SEQ])
        junk = sb("junk", [P, 2, DH])
        lam_in = sb("lam_in", [P, 4, QK])
        lam = sb("lam", [P, 8])
        row_max = sb("row_max", [P, TT, 2])
        neg_max = sb("neg_max", [P, TT, 2])
        row_sum = sb("row_sum", [P, TT, 2])
        inv_sum = sb("inv_sum", [P, TT, 2])
        coef = sb("coef", [P, TT])
        ps_s = [ctx.enter_context(nc.psum_tensor(f"ps_s{c}", [P, SEQ], F32)) for c in range(2)]
        ps_t = ctx.enter_context(nc.psum_tensor("ps_t", [P, SEQ], F32))
        ps_o = [ctx.enter_context(nc.psum_tensor(f"ps_o{n}", [P, HALF], F32)) for n in range(2)]

        lam_loaded = sem("lam_loaded")
        lam_sums = sem("lam_sums")
        lam_exp = sem("lam_exp")
        pool_own = sem("pool_own")
        bias_ready = sem("bias_ready")
        v_ready = sem("v_ready")
        qk_high = sem("qk_high")
        qk_split = sem("qk_split")
        qk_in = [sem(f"qk_in{n}") for n in range(3)]
        scores_done = sem("scores_done")
        scores_read = sem("scores_read")
        max_ready = sem("max_ready")
        exp_done = sem("exp_done")
        att_ready = sem("att_ready")
        turned = sem("turned")
        turned_out = sem("turned_out")
        pv_done = sem("pv_done")
        out_scaled = sem("out_scaled")
        out_squared = sem("out_squared")
        dve_own = sem("dve_own2")
        dve_seen = sem("dve_seen")
        block = ctx.enter_context(nc.Block("attend"))

        width = [(TT - s) * P for s in range(TT)]
        tile_of = [TT - 1 - s for s in range(TT)]

        def pipeline(eng, emit, link=None, per=0):
            for s in range(TT):
                emit(0, s)
            with eng.Fori(1, HEADS - 1) as h:
                if link:
                    link.loop(h - 1, per)
                for s in range(TT):
                    emit(h, s)
            if link:
                link.end(HEADS - 2)
            for s in range(TT):
                emit(HEADS - 1, s)
            for s in range(4):
                emit(HEADS, s)

        def behind(h, s, k):
            head, e = (h, s - k) if s >= k else (h - 1, s - k + TT)
            return None if isinstance(h, int) and not 0 <= head < HEADS else (h * TT + (s - k), head, e)

        def k_buffer(h):
            assert HEADS == 4
            return h % 2 if isinstance(h, int) else h * -1 + 2

        def last(h):
            return isinstance(h, int) and h >= HEADS - 1

        def turn_number(h, s):
            return h * (TT + 1) + (s - 1 if s == 0 or isinstance(h, int) and h == HEADS else s)

        def v_number(h):
            return 1 if isinstance(h, int) and h == 0 else h * (TT + 1)

        def tile(tensor, n):
            return tensor[:, span(n, 1)].rearrange("p o n -> p (o n)")

        @block.sync
        def _(sp):
            halves = [(c, slice(QK * c, QK * c + QK), row, slice(QK * row, QK * row + QK))
                      for c in range(2) for row in range(2)]

            def arrange_k(h, of=halves, n=0):
                for c, src, row, dst in of:
                    sp.dma_start(kk[dst, span(k_buffer(h), 1), :, c, :].rearrange("p o w n -> p (o w) n").bitcast(F32),
                                 k_parts[src, :, :].bitcast(F32)).then_inc(qk_in[n], 16)

            def arrange_q(n, cols, of=halves):
                for c, src, row, dst in of:
                    sp.dma_start(qq[dst, c, cols].bitcast(F32), q_parts[src, row, cols].bitcast(F32)).then_inc(qk_in[n], 16)

            def arrange(h):
                sp.wait_ge(qk_split, h * 2 + 2)
                sp.wait_ge(scores_done, h * TT + (1 - TT))
                arrange_k(h)
                sp.wait_ge(scores_done, h * TT - TT // 2)
                arrange_q(1, slice(HALF, SEQ))
                sp.wait_ge(scores_done, h * TT)
                arrange_q(2, slice(0, HALF))

            for n in range(2):
                arrange_k(0, halves[2 * n:2 * n + 2], n)
                arrange_q(n, slice(0, SEQ), halves[2 * n:2 * n + 2])
            for n, name in enumerate(("lambda_q1", "lambda_k1", "lambda_q2", "lambda_k2")):
                sp.dma_start(lam_in[:, n, :], io[name][0].partition_broadcast(P)).then_inc(lam_loaded, 16)
            with sp.Fori(1, HEADS - 1) as h:
                arrange(h)
            arrange(HEADS - 1)
            sp.dma_start(persist["head_w"][:, :], io["head_norm_w"][0].partition_broadcast(P)).then_inc(persist["wout_in"], 16)
            sp.dma_start(qkvT[:, 0:KT], io["w_out"][0].rearrange("(k p) n -> p k n", p=P)).then_inc(persist["wout_in"], 16)

        @block.gpsimd
        def _(pool):
            pool.iota(bias8[:, :], [[8, SEQ]], base=-8 * (SEQ - P), channel_multiplier=-8,
                      allow_small_or_imprecise_dtypes=True).then_inc(pool_own, 1)
            pool.wait_ge(pool_own, 1)
            pool.affine_select(out=bias8[:, :], in_=bias8[:, :], compare_op=ALU.is_ge, fill=-BIG,
                               base=SEQ - P, pattern=[[-1, SEQ]], channel_multiplier=1).then_inc(pool_own, 1)
            pool.wait_ge(pool_own, 2)
            with pool.Fori(0, HEADS) as h:
                pool.wait_ge(scores_read, h * TT + 1)
                pool.sem_inc(pool_own, 1)
                pool.tensor_scalar(bias8[:, :], bias8[:, :], 2.0 ** (-8.0 / HEADS), 1.0,
                                   ALU.mult, ALU.mult).then_inc(bias_ready, 1)
                pool.tensor_copy(vT[:, :], tile(qkvT, h + 8)).then_inc(v_ready, 1)

        @block.scalar
        def _(act):
            act.wait_ge(lam_sums, 2)
            act.activation(lam[:, 2:4], lam[:, 0:2], ACT.Exp).then_inc(lam_exp, 1)

            def split(h):
                act.wait_ge(qk_in[2], h * 64)
                act.activation(q_parts[:, 0], tile(qkvT, h), ACT.Copy).then_inc(qk_high, 1)
                act.activation(k_parts[:, 0], tile(qkvT, h + 4), ACT.Copy).then_inc(qk_high, 1)

            def emit(h, s):
                if s == 1 and not (isinstance(h, int) and h == HEADS):
                    act.wait_ge(turned, v_number(h))
                    act.activation(v_nat[:, span(h, 1)].rearrange("p o k n -> p (o k) n"),
                                   ps_t[:, :].rearrange("p (k n) -> p k n", n=P), ACT.Copy).then_inc(turned_out, 1)
                if at := behind(h, s, 2):
                    n, head, e = at
                    act.wait_ge(turned, turn_number(h, s))
                    act.wait_ge(pv_done, n + 1)
                    act.activation(attT[:, e % 2, 0:width[e]], ps_t[:, 0:width[e]], ACT.Copy).then_inc(turned_out, 1)
                if at := behind(h, s, 0):
                    n, head, e = at
                    act.wait_ge(max_ready, n + 1)
                    for c in range(2):
                        ins = act.activation(prob[:, e % 4, c, 0:width[e]], prob[:, e % 4, c, 0:width[e]], ACT.Exp,
                                             bias=neg_max[:, e, c:c + 1], scale=QK ** -0.5,
                                             accum_out=row_sum[:, e, c:c + 1])
                    ins.then_inc(exp_done, 1)
                if s == 2 and not last(h):
                    split(h + 1)
                if at := behind(h, s, 4):
                    n, head, e = at
                    act.wait_ge(out_scaled, n + 1)
                    act.activation(junk[:, e % 2], ps_o[e % 2][:, 0:DH], ACT.Square, scale=inv_sum[:, e, 0:1],
                                   accum_out=head_ss[:, span(head * TT + tile_of[e], 1)]).then_inc(out_squared, 1)

            act.sem_inc(qk_high, 2)
            pipeline(act, emit)

        @block.vector
        def _(dve):
            link = Link(dve, dve_own)
            dve.sem_inc(scores_read, 1)
            dve.sem_inc(qk_split, 2)
            dve.wait_ge(lam_loaded, 64)
            for n in range(2):
                dve.tensor_tensor_reduce(lam_in[:, 2 * n, :], lam_in[:, 2 * n, :], lam_in[:, 2 * n + 1, :], 1.0, 0.0,
                                         ALU.mult, ALU.add, lam[:, n:n + 1]).then_inc(lam_sums, 1)
            dve.wait_ge(lam_exp, 1)
            link(dve.tensor_tensor(lam[:, 4:5], lam[:, 3:4], lam[:, 2:3], ALU.subtract))
            link(dve.tensor_scalar(lam[:, 5:6], lam[:, 4:5], -LAM_INIT, None, ALU.add))

            def split(h):
                dve.wait_ge(qk_high, h * 2 + 2)
                dve.tensor_tensor(q_parts[:, 1], tile(qkvT, h), q_parts[:, 0].bitcast(F32), ALU.subtract).then_inc(qk_split, 1)
                dve.tensor_tensor(k_parts[:, 1], tile(qkvT, h + 4), k_parts[:, 0].bitcast(F32), ALU.subtract).then_inc(qk_split, 1)

            def emit(h, s):
                if at := behind(h, s, 0):
                    n, head, e = at
                    if s == 0:
                        dve.wait_ge(bias_ready, h + 1)
                    dve.wait_ge(scores_done, n + 1)
                    dve.sem_inc(dve_seen, 1)
                    b = bias8[:, SEQ - width[e]:SEQ]
                    dve.tensor_tensor_reduce(prob[:, e % 4, 0, 0:width[e]], ps_s[0][:, 0:width[e]], b, 1.0, -3e38,
                                             ALU.add, ALU.max, row_max[:, e, 0:1])
                    link(dve.tensor_tensor_reduce(prob[:, e % 4, 1, 0:width[e]], ps_s[1][:, 0:width[e]], b, 1.0,
                                                  -3e38, ALU.add, ALU.max, row_max[:, e, 1:2]))
                    dve.sem_inc(scores_read, 1)
                    dve.tensor_scalar(neg_max[:, e, :], row_max[:, e, :], -(QK ** -0.5), None,
                                      ALU.mult).then_inc(max_ready, 1)
                if at := behind(h, s, 1):
                    n, head, e = at
                    dve.wait_ge(exp_done, n + 1)
                    link(dve.reciprocal(inv_sum[:, e, :], row_sum[:, e, :]))
                    link(dve.scalar_tensor_tensor(out=coef[:, e:e + 1], in0=row_sum[:, e, 0:1], scalar=lam[:, 5:6],
                                                  in1=inv_sum[:, e, 1:2], op0=ALU.mult, op1=ALU.mult))
                    dve.scalar_tensor_tensor(out=prob[:, e % 4, 0, 0:width[e]], in0=prob[:, e % 4, 1, 0:width[e]],
                                             scalar=coef[:, e:e + 1], in1=prob[:, e % 4, 0, 0:width[e]],
                                             op0=ALU.mult, op1=ALU.add).then_inc(att_ready, 1)
                if s == 2 and not last(h):
                    split(h + 1)
                if at := behind(h, s, 4):
                    n, head, e = at
                    dve.wait_ge(pv_done, n + 3)
                    o = mixT[:, span(head + 4, 1), tile_of[e] * P:tile_of[e] * P + P]
                    dve.tensor_scalar(o.rearrange("p o n -> p (o n)"), ps_o[e % 2][:, 0:DH], inv_sum[:, e, 0:1], None,
                                      ALU.mult).then_inc(out_scaled, 1)

            pipeline(dve, emit, link, per=3 * TT)

        @block.tensor
        def _(pe):
            for free, n in ((turned_out, 1), (pv_done, 2), (out_squared, 2)):
                pe.sem_inc(free, n)
            pe.sem_inc(qk_in[2], 64)

            def scores(h, s):
                if s == 0:
                    pe.wait_ge(qk_in[0], h * 64 + 64)
                    if not (isinstance(h, int) and h == 0):
                        pe.wait_ge(qk_in[1], h * 64 + 64)
                if s == TT // 2:
                    pe.wait_ge(qk_in[2], h * 64 + 64)
                pe.wait_ge(scores_read, h * TT + (s + 1))
                qt = slice(tile_of[s] * P, tile_of[s] * P + P)
                for c in range(2):
                    if isinstance(h, int) and h == 0 and s == 0 and c == 1:
                        pe.wait_ge(qk_in[1], 64)
                    for part in range(2):
                        for lo in range(0, width[s], HALF):
                            cols = slice(lo, min(lo + HALF, width[s]))
                            keys = kk[:, span(k_buffer(h), 1), part, c, cols].rearrange("p o n -> p (o n)")
                            mm = pe.matmul(ps_s[c][:, cols], qq[:, c, qt], keys, start=part == 0, stop=part == 1)
                mm.then_inc(scores_done, 1)

            def emit(h, s):
                if behind(h, s, 0):
                    scores(h, s)
                if s == 1 and not (isinstance(h, int) and h == HEADS):
                    pe.wait_ge(turned_out, v_number(h))
                    pe.wait_ge(v_ready, h + 1)
                    for k in range(TT):
                        mm = pe.transpose(ps_t[:, k * P:(k + 1) * P], vT[:, k * P:(k + 1) * P], ident[:, :])
                    mm.then_inc(turned, 1)
                if at := behind(h, s, 2):
                    n, head, e = at
                    pe.wait_ge(att_ready, n + 1)
                    pe.wait_ge(turned_out, turn_number(h, s))
                    for k in range(TT - e):
                        mm = pe.transpose(ps_t[:, k * P:(k + 1) * P], prob[:, e % 4, 0, k * P:(k + 1) * P], ident[:, :])
                    mm.then_inc(turned, 1)
                if at := behind(h, s, 3):
                    n, head, e = at
                    pe.wait_ge(turned_out, (turn_number(h, s - 1) if s else turn_number(h - 1, TT - 1)) + 1)
                    pe.wait_ge(out_squared, n + 1)
                    for k in range(TT - e):
                        mm = pe.matmul(ps_o[e % 2][:, 0:DH], attT[:, e % 2, k * P:(k + 1) * P],
                                       v_nat[:, span(head, 1), k, :].rearrange("p o n -> p (o n)"),
                                       start=k == 0, stop=k == TT - e - 1)
                    mm.then_inc(pv_done, 1)

            pipeline(pe, emit)


def stage(a, b, k):
    n, half, par = a * 2 + (b - k), a + (b - k) // 2, (b - k) % 2
    return None if isinstance(a, int) and not 0 <= n < TT else (n, half, par)


def tile_steps(eng, emit, link=None, per=0):
    for b in (-1, 0, 1):
        emit(0, b)
    with eng.Fori(0, 2) as i:
        if link:
            link.loop(i, per)
        emit(i, 2)
        emit(i, 3)
    if link:
        link.end(2)
    for b in (6, 7, 8, 9):
        emit(0, b)


def need(eng, sem, value):
    if not isinstance(value, int) or value > 0:
        eng.wait_ge(sem, value)


def mix_out(nc, io, persist):
    mixT, ident, head_ss, logits = (persist[n] for n in ("mixT", "ident", "head_ss", "logits"))
    with ExitStack() as ctx:
        sb = lambda name, shape, dt=F32: ctx.enter_context(nc.sbuf_tensor(name, shape, dt))
        sem = lambda name: ctx.enter_context(nc.semaphore(name))
        wout_raw, hn_sb = persist["qkvT"][:, 0:KT], persist["qkvT"][:, KT:KT + 2]
        hnT = persist["qkvT"][:, KT + 2:KT + 4].rearrange("p b (k n) -> p b k n", n=P)
        wout_hi = sb("wout_hi", [P, KT, D], F32R)
        wout_lo = sb("wout_lo", [P, KT, D], F32R)
        c_hi = sb("c_hi", [P, 2, KT, P], F32R)
        c_lo = sb("c_lo", [P, 2, KT, P], F32R)
        heads_n = sb("heads_n", [P, 2, HEADS * DH])
        x_sb = sb("x_sb", [P, 2, D])
        x2_sb = sb("x2_sb", [P, 2, D])
        norm_w = sb("ffn_w", [P, D])
        head_w = persist["head_w"]
        head_r = sb("head_r", [P, HEADS * TT])
        w_rt = sb("w_rt", [P, KT, NG + NE])
        b_rt = sb("b_rt", [P, NG + NE])
        stat = sb("stat3", [P, 3, TT])
        eps = sb("eps3", [P, 2])
        ps_c = [ctx.enter_context(nc.psum_tensor(f"ps_c{n}", [P, HALF], F32)) for n in range(2)]
        ps_y = [ctx.enter_context(nc.psum_tensor(f"ps_y{n}", [P, D], F32)) for n in range(2)]
        ps_h = ctx.enter_context(nc.psum_tensor("ps_h", [P, D], F32))

        small_in = sem("small_in")
        x_in = [sem(f"x3_in{n}") for n in range(2)]
        x2_out = [sem(f"x2_out{n}") for n in range(2)]
        hn_out = [sem(f"hn_out{n}") for n in range(2)]
        eps_set = sem("eps_set")
        head_root = sem("head_root")
        wout_high = sem("wout_high")
        wout_split = sem("wout_split")
        heads_ready = sem("heads_ready")
        c_turned = sem("c_turned")
        c_high = sem("c_high")
        c_split = sem("c_split")
        y_done = sem("y_done")
        x2_ready = sem("x2_ready")
        root_ready = sem("root3_ready")
        hn_ready = sem("hn_ready")
        hn_turned = sem("hn_turned")
        hnT_ready = sem("hnT_ready")
        routed = sem("routed")
        logits_ready = sem("logits_ready")
        act_own = sem("act_own3")
        dve_own = sem("dve_own3")
        block = ctx.enter_context(nc.Block("mix"))
        k_order = [4, 5, 6, 7, 0, 1, 2, 3]

        @block.sync
        def _(sp):
            sp.dma_start(norm_w[:, :], io["ffn_norm_w"][0].partition_broadcast(P)).then_inc(small_in, 16)
            sp.dma_start(w_rt[:, :, 0:NG], io["w_router_group"][0].rearrange("(k p) n -> p k n", p=P)).then_inc(small_in, 16)
            sp.dma_start(w_rt[:, :, NG:], io["w_router_expert"][0].rearrange("(k p) n -> p k n", p=P)).then_inc(small_in, 16)
            sp.dma_start(b_rt[:, 0:NG], io["b_router_group"][0].partition_broadcast(P)).then_inc(small_in, 16)
            sp.dma_start(b_rt[:, NG:], io["b_router_expert"][0].partition_broadcast(P)).then_inc(small_in, 16)

            def emit(a, b):
                if at := stage(a, b, -1):
                    n, half, par = at
                    need(sp, x2_ready, n - 1)
                    sp.dma_start(x_sb[:, par], io["x"][0][span(n * P, P), :]).then_inc(x_in[par], 16)
                if isinstance(a, int) and b == 0:
                    sp.wait_ge(wout_split, KT)
                    load_gate_up(sp, io, persist, persist["main_sems"], 0, 0)
                if at := stage(a, b, 1):
                    n, half, par = at
                    sp.wait_ge(x2_ready, n + 1)
                    sp.dma_start(persist["x2_d"][span(n * P, P), :], x2_sb[:, par]).then_inc(x2_out[par], 16)
                    sp.wait_ge(hn_ready, n + 1)
                    for copy in range(2):
                        sp.dma_start(persist["hn_d"][copy][span(n * P, P), :], hn_sb[:, par]).then_inc(hn_out[par], 16)

            tile_steps(sp, emit)
            for par in range(2):
                sp.wait_ge(x2_out[par], 16 * (TT // 2))
                sp.wait_ge(hn_out[par], 32 * (TT // 2))

        @block.gpsimd
        def _(pool):
            pool.memset(eps[:, 0:1], HEAD_EPS).then_inc(eps_set, 1)
            pool.memset(eps[:, 1:2], NORM_EPS).then_inc(eps_set, 1)

        @block.scalar
        def _(act):
            link = Link(act, act_own)
            act.wait_ge(eps_set, 2)
            act.activation(head_r[:, :], head_ss[:, :], ACT.Sqrt, bias=eps[:, 0:1], scale=1.0 / DH).then_inc(head_root, 1)

            def emit(a, b):
                if at := stage(a, b, -1):
                    n, half, par = at
                    need(act, y_done, n - 1)
                    act.wait_ge(c_turned, n + 1)
                    act.activation(c_hi[:, par, 0:4], ps_c[par][:, :].rearrange("p (k n) -> p k n", n=P),
                                   ACT.Copy).then_inc(c_high, 1)
                    act.activation(c_hi[:, par, 4:8], mixT[:, 0:4, span(n * P, P)], ACT.Copy).then_inc(c_high, 1)
                if isinstance(a, int) and b == -1:
                    act.wait_ge(persist["wout_in"], 32)
                    for k in k_order:
                        act.activation(wout_hi[:, k], wout_raw[:, k], ACT.Copy).then_inc(wout_high, 1)
                if at := stage(a, b, 0):
                    n, half, par = at
                    act.wait_ge(x2_ready, n + 1)
                    need(act, hn_out[par], half * 32)
                    need(act, hn_turned, n - 1)
                    link(act.activation(hn_sb[:, par], x2_sb[:, par], ACT.Square, accum_out=stat[:, 0, span(n, 1)]))
                    act.activation(stat[:, 1, span(n, 1)], stat[:, 0, span(n, 1)], ACT.Sqrt, bias=eps[:, 1:2],
                                   scale=1.0 / D).then_inc(root_ready, 1)
                if at := stage(a, b, 1):
                    n, half, par = at
                    act.wait_ge(hn_turned, n + 1)
                    act.wait_ge(routed, n)
                    act.activation(hnT[:, par], ps_h[:, :].rearrange("p (k n) -> p k n", n=P), ACT.Copy).then_inc(hnT_ready, 1)

            tile_steps(act, emit, link, 2)

        @block.vector
        def _(dve):
            link = Link(dve, dve_own)
            dve.sem_inc(logits_ready, 1)
            dve.sem_inc(routed, 1)
            dve.wait_ge(persist["wout_in"], 32)
            link(dve.tensor_scalar(head_w[:, :], head_w[:, :], 1.0 - LAM_INIT, None, ALU.mult))
            dve.wait_ge(head_root, 1)
            link(dve.reciprocal(head_r[:, :], head_r[:, :]))

            def heads(n, par):
                need(dve, c_turned, n - 1)
                for h in range(HEADS):
                    ins = dve.scalar_tensor_tensor(out=heads_n[:, par, h * DH:(h + 1) * DH],
                                           in0=mixT[:, 4 + h, span(n * P, P)],
                                           scalar=head_r[:, span(n + h * TT, 1)], in1=head_w[:, :],
                                           op0=ALU.mult, op1=ALU.mult)
                ins.then_inc(heads_ready, 1)

            def emit(a, b):
                if isinstance(a, int) and b == -1:
                    heads(0, 0)
                if at := stage(a, b, -1):
                    n, half, par = at
                    dve.wait_ge(c_high, n * 2 + 2)
                    dve.tensor_tensor(c_lo[:, par, 0:4], ps_c[par][:, :].rearrange("p (k n) -> p k n", n=P),
                                      c_hi[:, par, 0:4].bitcast(F32), ALU.subtract)
                    dve.tensor_tensor(c_lo[:, par, 4:8], mixT[:, 0:4, span(n * P, P)],
                                      c_hi[:, par, 4:8].bitcast(F32), ALU.subtract).then_inc(c_split, 1)
                if isinstance(a, int) and b == -1:
                    heads(1, 1)
                    for j, k in enumerate(k_order):
                        dve.wait_ge(wout_high, j + 1)
                        dve.tensor_tensor(wout_lo[:, k], wout_raw[:, k], wout_hi[:, k].bitcast(F32),
                                          ALU.subtract).then_inc(wout_split, 1)
                if at := stage(a, b, 0):
                    n, half, par = at
                    dve.wait_ge(y_done, n + 1)
                    dve.wait_ge(x_in[par], half * 16 + 16)
                    need(dve, x2_out[par], half * 16)
                    dve.tensor_tensor(x2_sb[:, par], ps_y[par][:, :], x_sb[:, par], ALU.add).then_inc(x2_ready, 1)
                    if later := stage(a, b, -2):
                        heads(later[0], later[2])
                    if isinstance(n, int) and n == 0:
                        dve.wait_ge(small_in, 80)
                    dve.wait_ge(root_ready, n + 1)
                    link(dve.reciprocal(stat[:, 2, span(n, 1)], stat[:, 1, span(n, 1)]))
                    dve.scalar_tensor_tensor(out=hn_sb[:, par], in0=x2_sb[:, par], scalar=stat[:, 2, span(n, 1)],
                                             in1=norm_w[:, :], op0=ALU.mult, op1=ALU.mult).then_inc(hn_ready, 1)
                if at := stage(a, b, 2):
                    n, half, par = at
                    dve.wait_ge(routed, n + 2)
                    dve.tensor_tensor(logits[:, span(n, 1)].rearrange("p o n -> p (o n)"), ps_c[par][:, 0:NG + NE],
                                      b_rt[:, :], ALU.add).then_inc(logits_ready, 1)

            tile_steps(dve, emit, link, 2)

        @block.tensor
        def _(pe):
            def mix(n, par, js):
                for j in js:
                    k = k_order[j]
                    if isinstance(n, int) and n == 0:
                        pe.wait_ge(wout_split, j + 1)
                    mm = split_products(pe, [ps_y[par][:, h * HALF:(h + 1) * HALF] for h in range(2)],
                                        c_hi[:, par, k], c_lo[:, par, k],
                                        [wout_hi[:, k, h * HALF:(h + 1) * HALF] for h in range(2)],
                                        [wout_lo[:, k, h * HALF:(h + 1) * HALF] for h in range(2)],
                                        j == 0, j == KT - 1)
                return mm

            def emit(a, b):
                own = stage(a, b, 0)
                if own:
                    pe.wait_ge(c_split, own[0] + 1)
                    need(pe, x2_ready, own[0] - 1)
                    mix(own[0], own[2], range(KT // 2))
                if at := stage(a, b, -1):
                    n, half, par = at
                    pe.wait_ge(heads_ready, n + 1)
                    need(pe, c_split, n - 1)
                    need(pe, logits_ready, n - 2)
                    for h in range(HEADS):
                        mm = pe.transpose(ps_c[par][:, h * DH:(h + 1) * DH], heads_n[:, par, h * DH:(h + 1) * DH], ident[:, :])
                    mm.then_inc(c_turned, 1)
                if at := stage(a, b, 2):
                    n, half, par = at
                    pe.wait_ge(hnT_ready, n + 1)
                    if isinstance(n, int):
                        need(pe, logits_ready, n)
                    for k in range(KT):
                        mm = pe.matmul(ps_c[par][:, 0:NG + NE], hnT[:, par, k], w_rt[:, k], start=k == 0, stop=k == KT - 1)
                    mm.then_inc(routed, 1)
                if own:
                    mix(own[0], own[2], range(KT // 2, KT)).then_inc(y_done, 1)
                if at := stage(a, b, 1):
                    n, half, par = at
                    pe.wait_ge(hn_ready, n + 1)
                    need(pe, hnT_ready, n)
                    for k in range(KT):
                        mm = pe.transpose(ps_h[:, k * P:(k + 1) * P], hn_sb[:, par, k * P:(k + 1) * P], ident[:, :])
                    mm.then_inc(hn_turned, 1)

            tile_steps(pe, emit)


RING = 6
UNITS = KT + FT


def unit_number(s, u):
    if isinstance(s, int) and s in (0, NE):
        return u if s == 0 else s * UNITS - UNITS + u
    return s * UNITS + (u - FT)


class StepSems:

    def __init__(self, sem, tag, buffers):
        self.gu_in = [sem(f"{tag}_gu_in{p}") for p in range(buffers)]
        self.d_in = [sem(f"{tag}_d_in{p}") for p in range(buffers)]
        self.entry_ready = sem(f"{tag}_entry_ready")
        self.y_entry_ready = sem(f"{tag}_y_entry_ready")
        self.x_in = [sem(f"{tag}_x_in{p}") for p in range(buffers)]
        self.y_out = [sem(f"{tag}_y_out{p}") for p in range(buffers)]
        self.split_high = sem(f"{tag}_split_high")
        self.split_low = sem(f"{tag}_split_low")
        self.units_done = sem(f"{tag}_units_done")
        self.x_turned = sem(f"{tag}_x_turned")
        self.x_high = sem(f"{tag}_x_high")
        self.x_ready = sem(f"{tag}_x_ready")
        self.h_act_ready = sem(f"{tag}_h_act_ready")
        self.h_ready = sem(f"{tag}_h_ready")
        self.h_turned = sem(f"{tag}_h_turned")
        self.h_high = sem(f"{tag}_h_high")
        self.h_split = sem(f"{tag}_h_split")
        self.y_ready = sem(f"{tag}_y_ready")
        self.y_free = sem(f"{tag}_y_free")


def load_gate_up(sp, io, persist, q, e, par):
    for which, name in enumerate(("w_exp_gate", "w_exp_up")):
        sp.dma_start(persist["gu_raw"][par][:, which],
                     io[name][0][span(e, 1)].rearrange("o (k p) n -> p (o k) n", p=P)).then_inc(q.gu_in[par], 16)


def load_down(sp, io, persist, q, e, par):
    sp.dma_start(persist["d_raw"][par],
                 io["w_exp_down"][0][span(e, 1)].rearrange("o (f p) n -> p (o f) n", p=P)).then_inc(q.d_in[par], 16)


def route(nc, io, persist):
    logits, gates, extra = (persist[n] for n in ("logits", "gates", "extra"))
    with ExitStack() as ctx:
        sb = lambda name, shape, dt=F32: ctx.enter_context(nc.sbuf_tensor(name, shape, dt))
        sem = lambda name: ctx.enter_context(nc.semaphore(name))
        gmax = sb("gmax", [P, TT])
        gcand = sb("gcand", [P, TT, NG])
        gidx = sb("gidx", [P, TT])
        gexp = sb("gexp", [P, TT, NG])
        gsum = sb("gsum", [P, TT])
        masked = sb("masked", [P, TT, NE])
        cand = sb("cand", [P, TT, NE])
        top = sb("top", [P, 2, TT])
        idx = sb("idx", [P, TT])
        hot = sb("hot", [P, 2, TT, NE])
        both = sb("both", [P, TT, NE])
        diff = sb("diff", [P, 4, TT])
        cum = sb("cum", [P, TT + 1, NE])
        pos = sb("pos", [P, TT + 1, NE])
        more = sb("more", [P, NE])
        over = sb("over", [P, NE, TT - 1])
        limit = sb("limit", [P, NE, TT - 1])
        upto = sb("upto", [P, NE])
        base = sb("base", [P, NE])
        slot_e = sb("slot_e", [P, TT, NE])
        slot_f = sb("slot_f", [P, 2, TT])
        before = sb("before", [P, NX, NE])
        extra_f = sb("extra_f", [P, NX + 1])
        iota_g = sb("iota_g", [P, TT, NG])
        iota_e = sb("iota_e", [P, TT, NE])
        iota_s = sb("iota_s", [P, NE])
        iota_x = sb("iota_x", [P, NX, NE])
        ones = sb("ones", [P, P])
        earlier = sb("earlier", [P, P])
        slots = sb("slots", [P, 2, 2 * TT], I32)
        entry = sb("entry", [P, 2 * TT])
        place = sb("place", [P, 2, 2 * TT])
        iota_p = sb("iota_p", [P, 2 * TT, P])
        iota_c = sb("iota_c", [P, 2 * TT, CHUNKS])
        at_place = sb("at_place", [P, 2 * TT, P])
        in_chunk = sb("in_chunk", [P, 2 * TT, CHUNKS])
        found = sb("found", [P, 2, CHUNKS])
        ps = ctx.enter_context(nc.psum_tensor("ps_pos", [P, HALF], F32))
        ps_e = ctx.enter_context(nc.psum_tensor("ps_entry", [P, HALF], F32))

        set_up = sem("set_up")
        exp_asked = sem("exp_asked")
        exp_given = sem("exp_given")
        counts_asked = sem("counts_asked")
        counted = sem("counted")
        slots_ready = sem("slots_ready")
        found_sums = sem("found_sums")
        dve_own = sem("dve_own4")
        block = ctx.enter_context(nc.Block("route"))

        @block.sync
        def _(sp):
            m = persist["main_sems"]
            load_down(sp, io, persist, m, 0, 0)
            load_gate_up(sp, io, persist, m, 1, 1)
            load_down(sp, io, persist, m, 1, 1)

        @block.gpsimd
        def _(pool):
            f = dict(allow_small_or_imprecise_dtypes=True)
            pool.iota(iota_g[:, :, :], [[0, TT], [1, NG]], base=-NG, channel_multiplier=0, **f).then_inc(set_up, 1)
            pool.iota(iota_e[:, :, :], [[0, TT], [1, NE]], base=-NE, channel_multiplier=0, **f).then_inc(set_up, 1)
            pool.memset(ones[:, :], 1.0).then_inc(set_up, 1)
            pool.iota(limit[:, :, :], [[0, NE], [P, TT - 1]], base=P, channel_multiplier=0, **f).then_inc(set_up, 1)
            pool.iota(iota_s[:, :], [[P, NE]], base=0, channel_multiplier=0, **f).then_inc(set_up, 1)
            pool.iota(iota_x[:, :, :], [[1, NX], [0, NE]], base=0, channel_multiplier=0, **f).then_inc(set_up, 1)
            pool.iota(entry[:, :], [[SEQ, 2], [P, TT]], base=1, channel_multiplier=1, **f).then_inc(set_up, 1)
            pool.iota(iota_p[:, :, :], [[0, 2 * TT], [1, P]], base=0, channel_multiplier=0, **f).then_inc(set_up, 1)
            pool.iota(iota_c[:, :, :], [[0, 2 * TT], [1, CHUNKS]], base=0, channel_multiplier=0, **f).then_inc(set_up, 1)
            pool.memset(persist["x5_sb"][:, :, :], 0.0).then_inc(set_up, 1)
            pool.wait_ge(set_up, 10)
            pool.affine_select(out=earlier[:, :], in_=ones[:, :], compare_op=ALU.is_gt, fill=0.0, base=0,
                               pattern=[[1, P]], channel_multiplier=-1).then_inc(set_up, 1)

        @block.scalar
        def _(act):
            act.wait_ge(exp_asked, 1)
            act.activation(gexp[:, :, :], gexp[:, :, :], ACT.Exp).then_inc(exp_given, 1)
            act.wait_ge(exp_asked, 2)
            act.activation(diff[:, 1, :], diff[:, 0, :], ACT.Exp).then_inc(exp_given, 1)

        @block.vector
        def _(dve):
            link = Link(dve, dve_own)
            lg, le = logits[:, :, 0:NG], logits[:, :, NG:]
            wide_g = lambda x: x.unsqueeze(2).to_broadcast([P, TT, NG])
            wide_e = lambda x: x.unsqueeze(2).to_broadcast([P, TT, NE])
            per_tile = lambda x: x.unsqueeze(1).to_broadcast([P, TT, NE])
            dve.wait_ge(set_up, 2)

            def first_max(value, number, where, index, values, wide, one_hot):
                link(dve.tensor_reduce(values, value, AX.X, ALU.max))
                link(dve.tensor_tensor(where, value, wide(values), ALU.is_equal))
                link(dve.tensor_tensor(where, where, number, ALU.mult))
                link(dve.tensor_reduce(index, where, AX.X, ALU.min))
                link(dve.tensor_tensor(one_hot, number, wide(index), ALU.is_equal))

            first_max(lg, iota_g[:, :, :], gcand[:, :, :], gidx[:, :], gmax[:, :], wide_g, gcand[:, :, :])
            dve.tensor_tensor(gexp[:, :, :], lg, wide_g(gmax[:, :]), ALU.subtract).then_inc(exp_asked, 1)
            link(dve.tensor_scalar(gcand[:, :, :], gcand[:, :, :], -1.0, BIG, ALU.add, ALU.mult))
            link(dve.tensor_tensor(masked[:, :, :].rearrange("p t (g e) -> p t g e", g=NG),
                                   le.rearrange("p t (g e) -> p t g e", g=NG),
                                   gcand[:, :, :].unsqueeze(3).to_broadcast([P, TT, NG, EPG]), ALU.add))
            first_max(masked[:, :, :], iota_e[:, :, :], cand[:, :, :], idx[:, :], top[:, 0, :], wide_e, hot[:, 0])
            link(dve.scalar_tensor_tensor(out=masked[:, :, :].rearrange("p t e -> p (t e)"),
                                          in0=hot[:, 0].rearrange("p t e -> p (t e)"), scalar=-BIG,
                                          in1=masked[:, :, :].rearrange("p t e -> p (t e)"), op0=ALU.mult, op1=ALU.add))
            first_max(masked[:, :, :], iota_e[:, :, :], cand[:, :, :], idx[:, :], top[:, 1, :], wide_e, hot[:, 1])
            dve.tensor_tensor(diff[:, 0, :], top[:, 1, :], top[:, 0, :], ALU.subtract).then_inc(exp_asked, 1)
            link(dve.tensor_tensor(both[:, :, :], hot[:, 0], hot[:, 1], ALU.add))
            link(dve.memset(cum[:, 0, :], 0.0))
            for t in range(TT):
                link(dve.tensor_tensor(cum[:, t + 1, :], cum[:, t, :], both[:, t, :], ALU.add))
            dve.sem_inc(counts_asked, 1)
            dve.wait_ge(counted, 1)
            link(dve.tensor_copy(pos[:, :, :].rearrange("p t e -> p (t e)"), ps[:, 0:(TT + 1) * NE]))
            count = pos[:, TT, :]
            dve.wait_ge(set_up, 11)
            link(dve.tensor_tensor(over[:, :, :], count.unsqueeze(2).to_broadcast([P, NE, TT - 1]), limit[:, :, :], ALU.is_gt))
            link(dve.tensor_reduce(more[:, :], over[:, :, :], AX.X, ALU.add))
            link(dve.tensor_tensor_scan(upto[:, :], ones[:, 0:NE], more[:, :], 0.0, ALU.mult, ALU.add))
            link(dve.tensor_tensor(base[:, :], upto[:, :], more[:, :], ALU.subtract))
            link(dve.tensor_scalar(base[:, :], base[:, :], float(P), float((NE - 1) * P), ALU.mult, ALU.add))
            link(dve.tensor_tensor(base[:, :], base[:, :], iota_s[:, :], ALU.subtract))
            link(dve.tensor_scalar(slot_e[:, :, :], pos[:, 0:TT, :], float(P), None, ALU.is_ge))
            link(dve.tensor_tensor(slot_e[:, :, :], slot_e[:, :, :], per_tile(base[:, :]), ALU.mult))
            link(dve.tensor_tensor(slot_e[:, :, :], slot_e[:, :, :], pos[:, 0:TT, :], ALU.add))
            link(dve.tensor_tensor(slot_e[:, :, :], slot_e[:, :, :], per_tile(iota_s[:, :]), ALU.add))
            for which in range(2):
                link(dve.tensor_tensor(cand[:, :, :], slot_e[:, :, :], hot[:, which], ALU.mult))
                link(dve.tensor_reduce(slot_f[:, which, :], cand[:, :, :], AX.X, ALU.add))
            link(dve.tensor_copy(slots[:, 0, :], slot_f[:, :, :].rearrange("p w t -> p (w t)")))
            link(dve.tensor_scalar(slots[:, 1, :], slots[:, 0, :], 7, None, ALU.logical_shift_right))
            link(dve.tensor_scalar(slots[:, 0, :], slots[:, 0, :], P - 1, None, ALU.bitwise_and))
            link(dve.tensor_copy(place[:, :, :], slots[:, :, :]))
            link(dve.tensor_tensor(in_chunk[:, :, :], iota_c[:, :, :],
                                   place[:, 1, :].unsqueeze(2).to_broadcast([P, 2 * TT, CHUNKS]), ALU.is_equal))
            dve.tensor_tensor(in_chunk[:, :, :], in_chunk[:, :, :],
                              entry[:, :].unsqueeze(2).to_broadcast([P, 2 * TT, CHUNKS]), ALU.mult)
            for half in (slice(0, TT), slice(TT, 2 * TT)):
                dve.tensor_tensor(at_place[:, half, :], iota_p[:, half, :],
                                  place[:, 0, half].unsqueeze(2).to_broadcast([P, TT, P]), ALU.is_equal).then_inc(slots_ready, 1)
            link(dve.tensor_tensor(before[:, :, :], upto[:, :].unsqueeze(1).to_broadcast([P, NX, NE]),
                                   iota_x[:, :, :], ALU.is_le))
            link(dve.tensor_reduce(extra_f[:, 0:NX], before[:, :, :], AX.X, ALU.add))
            link(dve.tensor_scalar(extra_f[:, 0:NX], extra_f[:, 0:NX], float(NE - 1), None, ALU.min))
            link(dve.tensor_copy(extra_f[:, NX:], upto[:, NE - 1:]))
            link(dve.tensor_copy(extra[:, :], extra_f[:, :]))
            dve.wait_ge(exp_given, 1)
            link(dve.tensor_reduce(gsum[:, :], gexp[:, :, :], AX.X, ALU.add))
            link(dve.reciprocal(gsum[:, :], gsum[:, :]))
            dve.wait_ge(exp_given, 2)
            link(dve.tensor_scalar(diff[:, 2, :], diff[:, 1, :], 1.0, None, ALU.add))
            link(dve.reciprocal(diff[:, 2, :], diff[:, 2, :]))
            link(dve.tensor_tensor(gates[:, 0, :], diff[:, 2, :], gsum[:, :], ALU.mult))
            link(dve.tensor_tensor(gates[:, 1, :], gates[:, 0, :], diff[:, 1, :], ALU.mult))
            dve.wait_ge(found_sums, 1)
            link(dve.tensor_scalar(found[:, 0, :], ps_e[:, 0:CHUNKS], 0.0, float(4 * SEQ), ALU.is_equal, ALU.mult))
            link(dve.tensor_tensor(found[:, 0, :], found[:, 0, :], ps_e[:, 0:CHUNKS], ALU.add))
            link(dve.tensor_scalar(found[:, 1, :], found[:, 0, :], -1.0, None, ALU.add))
            link(dve.tensor_copy(persist["entries"][:, :], found[:, 1, :]))

        @block.tensor
        def _(pe):
            pe.wait_ge(set_up, 11)
            pe.wait_ge(counts_asked, 1)
            pe.matmul(ps[:, 0:(TT + 1) * NE], ones[:, :], cum[:, :, :].rearrange("p t e -> p (t e)"), start=True,
                      stop=False, skip_group_check=True)
            pe.matmul(ps[:, 0:TT * NE], earlier[:, :], both[:, :, :].rearrange("p t e -> p (t e)"), start=False,
                      stop=True, skip_group_check=True).then_inc(counted, 1)
            for n in range(2 * TT):
                if n % TT == 0:
                    pe.wait_ge(slots_ready, n // TT + 1)
                mm = pe.matmul(ps_e[:, 0:CHUNKS], at_place[:, n, :], in_chunk[:, n, :], start=n == 0, stop=n == 2 * TT - 1)
            mm.then_inc(found_sums, 1)
def x2_all(persist):
    return persist["gu_raw"][1].rearrange("p a k n -> p (a k n)").rearrange("p (t n) -> p t n", n=D)


def experts(nc, io, persist):
    ident, extra = persist["ident"], persist["extra"]
    entries, hn_d, y_d = (persist[n] for n in ("entries", "hn_d", "y_d"))
    gu_raw, d_raw, m = (persist[n] for n in ("gu_raw", "d_raw", "main_sems"))
    hn_rows = hn_d.rearrange("c t d -> (c t) d")
    with ExitStack() as ctx:
        sb = lambda name, shape, dt=F32: ctx.enter_context(nc.sbuf_tensor(name, shape, dt))
        sem = lambda name: ctx.enter_context(nc.semaphore(name))
        w_hi = sb("w5_hi", [P, RING, D], F32R)
        w_lo = sb("w5_lo", [P, RING, D], F32R)
        entry = sb("entry5", [P, 2], I32)
        y_entry = sb("y_entry5", [P, 2], I32)
        x_sb = persist["x5_sb"]
        x_hi = sb("x5_hi", [P, 2, KT, P], F32R)
        x_lo = sb("x5_lo", [P, 2, KT, P], F32R)
        h_act = sb("h_act", [P, FF])
        h_sb = sb("h_sb", [P, FF])
        h_hi = sb("h_hi", [P, FT, P], F32R)
        h_lo = sb("h_lo", [P, FT, P], F32R)
        y_sb = sb("y_sb", [P, 2, D])
        ps_gu = [ctx.enter_context(nc.psum_tensor(f"ps_gu{n}", [P, 2, HALF], F32)) for n in range(2)]
        ps_y = ctx.enter_context(nc.psum_tensor("ps_y5", [P, 2, HALF], F32))
        ps_t = ctx.enter_context(nc.psum_tensor("ps_t5", [P, 2, HALF], F32))

        x = StepSems(sem, "more", 1)
        pool_seen = sem("pool_seen")
        block = ctx.enter_context(nc.Block("experts"))


        def raw_unit(u, par):
            return gu_raw[par][:, :, u] if u < KT else d_raw[par][:, u - KT].rearrange("p (a n) -> p a n", a=2)

        def two(tensor, r):
            return tensor[:, r].rearrange("p (a n) -> p a n", a=2)

        def turned_rows(bank):
            return bank.rearrange("p a (k n) -> p (a k) n", n=P)


        def high(act, q, n, r, u, par):
            if n is not None:
                need(act, q.units_done, n - (RING - 1))
            act.activation(two(w_hi, r), raw_unit(u, par), ACT.Copy).then_inc(q.split_high, 1)

        def low(dve, q, n, r, u, par):
            dve.wait_ge(q.split_high, n + 1)
            dve.tensor_tensor(two(w_lo, r), raw_unit(u, par), two(w_hi, r).bitcast(F32),
                              ALU.subtract).then_inc(q.split_low, 1)

        def products(pe, q, n, r, outs, lh, ll, start, stop):
            pe.wait_ge(q.split_low, n + 1)
            split_products(pe, outs, lh, ll, [two(w_hi, r)[:, a] for a in range(2)],
                           [two(w_lo, r)[:, a] for a in range(2)], start, stop).then_inc(q.units_done, 1)


        def take_entries(pool, copy, ready, n, par, chunk):
            pool.sem_inc(pool_seen, 1)
            pool.tensor_copy(copy[:, par:par + 1], entries[:, span(chunk, 1)]).then_inc(ready, 1)
            pool.wait_ge(ready, n + 1)
            pool.sem_inc(pool_seen, 1)

        def gather(pool, q, n, par, chunk):
            take_entries(pool, entry, q.entry_ready, n, par, chunk)
            pool.indirect_dma_start(out=x_sb[:, par], out_offset=None, in_=hn_rows,
                                    in_offset=bass.IndirectOffsetOnAxis(ap=entry[:, par:par + 1], axis=0),
                                    bounds_check=2 * SEQ - 1, oob_is_err=False).then_inc(q.x_in[par], 16)

        def scatter_y(pool, q, n, par, chunk):
            pool.wait_ge(q.y_ready, n + 1)
            take_entries(pool, y_entry, q.y_entry_ready, n, par, chunk)
            pool.indirect_dma_start(out=y_d, in_=y_sb[:, par], in_offset=None,
                                    out_offset=bass.IndirectOffsetOnAxis(ap=y_entry[:, par:par + 1], axis=0),
                                    bounds_check=2 * SEQ - 1, oob_is_err=False).then_inc(q.y_out[par], 16)

        def turn_x(pe, q, par):
            for k in range(KT):
                mm = pe.transpose(ps_t[:, k // 4, (k % 4) * P:(k % 4 + 1) * P], x_sb[:, par, k * P:(k + 1) * P], ident[:, :])
            mm.then_inc(q.x_turned, 1)

        def x_high(act, q, n, par):
            act.wait_ge(q.x_turned, n + 1)
            act.activation(x_hi[:, par], turned_rows(ps_t[:, :, :]), ACT.Copy).then_inc(q.x_high, 1)

        def x_low(dve, q, n, par):
            dve.wait_ge(q.x_high, n + 1)
            dve.tensor_tensor(x_lo[:, par], turned_rows(ps_t[:, :, :]), x_hi[:, par].bitcast(F32),
                              ALU.subtract).then_inc(q.x_ready, 1)

        def silu(act, q, par):
            act.activation(h_act[:, :], ps_gu[par][:, 0], ACT.Silu).then_inc(q.h_act_ready, 1)

        def hidden(dve, q, n, par):
            dve.wait_ge(q.h_act_ready, n + 1)
            dve.tensor_tensor(h_sb[:, :], ps_gu[par][:, 1], h_act[:, :], ALU.mult).then_inc(q.h_ready, 1)

        def turn_h(pe, q, n):
            pe.wait_ge(q.h_ready, n + 1)
            for f in range(FT):
                mm = pe.transpose(ps_t[:, 0, f * P:(f + 1) * P], h_sb[:, f * P:(f + 1) * P], ident[:, :])
            mm.then_inc(q.h_turned, 1)

        def h_high(act, q, n):
            act.wait_ge(q.h_turned, n + 1)
            act.activation(h_hi[:, :, :], ps_t[:, 0].rearrange("p (f n) -> p f n", n=P), ACT.Copy).then_inc(q.h_high, 1)

        def h_low(dve, q, n):
            dve.wait_ge(q.h_high, n + 1)
            dve.tensor_tensor(h_lo[:, :, :], ps_t[:, 0].rearrange("p (f n) -> p f n", n=P),
                              h_hi[:, :, :].bitcast(F32), ALU.subtract).then_inc(q.h_split, 1)

        def take_y(dve, q, par):
            dve.tensor_copy(two(y_sb, par), ps_y[:, :, :]).then_inc(q.y_ready, 1)

        def await_y(sp, q, half, par):
            sp.wait_ge(q.y_out[par], half * 16 + 16)
            sp.sem_inc(q.y_free, 1)

        gate_up, rows_y = [[ps_gu[p][:, a] for a in range(2)] for p in range(2)], [ps_y[:, a] for a in range(2)]

        def steps(eng, emit):
            emit(0, 0, 0)
            emit(1, 0, 1)
            with eng.Fori(0, (NE - 4) // 2) as i:
                emit(i * 2 + 2, i + 1, 0)
                emit(i * 2 + 3, i + 1, 1)
            for s in range(NE - 2, NE + 1):
                emit(s, s // 2, s % 2)

        def slot(s, u):
            return (u if isinstance(s, int) and s in (0, NE) else u - FT) % RING

        def more_chunks(eng, body):
            count = eng.value_load(extra[0:1, NX:NX + 1], min_val=0, max_val=NX)
            with eng.If(count > 0):
                with eng.Fori(0, count) as j:
                    body(j)

        def has(s, k=0):
            return not isinstance(s, int) or 0 <= s - k < NE

        @block.sync
        def _(sp):
            def emit(s, half, par):
                if has(s, -2):
                    sp.wait_ge(m.split_low, unit_number(s, KT))
                    load_gate_up(sp, io, persist, m, s + 2, par)
                if has(s, 2):
                    await_y(sp, m, half - 1, par)
                if has(s, -1) and not (isinstance(s, int) and s == 0):
                    sp.wait_ge(m.split_low, unit_number(s, UNITS))
                    load_down(sp, io, persist, m, s + 1, 1 - par)
                if isinstance(s, int) and s == NE - 1:
                    sp.wait_ge(m.split_low, unit_number(s, KT))
                    sp.dma_start(x2_all(persist), persist["x2_d"].rearrange("(t p) n -> p t n", p=P)
                                 ).then_inc(persist["x2_in"], 16)

            steps(sp, emit)
            await_y(sp, m, NE // 2 - 1, 1)
            sp.wait_ge(m.split_low, NE * UNITS)

            def chunk(j):
                e = sp.value_load(extra[0:1, bass.ds(j, 1)], min_val=0, max_val=NE - 1)
                load_gate_up(sp, io, persist, x, e, 0)
                load_down(sp, io, persist, x, e, 0)
                await_y(sp, x, j, 0)

            more_chunks(sp, chunk)

        @block.gpsimd
        def _(pool):
            def step(n, par):
                pool.wait_ge(m.x_turned, n - 1)
                gather(pool, m, n, par, n)

            gather(pool, m, 0, 0, 0)
            gather(pool, m, 1, 1, 1)
            step(2, 0)
            with pool.Fori(0, NE // 2 - 2) as i:
                for par in range(2):
                    step(i * 2 + (3 + par), 1 - par)
                    scatter_y(pool, m, i * 2 + par, par, i * 2 + par)
            step(NE - 1, 1)
            for n in range(NE - 4, NE):
                scatter_y(pool, m, n, n % 2, n)
            pool.wait_ge(m.x_turned, NE)

            def chunk(j):
                gather(pool, x, j, 0, j + NE)
                pool.wait_ge(x.x_turned, j + 1)
                scatter_y(pool, x, j, 0, j + NE)

            more_chunks(pool, chunk)

        @block.scalar
        def _(act):
            def emit(s, half, par):
                for u in range(UNITS):
                    if u == 1 and has(s):
                        x_high(act, m, s, par)
                    if u == 1 and has(s, 1):
                        act.wait_ge(m.units_done, unit_number(s - 1, KT))
                        need(act, m.h_ready, s - 1)
                        silu(act, m, 1 - par)
                    if u == KT + 1 and has(s, 1):
                        h_high(act, m, s - 1)
                    if u < KT and has(s):
                        if u == 0:
                            act.wait_ge(m.gu_in[par], half * 32 + 32)
                        high(act, m, unit_number(s, u), slot(s, u), u, par)
                    if u >= KT and has(s, 1):
                        if u == KT:
                            act.wait_ge(m.d_in[1 - par], (half + par) * 16)
                        high(act, m, unit_number(s, u), slot(s, u), u, 1 - par)

            steps(act, emit)
            act.wait_ge(m.units_done, NE * UNITS)

            def chunk(j):
                x_high(act, x, j, 0)
                act.wait_ge(x.gu_in[0], j * 32 + 32)
                for u in range(UNITS):
                    if u == KT:
                        act.wait_ge(x.units_done, j * UNITS + KT)
                        silu(act, x, 0)
                        h_high(act, x, j)
                        act.wait_ge(x.d_in[0], j * 16 + 16)
                    high(act, x, None if u < RING else j * UNITS + u, u % RING, u, 0)
                act.wait_ge(x.units_done, j * UNITS + UNITS)

            more_chunks(act, chunk)

        @block.vector
        def _(dve):
            dve.sem_inc(m.y_free, 2)

            def take(n, par):
                dve.wait_ge(m.units_done, unit_number(n + 1, UNITS))
                dve.wait_ge(m.y_free, n + 1)
                take_y(dve, m, par)

            def emit(s, half, par):
                for u in range(UNITS):
                    if u == 1 and has(s):
                        x_low(dve, m, s, par)
                    if u == 1 and has(s, 1):
                        hidden(dve, m, s - 1, 1 - par)
                    if u == 5 and has(s, 2):
                        take(s - 2, par)
                    if u == KT + 1 and has(s, 1):
                        h_low(dve, m, s - 1)
                    if (u < KT and has(s)) or (u >= KT and has(s, 1)):
                        low(dve, m, unit_number(s, u), slot(s, u), u, par if u < KT else 1 - par)

            steps(dve, emit)
            take(NE - 1, 1)
            dve.wait_ge(m.y_free, NE + 2)

            def chunk(j):
                x_low(dve, x, j, 0)
                for u in range(UNITS):
                    if u == KT:
                        hidden(dve, x, j, 0)
                        h_low(dve, x, j)
                    low(dve, x, j * UNITS + u, u % RING, u, 0)
                dve.wait_ge(x.units_done, j * UNITS + UNITS)
                take_y(dve, x, 0)
                dve.wait_ge(x.y_free, j + 1)

            more_chunks(dve, chunk)

        @block.tensor
        def _(pe):
            def turn_next(n, half, par):
                pe.wait_ge(m.x_in[par], half * 16 + 16)
                need(pe, m.x_ready, n)
                need(pe, m.h_split, n - 1)
                turn_x(pe, m, par)

            def emit(s, half, par):
                if isinstance(s, int) and s == 0:
                    turn_next(0, 0, 0)
                for u in range(KT):
                    if u == KT // 2 and has(s, 1):
                        turn_h(pe, m, s - 1)
                    if has(s):
                        if u == 0:
                            pe.wait_ge(m.x_ready, s + 1)
                            need(pe, m.h_ready, s - 1)
                        products(pe, m, unit_number(s, u), slot(s, u), gate_up[par], x_hi[:, par, u], x_lo[:, par, u],
                                 u == 0, u == KT - 1)
                if has(s, -1):
                    turn_next(s + 1, half + par, 1 - par)
                if has(s, 1):
                    pe.wait_ge(m.h_split, s)
                    need(pe, m.y_ready, s - 1)
                    for f in range(FT):
                        products(pe, m, unit_number(s, KT + f), slot(s, KT + f), rows_y, h_hi[:, f], h_lo[:, f],
                                 f == 0, f == FT - 1)

            steps(pe, emit)
            pe.wait_ge(m.y_ready, NE)

            def chunk(j):
                pe.wait_ge(x.x_in[0], j * 16 + 16)
                turn_x(pe, x, 0)
                pe.wait_ge(x.x_ready, j + 1)
                for u in range(KT):
                    products(pe, x, j * UNITS + u, u % RING, gate_up[0], x_hi[:, 0, u], x_lo[:, 0, u], u == 0, u == KT - 1)
                turn_h(pe, x, j)
                pe.wait_ge(x.h_split, j + 1)
                for f in range(FT):
                    products(pe, x, j * UNITS + KT + f, (KT + f) % RING, rows_y, h_hi[:, f], h_lo[:, f], f == 0, f == FT - 1)
                pe.wait_ge(x.y_ready, j + 1)

            more_chunks(pe, chunk)


def combine(nc, io, persist, out):
    gates, x2_in, x2_sb = persist["gates"], persist["x2_in"], x2_all(persist)
    with ExitStack() as ctx:
        sb = lambda name, shape, dt=F32: ctx.enter_context(nc.sbuf_tensor(name, shape, dt))
        sem = lambda name: ctx.enter_context(nc.semaphore(name))
        y_sb = sb("y_6", [P, 2, TT, D])
        o_sb = sb("o_6", [P, 2, D])
        norm_w = sb("final_w", [P, D])
        stat = sb("stat6", [P, 3, TT])
        eps = sb("eps6", [P, 1])
        norm_w_in = sem("final_w_in")
        y_in = [sem(f"y_in{t}") for t in range(TT)]
        o_out = [sem(f"o_out{n}") for n in range(2)]
        eps_set = sem("eps_set6")
        scaled = sem("scaled")
        normed = sem("normed")
        sum_ready = sem("sum_ready")
        root_ready = sem("root6_ready")
        o_ready = sem("o_ready")
        act_own = sem("act_own6")
        dve_own = sem("dve_own6")
        block = ctx.enter_context(nc.Block("combine"))

        @block.sync
        def _(sp):
            for t in range(TT):
                for which in range(2):
                    row = which * SEQ + t * P
                    sp.dma_start(y_sb[:, which, t], persist["y_d"][row:row + P, :]).then_inc(y_in[t], 16)
                if t == 0:
                    sp.dma_start(norm_w[:, :], io["final_norm_w"].partition_broadcast(P)).then_inc(norm_w_in, 16)
            for t in range(TT):
                sp.wait_ge(o_ready, t + 1)
                sp.dma_start(out[0][t * P:(t + 1) * P, :], o_sb[:, t % 2]).then_inc(o_out[t % 2], 16)
            for par in range(2):
                sp.wait_ge(o_out[par], 16 * (TT // 2))

        @block.gpsimd
        def _(pool):
            pool.memset(eps[:, :], NORM_EPS).then_inc(eps_set, 1)
            pool.wait_ge(norm_w_in, 16)
            for t in range(TT):
                pool.wait_ge(normed, t + 1)
                need(pool, o_out[t % 2], 16 * (t // 2))
                pool.tensor_tensor(o_sb[:, t % 2], x2_sb[:, t], norm_w[:, :], ALU.mult).then_inc(o_ready, 1)

        @block.vector
        def _(dve):
            link = Link(dve, dve_own)

            def root(t):
                dve.wait_ge(root_ready, t + 1)
                dve.reciprocal(stat[:, 2, t:t + 1], stat[:, 1, t:t + 1]).then_inc(scaled, 1)

            for t in range(TT):
                dve.wait_ge(x2_in, 16)
                dve.wait_ge(y_in[t], 32)
                link(dve.scalar_tensor_tensor(out=x2_sb[:, t], in0=y_sb[:, 0, t], scalar=gates[:, 0, t:t + 1],
                                              in1=x2_sb[:, t], op0=ALU.mult, op1=ALU.add))
                dve.scalar_tensor_tensor(out=x2_sb[:, t], in0=y_sb[:, 1, t], scalar=gates[:, 1, t:t + 1],
                                         in1=x2_sb[:, t], op0=ALU.mult, op1=ALU.add).then_inc(sum_ready, 1)
                if t:
                    root(t - 1)
            root(TT - 1)

        @block.scalar
        def _(act):
            link = Link(act, act_own)
            act.wait_ge(eps_set, 1)

            def square(t):
                act.wait_ge(sum_ready, t + 1)
                link(act.activation(y_sb[:, 0, t], x2_sb[:, t], ACT.Square, accum_out=stat[:, 0, t:t + 1]))
                act.activation(stat[:, 1, t:t + 1], stat[:, 0, t:t + 1], ACT.Sqrt, bias=eps[:, 0:1],
                               scale=1.0 / D).then_inc(root_ready, 1)

            square(0)
            for t in range(TT):
                if t + 1 < TT:
                    square(t + 1)
                act.wait_ge(scaled, t + 1)
                act.activation(x2_sb[:, t], x2_sb[:, t], ACT.Copy, scale=stat[:, 2, t:t + 1]).then_inc(normed, 1)


def build(nc, io, out):
    with ExitStack() as ctx:
        persist = {
            "ident": ctx.enter_context(nc.sbuf_tensor("ident", [P, P], F32)),
        }
        persist["head_ss"] = ctx.enter_context(nc.sbuf_tensor("head_ss", [P, HEADS * TT], F32))
        persist["head_w"] = ctx.enter_context(nc.sbuf_tensor("head_w", [P, DH], F32))
        persist["logits"] = ctx.enter_context(nc.sbuf_tensor("logits", [P, TT, NG + NE], F32))
        persist["gates"] = ctx.enter_context(nc.sbuf_tensor("gates", [P, 2, TT], F32))
        persist["extra"] = ctx.enter_context(nc.sbuf_tensor("extra", [P, NX + 1], I32))
        persist["x2_d"] = nc.dram_tensor("x2_d", (SEQ, D), F32).ap()
        persist["hn_d"] = nc.dram_tensor("hn_d", (2, SEQ, D), F32).ap()
        persist["y_d"] = nc.dram_tensor("y_d", (2 * SEQ, D), F32).ap()
        persist["entries"] = ctx.enter_context(nc.sbuf_tensor("entries", [P, CHUNKS], I32))
        persist["wout_in"] = ctx.enter_context(nc.semaphore("wout_in"))
        persist["x2_in"] = ctx.enter_context(nc.semaphore("x2_in"))
        persist["main_sems"] = StepSems(lambda name: ctx.enter_context(nc.semaphore(name)), "main", 2)
        qkvT = ctx.enter_context(nc.sbuf_tensor("qkvT", [P, 12, SEQ], F32))
        persist["qkvT"] = qkvT
        with nc.sbuf_tensor("mixT", [P, 2 * CT, SEQ], F32) as mixT:
            persist["mixT"] = mixT
            with nc.sbuf_tensor("q_parts", [P, 2, SEQ], F32R) as q_parts, \
                    nc.sbuf_tensor("k_parts", [P, 2, SEQ], F32R) as k_parts:
                persist["q_parts"], persist["k_parts"] = q_parts, k_parts
                project_and_recur(nc, io, persist)
                attend(nc, io, persist)
            gate_up_0 = qkvT[:, 0:KT].rearrange("p t n -> p (t n)").rearrange("p (w k n) -> p w k n", w=2, k=KT)
            persist["gu_raw"], persist["d_raw"] = [gate_up_0], [qkvT[:, KT:KT + FT]]
            mix_out(nc, io, persist)
        with ExitStack() as moe:
            gate_up_1 = moe.enter_context(nc.sbuf_tensor("gate_up_1", [P, 2, KT, FF], F32))
            down_1 = moe.enter_context(nc.sbuf_tensor("down_1", [P, FT, D], F32))
            persist["gu_raw"].append(gate_up_1[:, :, :, :])
            persist["d_raw"].append(down_1[:, :, :])
            persist["x5_sb"] = moe.enter_context(nc.sbuf_tensor("x5_sb", [P, 2, D], F32))
            route(nc, io, persist)
            experts(nc, io, persist)
            combine(nc, io, persist, out)


_INS = ["x", "mix_norm_w", "w_in", "lambda_q1", "lambda_k1", "lambda_q2", "lambda_k2", "head_norm_w", "conv_w",
        "conv_b", "w_rgate", "b_rgate", "w_igate", "b_igate", "lru_lambda", "w_out", "ffn_norm_w",
        "w_router_group", "b_router_group", "w_router_expert", "b_router_expert", "w_exp_gate", "w_exp_up",
        "w_exp_down", "final_norm_w"]


def kernel(**inputs):
    import numpy as _np
    import concourse.bacc as _bacc
    from concourse.bass_utils import run_bass_kernel_spmd as _run

    nc = _bacc.Bacc("TRN2", target_bir_lowering=False, num_devices=1)
    arrays, io = {}, {}
    for name in _INS:
        a = _np.ascontiguousarray(inputs[name])
        arrays[f"in_{name}"] = a
        io[name] = nc.dram_tensor(f"in_{name}", a.shape, mybir.dt.from_np(a.dtype), kind="ExternalInput").ap()
    out = nc.dram_tensor("out_0", (1, SEQ, D), F32, kind="ExternalOutput").ap()
    build(nc, io, out)
    r = _run(nc, [arrays], core_ids=[0])
    return r.results[0]["out_0"]
```
